# Optimizing a Trainium2 kernel written in Bass

```python
import math
import jax, jax.numpy as jnp
from jax import lax
import numpy as np

D_MODEL = 1024
BATCH = 1
SEQ = 512
DEPTH = 2

CTX_LEN = 256
GRID_W = 64
Q_BLOCK = 128
ROPE_THETA = 10000.0
EPS = 1e-6
HEAD_DIM = 64
N_BRANCH = 4
BRANCH_WIDTH = 4 * HEAD_DIM
MLA_HEADS = 4
MLA_Q_LORA = 192
MLA_KV_LORA = 128
MLA_NOPE = 64
MLA_ROPE = 32
MLA_V = 64
MLA_QK = MLA_NOPE + MLA_ROPE
NA_HEADS = 4
NA_ROWS = 8
NA_COLS = 16
DIFF_HEADS = 4
DIFF_DIM = 32
GQA_HEADS = 4
GQA_KV_HEADS = 2
D_FF = 4 * D_MODEL
SPLIT_SIZES = (MLA_Q_LORA, MLA_KV_LORA, MLA_ROPE,
               3 * NA_HEADS * HEAD_DIM,
               3 * DIFF_HEADS * 2 * DIFF_DIM,
               (GQA_HEADS + 2 * GQA_KV_HEADS) * HEAD_DIM,
               N_BRANCH * D_MODEL)
IN_COLS = sum(SPLIT_SIZES)

kernel_name = 'hybrid_gated_branch_dit_block'

def rmsnorm(x, g):
    xf = x.astype(jnp.float32)
    y = xf * lax.rsqrt(jnp.mean(xf * xf, axis=-1, keepdims=True) + EPS)
    return (y * g.astype(jnp.float32)).astype(x.dtype)

def modulate(h, shift, scale):
    return h * (1.0 + scale) + shift

def split_last(z, sizes):
    parts, start = [], 0
    for n in sizes:
        parts.append(z[..., start:start + n])
        start += n
    return parts

def flat_heads(o):
    return o.reshape(*o.shape[:2], -1)

def rope_tables(rows, cols, rot_dim):
    n = rot_dim // 4
    inv_freq = jnp.power(ROPE_THETA, -jnp.arange(n, dtype=jnp.float32) / n)
    ang_r = rows.astype(jnp.float32)[:, None] * inv_freq
    ang_c = cols.astype(jnp.float32)[:, None] * inv_freq
    ang = jnp.concatenate([ang_r, ang_r, ang_c, ang_c], axis=-1)
    return jnp.cos(ang), jnp.sin(ang)

def apply_rope(t, cos, sin):
    shape = (cos.shape[0],) + (1,) * (t.ndim - 3) + (cos.shape[-1],)
    cos, sin = cos.reshape(shape), sin.reshape(shape)
    t1, t2, t3, t4 = jnp.split(t, 4, axis=-1)
    rot = jnp.concatenate([-t2, t1, -t4, t3], axis=-1)
    return (t * cos + rot * sin).astype(t.dtype)

def sweep_query_blocks(fn, q):
    B, S = q.shape[:2]
    nb = S // Q_BLOCK
    qb = jnp.moveaxis(q.reshape(B, nb, Q_BLOCK, *q.shape[2:]), 1, 0)
    out = lax.map(fn, qb)
    return jnp.moveaxis(out, 0, 1).reshape(B, S, *out.shape[3:])

def gqa_attention(q, k, v):
    B, _, H, d = q.shape
    n_kv = k.shape[2]
    G = H // n_kv
    scale = d ** -0.5

    def block(qb):
        qb = qb.reshape(B, Q_BLOCK, n_kv, G, d)
        s = jnp.einsum('bqngd,bknd->bngqk', qb, k).astype(jnp.float32) * scale
        p = jax.nn.softmax(s, axis=-1).astype(v.dtype)
        o = jnp.einsum('bngqk,bknd->bqngd', p, v)
        return o.reshape(B, Q_BLOCK, H, v.shape[-1])

    return sweep_query_blocks(block, q)

def mla_mixer(zl, zc, rope, g_qa, w_uq, g_kva, w_ukv, g_q, g_k, need_ctx):
    cos, sin = rope

    def queries(cq):
        q = (rmsnorm(cq, g_qa) @ w_uq).reshape(*cq.shape[:2], MLA_HEADS, MLA_QK)
        return rmsnorm(q, g_q)

    def keys_values(ckv, k_rope):
        kv = (rmsnorm(ckv, g_kva) @ w_ukv).reshape(*ckv.shape[:2], MLA_HEADS, MLA_NOPE + MLA_V)
        k_rope = jnp.broadcast_to(k_rope[:, :, None, :], (*k_rope.shape[:2], MLA_HEADS, MLA_ROPE))
        k = jnp.concatenate([kv[..., :MLA_NOPE], k_rope], axis=-1)
        return rmsnorm(k, g_k), kv[..., MLA_NOPE:]

    def rotate(t):
        return jnp.concatenate([t[..., :MLA_NOPE], apply_rope(t[..., MLA_NOPE:], cos, sin)], axis=-1)

    cq, ckv, kr = zl
    cq_c, ckv_c, kr_c = zc
    ql = rotate(queries(cq))
    kl, vl = keys_values(ckv, kr)
    kl = rotate(kl)
    k_ctx, v_ctx = keys_values(ckv_c, kr_c)
    o = gqa_attention(ql, jnp.concatenate([kl, k_ctx], axis=1), jnp.concatenate([vl, v_ctx], axis=1))
    o_c = flat_heads(gqa_attention(queries(cq_c), k_ctx, v_ctx)) if need_ctx else None
    return flat_heads(o), o_c

def na_mixer(zl, zc, g_q, g_k, rpb, need_ctx):
    def qkv(z):
        z = z.reshape(*z.shape[:2], 3, NA_HEADS, HEAD_DIM)
        return rmsnorm(z[:, :, 0], g_q), rmsnorm(z[:, :, 1], g_k), z[:, :, 2]

    ql, kl, vl = qkv(zl)
    qc, k_ctx, v_ctx = qkv(zc)
    B, S = ql.shape[:2]
    n_rows = S // GRID_W
    win_r = min(NA_ROWS, n_rows)
    win_c = NA_COLS
    n_nb = win_r * win_c
    scale = HEAD_DIM ** -0.5

    def to_grid(t):
        return t.reshape(B, n_rows, GRID_W, NA_HEADS, HEAD_DIM)

    k_grid, v_grid = to_grid(kl), to_grid(vl)
    row_start = jnp.clip(jnp.arange(n_rows) - win_r // 2, 0, n_rows - win_r)
    col = jnp.arange(GRID_W)
    col_idx = jnp.clip(col - win_c // 2, 0, GRID_W - win_c)[:, None] + jnp.arange(win_c)
    dc = col_idx - col[:, None] + (NA_COLS - 1)

    def row_block(args):
        q_row, r = args
        r0 = row_start[r]
        k_nb = jnp.take(lax.dynamic_slice_in_dim(k_grid, r0, win_r, axis=1), col_idx, axis=2)
        v_nb = jnp.take(lax.dynamic_slice_in_dim(v_grid, r0, win_r, axis=1), col_idx, axis=2)
        dr = r0 + jnp.arange(win_r) - r + (NA_ROWS - 1)
        bias = rpb[:, dr[:, None, None], dc[None, :, :]].transpose(0, 2, 1, 3)
        s_nb = jnp.einsum('bqhd,brqchd->bhqrc', q_row, k_nb).astype(jnp.float32) * scale + bias.astype(jnp.float32)
        s_ctx = jnp.einsum('bqhd,bkhd->bhqk', q_row, k_ctx).astype(jnp.float32) * scale
        p = jax.nn.softmax(jnp.concatenate([s_nb.reshape(B, NA_HEADS, GRID_W, n_nb), s_ctx], axis=-1), axis=-1)
        p = p.astype(v_nb.dtype)
        p_nb = p[..., :n_nb].reshape(B, NA_HEADS, GRID_W, win_r, win_c)
        return (jnp.einsum('bhqrc,brqchd->bqhd', p_nb, v_nb)
                + jnp.einsum('bhqk,bkhd->bqhd', p[..., n_nb:], v_ctx))

    out = lax.map(row_block, (jnp.moveaxis(to_grid(ql), 1, 0), jnp.arange(n_rows)))
    o = jnp.moveaxis(out, 0, 1).reshape(B, S, NA_HEADS * HEAD_DIM)
    o_c = flat_heads(gqa_attention(qc, k_ctx, v_ctx)) if need_ctx else None
    return o, o_c

def diff_mixer(zl, zc, rope, g_q, g_k, lq1, lk1, lq2, lk2, g_sub, lam_init, need_ctx):
    cos, sin = rope
    width = DIFF_HEADS * 2 * DIFF_DIM

    def qk(z, which, g):
        t = z[..., which * width:(which + 1) * width].reshape(*z.shape[:2], DIFF_HEADS, 2, DIFF_DIM)
        return rmsnorm(t, g)

    def vals(z):
        return z[..., 2 * width:].reshape(*z.shape[:2], DIFF_HEADS, 2 * DIFF_DIM)

    lam = (jnp.exp(jnp.sum(lq1.astype(jnp.float32) * lk1.astype(jnp.float32)))
           - jnp.exp(jnp.sum(lq2.astype(jnp.float32) * lk2.astype(jnp.float32))) + lam_init)
    scale = DIFF_DIM ** -0.5

    def attend(q, k, v):
        def block(qb):
            s = jnp.einsum('bqhmd,bkhmd->bhmqk', qb, k).astype(jnp.float32) * scale
            p = jax.nn.softmax(s, axis=-1)
            p_diff = (p[:, :, 0] - lam * p[:, :, 1]).astype(v.dtype)
            return jnp.einsum('bhqk,bkhd->bqhd', p_diff, v)
        o = rmsnorm(sweep_query_blocks(block, q), g_sub) * (1.0 - lam_init)
        return flat_heads(o)

    ql = apply_rope(qk(zl, 0, g_q), cos, sin)
    kl = apply_rope(qk(zl, 1, g_k), cos, sin)
    vl = vals(zl)
    k_ctx, v_ctx = qk(zc, 1, g_k), vals(zc)
    o = attend(ql, jnp.concatenate([kl, k_ctx], axis=1), jnp.concatenate([vl, v_ctx], axis=1))
    o_c = attend(qk(zc, 0, g_q), k_ctx, v_ctx) if need_ctx else None
    return o, o_c

def gqa_mixer(zl, zc, rope, g_q, g_k, need_ctx):
    cos, sin = rope
    nq, nkv = GQA_HEADS * HEAD_DIM, GQA_KV_HEADS * HEAD_DIM

    def qkv(z):
        q = rmsnorm(z[..., :nq].reshape(*z.shape[:2], GQA_HEADS, HEAD_DIM), g_q)
        k = rmsnorm(z[..., nq:nq + nkv].reshape(*z.shape[:2], GQA_KV_HEADS, HEAD_DIM), g_k)
        v = z[..., nq + nkv:].reshape(*z.shape[:2], GQA_KV_HEADS, HEAD_DIM)
        return q, k, v

    ql, kl, vl = qkv(zl)
    qc, k_ctx, v_ctx = qkv(zc)
    ql, kl = apply_rope(ql, cos, sin), apply_rope(kl, cos, sin)
    o = gqa_attention(ql, jnp.concatenate([kl, k_ctx], axis=1), jnp.concatenate([vl, v_ctx], axis=1))
    o_c = flat_heads(gqa_attention(qc, k_ctx, v_ctx)) if need_ctx else None
    return flat_heads(o), o_c

def merge_branches(branches, z_gate, w_branch, w_out):
    o = jnp.stack(branches, axis=2)
    proj = jnp.einsum('bsnw,nwd->bsnd', o, w_branch)
    gate = jax.nn.sigmoid(z_gate.reshape(*z_gate.shape[:2], N_BRANCH, D_MODEL))
    return jnp.sum(gate * proj, axis=2) @ w_out

def sq_relu_mlp(h, w_up, w_down):
    return jnp.square(jax.nn.relu(h @ w_up)) @ w_down

def setup_inputs(seed: int = 0) -> dict:
    key = jax.random.key(seed)
    k = jax.random.split(key, 31)
    L, D = DEPTH, D_MODEL

    def nrm(i, shape, scale):
        return scale * jax.random.normal(k[i], shape, jnp.float32)

    def gain(i, shape):
        return 1.0 + nrm(i, shape, 0.1)

    return {
        'x': nrm(0, (BATCH, SEQ, D), 1.0),
        'c': nrm(1, (BATCH, D), 1.0),
        'ctx': nrm(2, (BATCH, CTX_LEN, D), 1.0),
        'c_ctx': nrm(3, (D,), 1.0),
        'w_ada': nrm(4, (L, D, 6 * D), 0.5 * D ** -0.5),
        'b_ada': nrm(5, (L, 6 * D), 0.02),
        'g_norm1': gain(6, (L, D)),
        'g_norm2': gain(7, (L, D)),
        'w_in': nrm(8, (L, D, IN_COLS), D ** -0.5),
        'g_mla_qa': gain(9, (L, MLA_Q_LORA)),
        'w_mla_uq': nrm(10, (L, MLA_Q_LORA, MLA_HEADS * MLA_QK), MLA_Q_LORA ** -0.5),
        'g_mla_kva': gain(11, (L, MLA_KV_LORA)),
        'w_mla_ukv': nrm(12, (L, MLA_KV_LORA, MLA_HEADS * (MLA_NOPE + MLA_V)), MLA_KV_LORA ** -0.5),
        'g_mla_q': gain(13, (L, MLA_QK)),
        'g_mla_k': gain(14, (L, MLA_QK)),
        'g_na_q': gain(15, (L, HEAD_DIM)),
        'g_na_k': gain(16, (L, HEAD_DIM)),
        'na_rpb': nrm(17, (L, NA_HEADS, 2 * NA_ROWS - 1, 2 * NA_COLS - 1), 0.02),
        'g_diff_q': gain(18, (L, DIFF_DIM)),
        'g_diff_k': gain(19, (L, DIFF_DIM)),
        'diff_lq1': nrm(20, (L, DIFF_DIM), 0.1),
        'diff_lk1': nrm(21, (L, DIFF_DIM), 0.1),
        'diff_lq2': nrm(22, (L, DIFF_DIM), 0.1),
        'diff_lk2': nrm(23, (L, DIFF_DIM), 0.1),
        'g_diff_sub': gain(24, (L, 2 * DIFF_DIM)),
        'g_gqa_q': gain(25, (L, HEAD_DIM)),
        'g_gqa_k': gain(26, (L, HEAD_DIM)),
        'w_branch': nrm(27, (L, N_BRANCH, BRANCH_WIDTH, D), BRANCH_WIDTH ** -0.5),
        'w_out': nrm(28, (L, D, D), D ** -0.5),
        'w_up': nrm(29, (L, D, D_FF), D ** -0.5),
        'w_down': nrm(30, (L, D_FF, D), D_FF ** -0.5),
    }

def reference(x, c, ctx, c_ctx, w_ada, b_ada, g_norm1, g_norm2, w_in,
              g_mla_qa, w_mla_uq, g_mla_kva, w_mla_ukv, g_mla_q, g_mla_k,
              g_na_q, g_na_k, na_rpb,
              g_diff_q, g_diff_k, diff_lq1, diff_lk1, diff_lq2, diff_lk2, g_diff_sub,
              g_gqa_q, g_gqa_k, w_branch, w_out, w_up, w_down):
    S = x.shape[1]
    t = jnp.arange(S)
    rows, cols = t // GRID_W, t % GRID_W
    rope32 = rope_tables(rows, cols, MLA_ROPE)
    rope64 = rope_tables(rows, cols, HEAD_DIM)
    xc = ctx
    for l in range(DEPTH):
        need_ctx = l < DEPTH - 1
        lam_init = 0.8 - 0.6 * math.exp(-0.3 * l)
        mod = jax.nn.silu(c) @ w_ada[l] + b_ada[l]
        mod_c = jax.nn.silu(c_ctx) @ w_ada[l] + b_ada[l]
        sh1, sc1, gt1, sh2, sc2, gt2 = jnp.split(mod[:, None, :], 6, axis=-1)
        csh1, csc1, cgt1, csh2, csc2, cgt2 = jnp.split(mod_c, 6, axis=-1)

        z = split_last(modulate(rmsnorm(x, g_norm1[l]), sh1, sc1) @ w_in[l], SPLIT_SIZES)
        zc = split_last(modulate(rmsnorm(xc, g_norm1[l]), csh1, csc1) @ w_in[l], SPLIT_SIZES)

        oa, oa_c = mla_mixer(z[0:3], zc[0:3], rope32, g_mla_qa[l], w_mla_uq[l], g_mla_kva[l],
                             w_mla_ukv[l], g_mla_q[l], g_mla_k[l], need_ctx)
        ob, ob_c = na_mixer(z[3], zc[3], g_na_q[l], g_na_k[l], na_rpb[l], need_ctx)
        oc, oc_c = diff_mixer(z[4], zc[4], rope32, g_diff_q[l], g_diff_k[l], diff_lq1[l], diff_lk1[l],
                              diff_lq2[l], diff_lk2[l], g_diff_sub[l], lam_init, need_ctx)
        od, od_c = gqa_mixer(z[5], zc[5], rope64, g_gqa_q[l], g_gqa_k[l], need_ctx)

        x = x + gt1 * merge_branches([oa, ob, oc, od], z[6], w_branch[l], w_out[l])
        x = x + gt2 * sq_relu_mlp(modulate(rmsnorm(x, g_norm2[l]), sh2, sc2), w_up[l], w_down[l])
        if need_ctx:
            xc = xc + cgt1 * merge_branches([oa_c, ob_c, oc_c, od_c], zc[6], w_branch[l], w_out[l])
            xc = xc + cgt2 * sq_relu_mlp(modulate(rmsnorm(xc, g_norm2[l]), csh2, csc2), w_up[l], w_down[l])
    return x


_drawn_inputs = setup_inputs


def setup_inputs(seed=0):
    import zlib

    import numpy as np

    out = dict(_drawn_inputs(seed))
    spreads = {}
    factors = {'g_norm1': 3.587,
     'g_mla_qa': 8.0,
     'g_mla_kva': 8.0,
     'g_mla_q': 8.0,
     'g_mla_k': 8.0,
     'g_na_q': 8.0,
     'g_na_k': 8.0,
     'na_rpb': 8.0,
     'g_diff_q': 8.0,
     'g_diff_k': 8.0,
     'diff_lq1': 8.0,
     'diff_lk1': 8.0,
     'diff_lq2': 8.0,
     'diff_lk2': 8.0,
     'g_diff_sub': 3.187,
     'g_gqa_q': 8.0,
     'g_gqa_k': 8.0}
    for name, (base, spread) in spreads.items():
        noise = np.random.default_rng([zlib.crc32(name.encode()), seed]).standard_normal(out[name].shape)
        drawn = base * np.exp(spread * noise) if base else spread * noise
        out[name] = __import__('jax').numpy.asarray(drawn.astype(out[name].dtype))
    for name, factor in factors.items():
        out[name] = (out[name] * factor).astype(out[name].dtype)
    return out
```

```python
import math
from contextlib import ExitStack

import numpy as np
import concourse.bass as bass
from concourse import mybir

D, DEPTH, S, C = 1024, 2, 512, 256
T = S + C
P = 128
KT = D // P
GW, GR = 64, S // 64
HD, NH = 64, 4
QL, KVL, RD, NOPE, QK = 192, 128, 32, 64, 96
DD = 32
EPS = 1e-6
NEG = -1.0e30
GQA_ORDER = (0, 2, 1, 3)
NT, NTL = T // P, S // P
ZG = 480
NKVG, NQG = 3, 2
ZC = ZG * (NKVG + NQG)
CKV, KR, NAK, NAV, DK, DV, GK, GV, CQ, NAQ, DQ, GQ = np.cumsum(
    [0, 128, 32, 256, 256, 256, 256, 128, 128, 192, 256, 256]).tolist()
MLO = NAK
NZ, NP4, NO, NM = 20, 32, 8, 64
NCH = NZ + NP4 + NO + NM
SLOTS = 4
WMAX = 10 * P
ADA0 = 16
ADAN = 48
names = [("qa", 192), ("kva", 128), ("mq", 96), ("mk", 96), ("nq", 64), ("nk", 64), ("dq", 32),
         ("dk", 32), ("sub", 64), ("gq", 64), ("gk", 64), ("lq1", 32), ("lk1", 32), ("lq2", 32), ("lk2", 32)]
GO, _o = {}, 0
for _n, _w in names:
    GO[_n] = (_o, _w)
    _o += _w
SM = _o


def na_tiles(i):
    return list(range(max(i - 1, 0), min(i + 2, NTL)))


NA_KIND = [0, 1, 1, 2]
NA_TAB = [(0, 256), (256, 384), (640, 256)]
NA_SRC = [128, 0, 0]


def program(nc, a, out):
    f32, f32r = mybir.dt.float32, mybir.dt.float32r
    ALU, ACT, AX = mybir.AluOpType, mybir.ActivationFunctionType, mybir.AxisListType
    ctx = ExitStack()
    with ctx:
        sem = lambda name: ctx.enter_context(nc.semaphore(name))
        persistent = lambda name, shape, dt=f32: ctx.enter_context(nc.sbuf_tensor(name, shape, dt))

        x_sb = persistent("x_sb", [P, KT, T])
        w_hi = persistent("w_hi", [P, SLOTS, WMAX], f32r)
        w_lo = persistent("w_lo", [P, SLOTS, WMAX], f32r)
        w_raw = persistent("w_raw", [P, 2, WMAX])
        ada_w = persistent("ada_w", [P, 2, KT * P])
        rstd = persistent("rstd", [P, T])
        ident = persistent("ident", [P, P])
        ones = persistent("ones", [P, P])
        eps_sb = persistent("eps_sb", [P, 1])
        c_sb = persistent("c_sb", [P, KT, 2])
        csig = persistent("csig", [P, KT, 2])
        csilu = persistent("csilu", [P, KT, 2])
        b_sb = persistent("b_sb", [P, DEPTH, ADAN])
        gn_sb = persistent("gn_sb", [P, DEPTH, 2, KT])
        mod = persistent("mod", [P, DEPTH, ADAN, 2])
        nscale = persistent("nscale", [P, DEPTH, 2, KT, 2])
        neglam = persistent("neglam", [P, 1])
        lam_t = persistent("lam_t", [P, 4])
        lam_p = persistent("lam_p", [P, 2, DD])
        nmax = persistent("nmax", [P, 8, 2, 2])
        rsum = persistent("rsum", [P, 8, 2, 2])
        rinv = persistent("rinv", [P, 8, 2])

        KB = 1024
        Z_END = NT * ZC * 4
        F1 = Z_END
        Y0 = F1 + 2 * KT * T * 4
        A0 = (nc.sbuf_usable_end - (Y0 + 25 * KB)) // 64 * 64
        assert nc.sbuf_base <= A0
        at = lambda name, off, shape, dt=f32: nc.alloc_sbuf_tensor_at(name, shape, dt, offset=A0 + off)
        z = at("z", 0, [P, NT, ZC])
        act0 = at("act0", 0, [P, 2, KT, T], f32r)
        act1 = at("act1", F1, [P, 2, KT, T], f32r)
        ada_init = at("ada_init", 0, [P, ADA0, KT * P])
        sig = at("sig", 48 * KB, [P, 2, T])
        y_sb = at("y_sb", Y0, [P, KT, T])
        n_a = at("n_a", Y0, [P, 2, T])
        n_b = at("n_b", Y0 + 6 * KB, [P, 2, T])
        r_sb = at("r_sb", Y0, [P, 2, T])
        q_sb = at("q_sb", Y0 + 6 * KB, [P, 2, T])
        tmp_z = [at("tmp_z0", Y0, [P, NT, 256]), at("tmp_z1", Y0 + 6 * KB, [P, NT, 256])]
        ss_z = at("ss_z", Y0 + 12 * KB, [P, 256])
        ukv_sb = at("ukv_sb", Y0 + 13 * KB, [P, 512])
        uq_sb = at("uq_sb", Y0 + 15 * KB, [P, 2, 384])
        rope_sb = at("rope_sb", Y0 + 18 * KB, [P, NTL, 192])
        small = at("small", Y0 + 21 * KB, [P, SM])
        A_ = F1
        mtmp = [at("mtmp0", A_, [P, NT, 384]), None]
        cT = at("cT", A_ + 9 * KB, [P, 3, T])
        ss_m = at("ss_m", A_ + 18 * KB, [P, 64])
        mtmp[1] = at("mtmp1", A_ + 19 * KB, [P, NTL, 128])
        mlaq = at("mlaq", A_ + 24 * KB, [P, NT, 384])
        mlak = at("mlak", A_ + 33 * KB, [P, NT, 384])
        mlav = at("mlav", A_ + 42 * KB, [P, NT, 256])
        dtmp = at("dtmp", A_ + 18 * KB, [P, NT, 256])
        QT = at("QT", A_, [P, 2, T])
        KTr = at("KTr", A_ + 6 * KB, [P, 2, T])
        QTm = at("QTm", A_, [P, 4, T])
        KTm = at("KTm", A_ + 12 * KB, [P, 4, T])
        na_T = at("na_T", A_ + 12 * KB, [P, NH, 384])
        na_tab = at("na_tab", A_ + 18 * KB, [P, 896])
        na_mask = at("na_mask", Y0 + 13 * KB, [P, 896])
        Pp = [at("Pp0", Y0, [P, T]), at("Pp1", Y0 + 3 * KB, [P, T])]
        Pq = [at("Pq0", A_ + 12 * KB, [P, T]), at("Pq1", A_ + 15 * KB, [P, T])]
        PTs = at("PTs", Y0 + 6 * KB, [P, 2, T])

        ps = ctx.enter_context(nc.psum_tensor("ps", [P, 8, 512], f32))
        flat = ps[:, :, :].rearrange("p b c -> p (b c)")
        ada_ps = ps[:, 7, :]

        const_in = sem("const_in")
        late_in = sem("late_in")
        na_in = sem("na_in")
        w_in = [sem("w_in0"), sem("w_in1")]
        w_rounded = sem("w_rounded")
        w_ready = sem("w_ready")
        w_used = sem("w_used")
        ada_first = sem("ada_first")
        ada_in = [sem("ada_in0"), sem("ada_in1")]
        ada_used = sem("ada_used")
        pe_phase, act_phase, dve_phase = sem("pe_phase"), sem("act_phase"), sem("dve_phase")
        act_step, dve_step = sem("act_step"), sem("dve_step")
        sq_ready, ssq_done = sem("sq_ready"), sem("ssq_done")
        std_ready, normed, modded, h_ready = sem("std_ready"), sem("normed"), sem("modded"), sem("h_ready")
        z_prod, z_copied = sem("z_prod"), sem("z_copied")
        ss_ready, rt_ready = sem("ss_ready"), sem("rt_ready")
        piece_t, piece_c = sem("piece_t"), sem("piece_c")
        up_done, up_copied = sem("up_done"), sem("up_copied")
        s_ready, max_ready, exp_done = sem("s_ready"), sem("max_ready"), sem("exp_done")
        diff_done = sem("diff_done")
        pt_ready, pt_copied = sem("pt_ready"), sem("pt_copied")
        o_ready, o_done = sem("o_ready"), sem("o_done")
        ot_ready, ot_hi, ot_lo = sem("ot_ready"), sem("ot_hi"), sem("ot_lo")
        bank_free = sem("bank_free")
        sig_ready = sem("sig_ready")
        y_hi, y_ready = sem("y_hi"), sem("y_ready")
        a_hi, a_ready = sem("a_hi"), sem("a_ready")
        c_sig, c_ready, lam_e = sem("c_sig"), sem("c_ready"), sem("lam_e")
        ss_ready_d, rt_d = sem("ss_ready_d"), sem("rt_d")
        relu_ready, gated = sem("relu_ready"), sem("gated")
        mla_prepared, lam_s = sem("mla_prepared"), sem("lam_s")
        out_done = sem("out_done")

        block = ctx.enter_context(nc.Block())

        segs = lambda l: [(0, S), (S, C)] if l == 0 else [(0, S)]
        both = [(0, S), (S, C)]
        ntq = lambda l: NT if l == 0 else NTL
        zt = lambda l, g: NT if g < NKVG else ntq(l)
        zbase = lambda l, g: sum(zt(k, j) for k in range(l) for j in range(5)) + sum(zt(l, j) for j in range(g))
        PREP = [("ckv", CKV, 1, 128, "kva", False, 0, 0), ("nak", NAK, 4, 64, "nk", False, 0, 0),
                ("dk", DK, 8, 32, "dk", False, 32, 1), ("gk", GK, 2, 64, "gk", False, 64, 2),
                ("cq", CQ, 1, 192, "qa", True, 0, 3), ("naq", NAQ, 4, 64, "nq", True, 0, 3),
                ("dq", DQ, 8, 32, "dq", True, 32, 3), ("gq", GQ, 4, 64, "gq", True, 64, 3)]
        NB = 4
        ready_group = [0, 1, 2, 4]
        ss_off, off = {}, 0
        batch_span = []
        for k in range(NB):
            b0 = off
            for p in PREP:
                if p[7] == k:
                    ss_off[p[0]] = off
                    off += NT * p[2]
            batch_span.append((b0, off))
        assert off <= 256

        BR = ("na", "diff", "gqa", "mla")
        PIECES = {"na": 4, "diff": 4, "gqa": 3, "mla": 8}
        units = {l: {b: [(h, t) for h in range(NH) for t in range(ntq(l))] for b in BR} for l in range(DEPTH)}
        nmaps = {"na": 1, "diff": 2, "gqa": 1, "mla": 1}

        def unit_base(l, b):
            u = m = 0
            for k in range(DEPTH):
                for c in BR:
                    if (k, c) == (l, b):
                        return u, m
                    u += len(units[k][c])
                    m += len(units[k][c]) * nmaps[c]

        def piece_base(l, b):
            per = 3 + sum(PIECES.values())
            return l * per + (0 if b == "up" else 3 + sum(PIECES[c] for c in BR[:BR.index(b)]))

        def key_tiles(b, t):
            if t >= NTL:
                return list(range(NTL, NT))
            return (na_tiles(t) if b == "na" else list(range(NTL))) + list(range(NTL, NT))

        def branch_view(b):
            return {"na": ((z, NAQ), (z, NAK), (z, NAV)), "diff": ((z, DQ), (z, DK), (z, DV)),
                    "gqa": ((z, GQ), (z, GK), (z, GV)), "mla": ((mlaq, 0), (mlak, 0), (mlav, 0))}[b]

        def pieces(l, b):
            (qs, q0), (ks, k0), _ = branch_view(b)
            if b == "mla":
                return ([(qs, q0 + 96 * h, 96, ntq(l), QTm[0:96, h, :]) for h in range(4)]
                        + [(ks, k0 + 96 * h, 96, NT, KTm[0:96, h, :]) for h in range(4)])
            nk = 1 if b == "gqa" else 2
            return ([(qs, q0 + 128 * j, 128, ntq(l), QT[:, j, :]) for j in range(2)]
                    + [(ks, k0 + 128 * j, 128, NT, KTr[:, j, :]) for j in range(nk)])

        def o_dest(b, h, t):
            if b == "gqa":
                h = GQA_ORDER[h]
            c0 = {"na": NAQ, "diff": DQ, "gqa": GQ, "mla": MLO}[b] + 64 * h
            return z[:, t, c0:c0 + 64]

        def qk_operands(b, h, mp, t):
            q = slice(t * P, t * P + P)
            if b == "mla":
                return QTm[0:96, h, q], KTm[0:96, h, :]
            if b == "diff":
                r = (h % 2) * 64 + mp * 32
                return QT[r:r + 32, h // 2, q], KTr[r:r + 32, h // 2, :]
            r = (h % 2) * 64
            if b == "na":
                return QT[r:r + 64, h // 2, q], KTr[r:r + 64, h // 2, :]
            return QT[r:r + 64, h // 2, q], KTr[r:r + 64, 0, :]

        def v_slice(b, h, kt):
            (vs, v0) = branch_view(b)[2]
            hv = h % 2 if b == "gqa" else h
            return vs[:, kt, v0 + 64 * hv:v0 + 64 * hv + 64]

        S_BANK = [0, 2]
        PT_BANK, O_BANK = 4, 6

        NSTEP = NP4 + NO + NM
        up_list = lambda l: [("q", t) for t in range(ntq(l))] + [("kv", t) for t in range(NT)]
        up_base = lambda l: sum(len(up_list(k)) for k in range(l))
        h_base = lambda l: l * 3 * KT
        std_seen = lambda l: 2 + 4 * l
        LAST_PHASE = 1 + 14 * DEPTH

        phase = {"pe": 0, "act": 0, "dve": 0}
        norm_no, norm_f = {"act": 0, "dve": 0}, {"act": 0, "dve": 0, "pe": 0}
        PH = {"pe": pe_phase, "act": act_phase, "dve": dve_phase}

        def barrier(eng, me):
            eng.drain().then_inc(PH[me], 1)
            phase[me] += 1
            for other in PH:
                if other != me:
                    eng.wait_ge(PH[other], phase[me])

        CH0 = lambda l: l * NCH

        @block.sync
        def _(sp):
            for dst, src in ((c_sb, a["cT"]), (b_sb, a["b_ada"]), (gn_sb, a["gn"]), (ident, a["ident"])):
                sp.dma_start(dst[:], src).then_inc(const_in, 16)
            for j in range(2):
                n = ADA0 // 2
                sp.dma_start(ada_init[:, j * n:(j + 1) * n, :],
                             a["w_ada"][j * n:(j + 1) * n].rearrange("j p n -> p j n")).then_inc(ada_first, 16)
            sp.dma_start(x_sb[:], a["xT"]).then_inc(const_in, 16)

            def load(c, src, width, k):
                if not isinstance(c, int) or c >= 2:
                    sp.wait_ge(w_ready, c - 1)
                sp.dma_start(w_raw[:, k, 0:width], src).then_inc(w_in[k], 16)

            for l in range(DEPTH):
                c0 = CH0(l)
                for j in range(NZ):
                    load(c0 + j, a["wz"][l, j], 2 * ZG, j % 2)
                c0 += NZ
                with sp.Fori(0, KT) as m:
                    for b in range(4):
                        load(m * 4 + (c0 + b), a["wp"][l * NP4 + 4 * m + b], WMAX, b % 2)
                c0 += NP4
                for j in range(NO):
                    load(c0 + j, a["wo"][l * NO + j], KT * P, j % 2)
                c0 += NO
                with sp.Fori(0, 4) as q:
                    for j in range(16):
                        load(q * 16 + (c0 + j), a["wm"][l * NM + 16 * q + j], KT * P, j % 2)
            sp.wait_ge(dve_phase, LAST_PHASE)
            sp.dma_start(out, x_sb[:, :, 0:S]).then_inc(out_done, 16)
            sp.wait_ge(out_done, 16)

        @block.gpsimd
        def _(pool):
            def low(c, width, k):
                pool.wait_ge(w_rounded, c + 1)
                nc.gpsimd.tensor_tensor(w_lo[:, k, 0:width], w_raw[:, k % 2, 0:width],
                                        w_hi[:, k, 0:width].bitcast(f32), ALU.subtract).then_inc(w_ready, 1)

            for l in range(DEPTH):
                c0 = CH0(l)
                for j in range(NZ):
                    low(c0 + j, 2 * ZG, j % SLOTS)
                c0 += NZ
                with pool.Fori(0, KT) as m:
                    for b in range(4):
                        low(m * 4 + (c0 + b), WMAX, b)
                c0 += NP4
                for j in range(NO):
                    low(c0 + j, KT * P, j % SLOTS)
                c0 += NO
                with pool.Fori(0, 4) as q:
                    for j in range(16):
                        low(q * 16 + (c0 + j), KT * P, j % SLOTS)

        def residual(l, part, m, sg, p):
            for i, (t0, tn) in enumerate(sg):
                ins = nc.vector.scalar_tensor_tensor(
                    x_sb[:, m, t0:t0 + tn], ps[:, 3 * p + 2 * i, 0:tn], mod[:, l, part * KT + m, i:i + 1],
                    x_sb[:, m, t0:t0 + tn], ALU.mult, ALU.add)
            ins.then_inc(bank_free, 1)

        @block.scalar
        def _(act):
            chain = [0]

            def link(ins):
                chain[0] += 1
                ins.then_inc(act_step, 1)
                act.wait_ge(act_step, chain[0])

            def high(c, width, k, first=False):
                act.wait_ge(w_in[k % 2], (c // 2) * 16 + 16 if isinstance(c, int) else c * 8 + (16 - 8 * (k % 2)))
                if not first:
                    act.wait_ge(w_used, c - 3)
                nc.scalar.activation(w_hi[:, k, 0:width], w_raw[:, k % 2, 0:width], ACT.Copy).then_inc(w_rounded, 1)

            def norm(l, which, dst, sg, fresh):
                n = norm_no["act"]
                if fresh:
                    for kt in range(KT):
                        if kt >= 2:
                            act.wait_ge(ssq_done, norm_f["act"] * KT + kt - 1)
                        nc.scalar.activation(n_a[:, kt % 2, 0:sg[-1][0] + sg[-1][1]],
                                             x_sb[:, kt, 0:sg[-1][0] + sg[-1][1]],
                                             ACT.Square).then_inc(sq_ready, 1)
                    norm_f["act"] += 1
                    act.wait_ge(ssq_done, norm_f["act"] * KT)
                    for i, (t0, tn) in enumerate(sg):
                        nc.scalar.activation(rstd[:, t0:t0 + tn], ps[:, i, 0:tn], ACT.Sqrt, bias=eps_sb[:, 0:1],
                                             scale=1.0 / D).then_inc(std_ready, 1)
                for kt in range(KT):
                    act.wait_ge(normed, n * KT + kt + 1)
                    if kt >= 2:
                        act.wait_ge(h_ready, n * KT + kt - 1)
                    for v, (t0, tn) in enumerate(sg):
                        ins = nc.scalar.activation(n_a[:, kt % 2, t0:t0 + tn], n_b[:, kt % 2, t0:t0 + tn], ACT.Identity,
                                                   bias=mod[:, l, (3 * which) * KT + kt, v:v + 1],
                                                   scale=nscale[:, l, which, kt, v:v + 1])
                        if v < len(sg) - 1:
                            continue
                        link(ins)
                    tt = sg[-1][0] + sg[-1][1]
                    nc.scalar.activation(dst[:, 0, kt, 0:tt], n_a[:, kt % 2, 0:tt], ACT.Copy).then_inc(modded, 1)
                norm_no["act"] += 1

            
            act.wait_ge(const_in, 16 * 5)
            nc.scalar.activation(csig[:], c_sb[:], ACT.Sigmoid).then_inc(c_sig, 1)
            for c in range(SLOTS):
                high(c, 2 * ZG, c, first=True)
            barrier(act, "act")

            for l in range(DEPTH):
                sg, c0 = segs(l), CH0(l)
                for dst, src in ((small, a["small"][l:l + 1, :].to_broadcast([P, SM])), (rope_sb, a["rope"]),
                                 (uq_sb, a["uq"][l]), (ukv_sb, a["ukv"][l])):
                    act.dma_start(dst[:], src).then_inc(late_in, 16)
                norm(l, 0, act1, both, True)
                for g in range(5):
                    n = zt(l, g)
                    for tt in range(n):
                        if tt == n - 1:
                            for i in range(4):
                                cc = 4 * g + 4 + i
                                high(c0 + cc, 2 * ZG if cc < NZ else WMAX, cc % SLOTS)
                        act.wait_ge(z_prod, zbase(l, g) + tt + 1)
                        nc.scalar.activation(z[:, tt, g * ZG:(g + 1) * ZG], ps[:, (zbase(l, g) + tt) % 2, 0:ZG],
                                             ACT.Copy).then_inc(z_copied, 1)
                    if g in (1, 2, 3):
                        k = g - 1
                        act.wait_ge(ss_ready, l * (NB + 1) + k + 1)
                        s0, s1 = batch_span[k]
                        nc.scalar.activation(ss_z[:, s0:s1], ss_z[:, s0:s1], ACT.Sqrt).then_inc(rt_ready, 1)
                k = 3
                act.wait_ge(ss_ready, l * (NB + 1) + k + 1)
                for i, p in enumerate([p for p in PREP if p[7] == 3]):
                    s0 = ss_off[p[0]]
                    s1 = s0 + ntq(l) * p[2]
                    ins = nc.scalar.activation(ss_z[:, s0:s1], ss_z[:, s0:s1], ACT.Sqrt)
                ins.then_inc(rt_ready, 1)
                act.wait_ge(lam_s, l + 1)
                nc.scalar.activation(lam_t[:, 2:4], lam_t[:, 0:2], ACT.Exp).then_inc(lam_e, 1)
                barrier(act, "act")
                barrier(act, "act")
                act.wait_ge(ss_ready, l * (NB + 1) + NB + 1)
                for s0, s1 in ((0, 4 * ntq(l)), (24, 48)):
                    ins = nc.scalar.activation(ss_m[:, s0:s1], ss_m[:, s0:s1], ACT.Sqrt)
                ins.then_inc(rt_ready, 1)
                act.wait_ge(mla_prepared, l + 1)
                act.dma_start(na_T[:], a["na_rows"][l].rearrange("h p n -> p h n")).then_inc(na_in, 16)
                act.dma_start(na_mask[:], a["na_mask"]).then_inc(na_in, 16)
                for b in BR:
                    barrier(act, "act")
                    ub, mb = unit_base(l, b)
                    us = units[l][b]

                    def exps(u):
                        h, t = us[u]
                        kts = key_tiles(b, t)
                        if u >= 2:
                            act.wait_ge(pt_ready, ub + u - 1)
                        for mp in range(nmaps[b]):
                            m = u * nmaps[b] + mp
                            act.wait_ge(max_ready, mb + m + 1)
                            dst = (Pq if mp else Pp)[u % 2]
                            s = flat[:, S_BANK[m % 2] * 512:S_BANK[m % 2] * 512 + T]
                            e = (ub + u) % 8
                            W = P * len(kts)
                            if b == "na" and t < NTL:
                                L = W - C
                                nc.scalar.activation(dst[:, 0:L], dst[:, 0:L], ACT.Exp, bias=nmax[:, e, 0, 0:1],
                                                     accum_out=rsum[:, e, 0, 0:1])
                                nc.scalar.activation(dst[:, L:W], s[:, 512:512 + C], ACT.Exp, bias=nmax[:, e, 0, 0:1],
                                                     accum_out=rsum[:, e, 0, 1:2]).then_inc(exp_done, 1)
                            else:
                                nc.scalar.activation(dst[:, 0:W], s[:, 0:W], ACT.Exp, bias=nmax[:, e, mp, 0:1],
                                                     accum_out=rsum[:, e, mp, 0:1]).then_inc(exp_done, 1)

                    def pt_copy(u):
                        W = P * len(key_tiles(b, us[u][1]))
                        act.wait_ge(pt_ready, ub + u + 1)
                        if u >= 2:
                            act.wait_ge(o_ready, ub + u - 1)
                        nc.scalar.activation(PTs[:, u % 2, 0:W], flat[:, PT_BANK * 512:PT_BANK * 512 + W],
                                             ACT.Copy).then_inc(pt_copied, 1)

                    exps(0)
                    for u in range(len(us)):
                        if u + 1 < len(us):
                            exps(u + 1)
                        pt_copy(u)
                    if b == "diff":
                        act.wait_ge(ss_ready_d, l + 1)
                        nc.scalar.activation(ss_z[:, 0:4 * ntq(l)], ss_z[:, 0:4 * ntq(l)], ACT.Sqrt).then_inc(rt_d, 1)
                    barrier(act, "act")
                for i in range(8):
                    act.wait_ge(ot_ready, l * 8 + i + 1)
                    tn = ntq(l) * P
                    src = flat[:, (i % 3) * 1024:(i % 3) * 1024 + tn]
                    nc.scalar.activation(act1[:, 0, i, 0:tn], src, ACT.Copy).then_inc(ot_hi, 1)
                barrier(act, "act")
                norm(l, 0, act0, sg, False)
                s0b, cb = l * NSTEP, c0 + NZ
                ada_on = l == 0
                if ada_on:
                    for n in range(2):
                        act.dma_start(ada_w[:, n, :], a["w_ada"][ADA0 + n]).then_inc(ada_in[n], 16)
                with act.Fori(0, KT) as m:
                    for bb in range(4):
                        act.wait_ge(w_used, m * 4 + (cb + bb + 1))
                        p = bb % 2
                        for i, (t0, tn) in enumerate(sg):
                            ins = nc.scalar.activation(sig[:, p, t0:t0 + tn],
                                                       ps[:, 3 * p, 0:tn] if i == 0 else ps[:, 3 * p + 2, 0:tn], ACT.Sigmoid)
                        ins.then_inc(sig_ready, 1)
                        high(m * 4 + (cb + bb + 4), WMAX, bb)
                        if ada_on:
                            act.wait_ge(ada_used, m * 4 + (bb + 1))
                            act.dma_start(ada_w[:, bb % 2, :], a["w_ada"][m * 4 + (ADA0 + bb + 2)]).then_inc(ada_in[bb % 2], 16)
                barrier(act, "act")
                tt = sg[-1][0] + sg[-1][1]
                for kt in range(KT):
                    nc.scalar.activation(act0[:, 0, kt, 0:tt], y_sb[:, kt, 0:tt], ACT.Copy).then_inc(y_hi, 1)
                cb += NP4
                for j in range(NO):
                    high(cb + j + 4, KT * P, j % SLOTS)
                barrier(act, "act")
                norm(l, 1, act1, sg, True)
                cb += NO

                def quarter(q, last):
                    for j in range(16):
                        c = q * 16 + (cb + j)
                        act.wait_ge(w_used, c + 1)
                        if j < 8:
                            p = j % 2
                            for i, (t0, tn) in enumerate(sg):
                                ins = nc.scalar.activation(r_sb[:, p, t0:t0 + tn],
                                                           ps[:, 3 * p + 2 * i, 0:tn], ACT.Relu)
                            ins.then_inc(relu_ready, 1)
                            act.wait_ge(relu_ready, q * 8 + (l * 32 + j + 1))
                            nc.scalar.activation(act0[:, 0, j, 0:tt], r_sb[:, p, 0:tt], ACT.Square).then_inc(a_hi, 1)
                        if not last:
                            high(c + 4, KT * P, j % SLOTS)
                        elif j < 12:
                            high(c + 4, KT * P, j % SLOTS)
                        elif l + 1 < DEPTH:
                            high(c + 4, 2 * ZG, j % SLOTS)
                        if ada_on and j < 12 and not (last and j >= 10):
                            act.wait_ge(ada_used, q * 12 + (NP4 + j + 1))
                            act.dma_start(ada_w[:, j % 2, :], a["w_ada"][q * 12 + (ADAN + j + 2)]).then_inc(ada_in[j % 2], 16)

                with act.Fori(0, 3) as q:
                    quarter(q, False)
                quarter(3, True)
                barrier(act, "act")

        @block.vector
        def _(dve):
            chain = [0]

            def link(ins):
                chain[0] += 1
                ins.then_inc(dve_step, 1)
                dve.wait_ge(dve_step, chain[0])

            tt_op = nc.vector.tensor_tensor

            def take_mod(l, j0, j1):
                src = ada_ps[:, l * 2 * ADAN + 2 * j0:l * 2 * ADAN + 2 * j1].rearrange("p (j v) -> p j v", v=2)
                link(tt_op(mod[:, l, j0:j1, :], src, b_sb[:, l, j0:j1].unsqueeze(2).to_broadcast([P, j1 - j0, 2]), ALU.add))

            def take_scale(l, which):
                j0 = (3 * which + 1) * KT
                link(nc.vector.tensor_scalar(nscale[:, l, which, :, :], mod[:, l, j0:j0 + KT, :], 1.0, None, ALU.add))
                link(tt_op(nscale[:, l, which, :, :], nscale[:, l, which, :, :],
                           gn_sb[:, l, which, :].unsqueeze(2).to_broadcast([P, KT, 2]), ALU.mult))

            def norm(l, which, dst, sg, fresh):
                n = norm_no["dve"]
                tt = sg[-1][0] + sg[-1][1]
                if fresh:
                    norm_f["dve"] += len(sg)
                    dve.wait_ge(std_ready, norm_f["dve"])
                    link(nc.vector.reciprocal(rstd[:, 0:tt], rstd[:, 0:tt]))

                def times(kt):
                    if kt >= 2:
                        dve.wait_ge(modded, n * KT + kt - 1)
                    tt_op(n_b[:, kt % 2, 0:tt], x_sb[:, kt, 0:tt], rstd[:, 0:tt], ALU.mult).then_inc(normed, 1)

                times(0)
                for kt in range(KT):
                    if kt + 1 < KT:
                        times(kt + 1)
                    dve.wait_ge(modded, n * KT + kt + 1)
                    tt_op(dst[:, 1, kt, 0:tt], n_a[:, kt % 2, 0:tt], dst[:, 0, kt, 0:tt].bitcast(f32),
                          ALU.subtract).then_inc(h_ready, 1)
                norm_no["dve"] += 1

            def sums(src, c0, heads, d, nt, tmp, ss):
                v = src[:, 0:nt, c0:c0 + heads * d]
                w = tmp[:, 0:nt, 0:heads * d]
                link(tt_op(w, v, v, ALU.mult))
                link(nc.vector.tensor_reduce(ss, w.rearrange("p t (h d) -> p t h d", d=d), AX.X, ALU.add))
                return nc.vector.tensor_scalar(ss, ss, 1.0 / d, EPS, ALU.mult, ALU.add)

            def scale_rows(src, c0, heads, d, nt, ss, g, mul):
                link(nc.vector.reciprocal(ss, ss))
                for t in range(nt):
                    v = src[:, t, c0:c0 + heads * d].rearrange("p (h d) -> p h d", d=d)
                    ins = tt_op(v, v, ss[:, t, :].unsqueeze(2).to_broadcast([P, heads, d]), ALU.mult)
                link(ins)
                o, w = GO[g]
                for t in range(nt):
                    v = src[:, t, c0:c0 + heads * d].rearrange("p (h d) -> p h d", d=d)
                    gb = small[:, o:o + w].unsqueeze(1).to_broadcast([P, heads, d])
                    if mul == 1.0:
                        ins = tt_op(v, v, gb, ALU.mult)
                    else:
                        ins = nc.vector.scalar_tensor_tensor(v, v, mul, gb, ALU.mult, ALU.mult)
                link(ins)

            def rope(src, c0, heads, stride, d, tab, tmp):
                n = d // 4
                for t in range(NTL):
                    s0 = c0 - (stride - d)
                    v = src[:, t, s0:s0 + heads * stride].rearrange("p (h s) -> p h s", s=stride)[:, :, stride - d:stride]
                    w = tmp[:, t, 0:heads * d].rearrange("p (h d) -> p h d", d=d)
                    cos = rope_sb[:, t, tab:tab + d].unsqueeze(1).to_broadcast([P, heads, d])
                    sin = rope_sb[:, t, tab + d:tab + 2 * d]
                    for q in range(4):
                        o = q ^ 1
                        ins = tt_op(w[:, :, q * n:(q + 1) * n], v[:, :, o * n:(o + 1) * n],
                                    sin[:, q * n:(q + 1) * n].unsqueeze(1).to_broadcast([P, heads, n]), ALU.mult)
                    link(ins)
                    link(tt_op(v, v, cos, ALU.mult))
                    ins = tt_op(v, v, w, ALU.add)
                link(ins)

            nc.vector.memset(ones[:], 1.0)
            ins = nc.vector.memset(eps_sb[:], EPS)
            link(ins)
            
            dve.drain().then_inc(bank_free, 2)
            dve.wait_ge(c_sig, 1)
            dve.wait_ge(const_in, 16 * 5)
            tt_op(csilu[:], c_sb[:], csig[:], ALU.mult).then_inc(c_ready, 1)
            dve.wait_ge(pe_phase, 1)
            take_mod(0, 0, ADA0)
            take_scale(0, 0)
            barrier(dve, "dve")

            for l in range(DEPTH):
                sg, c0 = segs(l), CH0(l)
                lam_init = 0.8 - 0.6 * math.exp(-0.3 * l)
                norm(l, 0, act1, both, True)
                dve.wait_ge(late_in, 16 * 4 * (l + 1))
                for k in range(NB):
                    g = ready_group[k]
                    dve.wait_ge(z_copied, zbase(l, g) + zt(l, g))
                    group = [p for p in PREP if p[7] == k]
                    for p in group:
                        nt = ntq(l) if p[5] else NT
                        ss = ss_z[:, ss_off[p[0]]:ss_off[p[0]] + nt * p[2]].rearrange("p (t h) -> p t h", h=p[2])
                        ins = sums(z, p[1], p[2], p[3], nt, tmp_z[0], ss)
                        if p is group[-1]:
                            ins.then_inc(ss_ready, 1)
                        else:
                            link(ins)
                    dve.wait_ge(rt_ready, l * (NB + 1) + k + 1)
                    for p in group:
                        nt = ntq(l) if p[5] else NT
                        ss = ss_z[:, ss_off[p[0]]:ss_off[p[0]] + nt * p[2]].rearrange("p (t h) -> p t h", h=p[2])
                        mul = {"naq": HD ** -0.5, "dq": DD ** -0.5, "gq": HD ** -0.5}.get(p[0], 1.0)
                        scale_rows(z, p[1], p[2], p[3], nt, ss, p[4], mul)
                        if p[6]:
                            rope(z, p[1], p[2], p[3], p[3], 0 if p[6] == 64 else 128, tmp_z[1])
                for i, (u, v) in enumerate((("lq1", "lk1"), ("lq2", "lk2"))):
                    u, v = GO[u][0], GO[v][0]
                    link(tt_op(lam_p[:, i, :], small[:, u:u + DD], small[:, v:v + DD], ALU.mult))
                    ins = nc.vector.tensor_reduce(lam_t[:, i:i + 1], lam_p[:, i, :], AX.X, ALU.add)
                ins.then_inc(lam_s, 1)
                dve.wait_ge(lam_e, l + 1)
                link(tt_op(neglam[:], lam_t[:, 3:4], lam_t[:, 2:3], ALU.subtract))
                link(nc.vector.tensor_scalar(neglam[:], neglam[:], -lam_init, None, ALU.add))
                barrier(dve, "dve")
                pb = piece_base(l, "up")
                for i in range(3):
                    rows, n = ((P, ntq(l)), (64, ntq(l)), (P, NT))[i]
                    dve.wait_ge(piece_t, pb + i + 1)
                    nc.vector.tensor_copy(cT[0:rows, i, 0:n * P],
                                          flat[0:rows, S_BANK[i % 2] * 512:S_BANK[i % 2] * 512 + n * P]).then_inc(piece_c, 1)
                for i in range(len(up_list(l))):
                    kind, t = up_list(l)[i]
                    dve.wait_ge(up_done, up_base(l) + i + 1)
                    bank = 4 + i % 2
                    if kind == "q":
                        nc.vector.tensor_copy(mlaq[:, t, :], ps[:, bank, 0:384]).then_inc(up_copied, 1)
                    else:
                        nc.vector.tensor_copy(mlak[:, t, :].rearrange("p (h d) -> p h d", d=QK)[:, :, 0:NOPE],
                                              ps[:, bank, 0:256].rearrange("p (h d) -> p h d", d=NOPE))
                        nc.vector.tensor_copy(mlak[:, t, :].rearrange("p (h d) -> p h d", d=QK)[:, :, NOPE:QK],
                                              z[:, t, KR:KR + RD].unsqueeze(1).to_broadcast([P, NH, RD]))
                        nc.vector.tensor_copy(mlav[:, t, :], ps[:, bank, 256:512]).then_inc(up_copied, 1)
                dve.wait_ge(up_copied, up_base(l) + len(up_list(l)))
                barrier(dve, "dve")
                ssq = ss_m[:, 0:4 * ntq(l)].rearrange("p (t h) -> p t h", h=4)
                ssk = ss_m[:, 24:48].rearrange("p (t h) -> p t h", h=4)
                link(sums(mlaq, 0, 4, QK, ntq(l), mtmp[0], ssq))
                sums(mlak, 0, 4, QK, NT, mtmp[0], ssk).then_inc(ss_ready, 1)
                dve.wait_ge(rt_ready, l * (NB + 1) + NB + 1)
                scale_rows(mlaq, 0, 4, QK, ntq(l), ssq, "mq", QK ** -0.5)
                scale_rows(mlak, 0, 4, QK, NT, ssk, "mk", 1.0)
                rope(mlaq, NOPE, 4, QK, RD, 128, mtmp[1])
                rope(mlak, NOPE, 4, QK, RD, 128, mtmp[1])
                dve.drain().then_inc(mla_prepared, 1)

                for b in BR:
                    pb = piece_base(l, b)
                    for i, (src, col, w, n, dst) in enumerate(pieces(l, b)):
                        dve.wait_ge(piece_t, pb + i + 1)
                        nc.vector.tensor_copy(dst[:, 0:n * P], flat[0:w, S_BANK[i % 2] * 512:S_BANK[i % 2] * 512 + n * P]).then_inc(piece_c, 1)
                    if b == "na":
                        dve.wait_ge(na_in, 32 * (l + 1))
                    barrier(dve, "dve")
                    ub, mb = unit_base(l, b)
                    us = units[l][b]

                    def maxima(u):
                        h, t = us[u]
                        kts = key_tiles(b, t)
                        W = P * len(kts)
                        e = (ub + u) % 8
                        if b == "na" and t == 0:
                            for (o, w), s0 in zip(NA_TAB, NA_SRC):
                                ins = tt_op(na_tab[:, o:o + w], na_T[:, h, s0:s0 + w], na_mask[:, o:o + w], ALU.add)
                            link(ins)
                        for mp in range(nmaps[b]):
                            m = u * nmaps[b] + mp
                            dve.wait_ge(s_ready, mb + m + 1)
                            s = flat[:, S_BANK[m % 2] * 512:S_BANK[m % 2] * 512 + T]
                            if b == "na" and t < NTL:
                                L = W - C
                                o, w = NA_TAB[NA_KIND[t]]
                                if u >= 2:
                                    dve.wait_ge(pt_ready, ub + u - 1)
                                link(nc.vector.tensor_tensor_reduce(
                                    out=Pp[u % 2][:, 0:L], in0=s[:, 0:L], in1=na_tab[:, o:o + w], scale=1.0,
                                    scalar=NEG, op0=ALU.add, op1=ALU.max, accum_out=nmax[:, e, 1, 0:1]))
                                link(nc.vector.tensor_reduce(nmax[:, e, 1, 1:2], s[:, 512:512 + C], AX.X, ALU.max, negate=True))
                                nc.vector.scalar_tensor_tensor(nmax[:, e, 0, 0:1], nmax[:, e, 1, 0:1], -1.0,
                                                               nmax[:, e, 1, 1:2], ALU.mult, ALU.min).then_inc(max_ready, 1)
                            else:
                                nc.vector.tensor_reduce(nmax[:, e, mp, 0:1], s[:, 0:W], AX.X, ALU.max,
                                                        negate=True).then_inc(max_ready, 1)

                    def combine(u):
                        e = (ub + u) % 8
                        W = P * len(key_tiles(b, us[u][1]))
                        dve.wait_ge(exp_done, mb + 2 * u + 2)
                        link(nc.vector.reciprocal(rinv[:, e, :], rsum[:, e, :, 0]))
                        link(nc.vector.scalar_tensor_tensor(rinv[:, e, 1:2], rinv[:, e, 1:2], neglam[:, 0:1],
                                                            rsum[:, e, 0, 0:1], ALU.mult, ALU.mult))
                        nc.vector.scalar_tensor_tensor(Pp[u % 2][:, 0:W], Pq[u % 2][:, 0:W], rinv[:, e, 1:2],
                                                       Pp[u % 2][:, 0:W], ALU.mult, ALU.add).then_inc(diff_done, 1)

                    def outputs(u):
                        h, t = us[u]
                        e = (ub + u) % 8
                        if b != "diff":
                            dve.wait_ge(exp_done, mb + u + 1)
                            if b == "na" and t < NTL:
                                link(tt_op(rsum[:, e, 0, 0:1], rsum[:, e, 0, 0:1], rsum[:, e, 0, 1:2], ALU.add))
                            link(nc.vector.reciprocal(rinv[:, e, 0:1], rsum[:, e, 0, 0:1]))
                        dve.wait_ge(o_ready, ub + u + 1)
                        nc.vector.tensor_scalar(o_dest(b, h, t), ps[:, O_BANK + u % 2, 0:HD],
                                                rinv[:, e, 0:1], None, ALU.mult).then_inc(o_done, 1)

                    maxima(0)
                    if b == "diff":
                        combine(0)
                    for u in range(len(us)):
                        if u + 1 < len(us):
                            maxima(u + 1)
                        if u >= 1:
                            outputs(u - 1)
                        if b == "diff" and u + 1 < len(us):
                            combine(u + 1)
                    outputs(len(us) - 1)
                    if b == "diff":
                        dve.wait_ge(o_done, ub + len(us))
                        ss = ss_z[:, 0:4 * ntq(l)].rearrange("p (t h) -> p t h", h=4)
                        sums(z, DQ, 4, 64, ntq(l), dtmp, ss).then_inc(ss_ready_d, 1)
                        dve.wait_ge(rt_d, l + 1)
                        scale_rows(z, DQ, 4, 64, ntq(l), ss, "sub", 1.0 - lam_init)
                    barrier(dve, "dve")
                for i in range(8):
                    dve.wait_ge(ot_hi, l * 8 + i + 1)
                    tn = ntq(l) * P
                    src = flat[:, (i % 3) * 1024:(i % 3) * 1024 + tn]
                    tt_op(act1[:, 1, i, 0:tn], src, act1[:, 0, i, 0:tn].bitcast(f32), ALU.subtract).then_inc(ot_lo, 1)
                barrier(dve, "dve")
                norm(l, 0, act0, sg, False)
                fb = 2 + l * NSTEP
                with dve.Fori(0, KT) as m:
                    for bb in range(4):
                        p = bb % 2
                        dve.wait_ge(sig_ready, m * 4 + (l * NP4 + bb + 1))
                        for i, (t0, tn) in enumerate(sg):
                            src = ps[:, 3 * p + 1, 0:tn] if i == 0 else ps[:, 3 * p + 2, C:2 * C]
                            dst = y_sb[:, m, t0:t0 + tn] if bb == 0 else sig[:, p, t0:t0 + tn]
                            ins = tt_op(dst, sig[:, p, t0:t0 + tn], src, ALU.mult)
                        tt = sg[-1][0] + sg[-1][1]
                        if bb:
                            ins.then_inc(gated, 1)
                            dve.wait_ge(gated, m * 3 + (l * 24 + bb))
                            ins = tt_op(y_sb[:, m, 0:tt], y_sb[:, m, 0:tt], sig[:, p, 0:tt], ALU.add)
                        ins.then_inc(bank_free, 1)
                        dve.wait_ge(bank_free, m * 4 + (fb + bb + 1))
                if l == 0:
                    dve.wait_ge(ada_used, NP4)
                    take_mod(0, ADA0, ADAN)
                    take_scale(0, 1)
                barrier(dve, "dve")
                fb += NP4
                for kt in range(KT):
                    dve.wait_ge(y_hi, l * KT + kt + 1)
                    tt_op(act0[:, 1, kt, 0:tt], y_sb[:, kt, 0:tt], act0[:, 0, kt, 0:tt].bitcast(f32),
                          ALU.subtract).then_inc(y_ready, 1)
                for j in range(NO):
                    dve.wait_ge(w_used, c0 + NZ + NP4 + j + 1)
                    residual(l, 2, j, sg, j % 2)
                fb += NO
                barrier(dve, "dve")
                norm(l, 1, act1, sg, True)
                cb = c0 + NZ + NP4 + NO

                def quarter(q):
                    for j in range(8):
                        dve.wait_ge(a_hi, q * 8 + (l * 32 + j + 1))
                        tt_op(q_sb[:, j % 2, 0:tt], r_sb[:, j % 2, 0:tt], r_sb[:, j % 2, 0:tt], ALU.mult).then_inc(bank_free, 1)
                        dve.wait_ge(bank_free, q * 16 + (fb + j + 1))
                        tt_op(act0[:, 1, j, 0:tt], q_sb[:, j % 2, 0:tt], act0[:, 0, j, 0:tt].bitcast(f32),
                              ALU.subtract).then_inc(a_ready, 1)
                    for j in range(8):
                        dve.wait_ge(w_used, q * 16 + (cb + 8 + j + 1))
                        residual(l, 5, j, sg, j % 2)
                        dve.wait_ge(bank_free, q * 16 + (fb + 8 + j + 1))

                with dve.Fori(0, 4) as q:
                    quarter(q)
                if l == 0:
                    dve.wait_ge(ada_used, NP4 + ADAN)
                    take_mod(1, 0, ADAN)
                    take_scale(1, 0)
                    take_scale(1, 1)
                barrier(dve, "dve")

        @block.tensor
        def _(pe):
            mm, tr = nc.tensor.matmul, nc.tensor.transpose

            def norm(sg, fresh):
                if not fresh:
                    return
                n = norm_f["pe"]
                for kt in range(KT):
                    pe.wait_ge(sq_ready, n * KT + kt + 1)
                    for i, (t0, tn) in enumerate(sg):
                        ins = mm(ps[:, i, 0:tn], ones[:], n_a[:, kt % 2, t0:t0 + tn], start=kt == 0, stop=kt == KT - 1)
                    ins.then_inc(ssq_done, 1)
                norm_f["pe"] += 1

            def chunk_products(outs, slot, kts, act_t, act_kt, sg, before=None):
                for i, kt in enumerate(kts):
                    if before:
                        before(i)
                    for n, (w, h) in enumerate(((w_hi, 0), (w_hi, 1), (w_lo, 0))):
                        for o, (t0, tn) in zip(outs, sg):
                            ins = mm(o[:, 0:tn], w[:, slot, kt * P:kt * P + P], act_t[:, h, act_kt + i, t0:t0 + tn],
                                     start=i == 0 and n == 0, stop=i == len(kts) - 1 and n == 2)
                return ins

            def ada_product(w, col):
                for kt in range(KT):
                    ins = mm(ada_ps[:, col] if not isinstance(col, int) else ada_ps[:, col:col + 2],
                             w[:, kt * P:kt * P + P], csilu[:, kt, :], start=kt == 0, stop=kt == KT - 1)
                return ins

            pe.wait_ge(const_in, 16 * 5)
            pe.wait_ge(c_ready, 1)
            for j in range(ADA0):
                if j % (ADA0 // 2) == 0:
                    pe.wait_ge(ada_first, 32)
                ada_product(ada_init[:, j, :], 2 * j)
            barrier(pe, "pe")

            for l in range(DEPTH):
                sg, c0 = segs(l), CH0(l)
                norm(both, True)
                for g in range(5):
                    n = zt(l, g)
                    for tt in range(n):
                        k = zbase(l, g) + tt
                        if g == 0 and tt == 0:
                            pe.wait_ge(std_ready, std_seen(l))
                        elif k >= 2:
                            pe.wait_ge(z_copied, k - 1)
                        for kt in range(KT):
                            if tt == 0 and kt % 2 == 0:
                                pe.wait_ge(w_ready, c0 + 4 * g + kt // 2 + 1)
                            if g == 0 and tt == 0:
                                pe.wait_ge(h_ready, h_base(l) + kt + 1)
                            slot, w0 = (4 * g + kt // 2) % SLOTS, (kt % 2) * ZG
                            for i, (h, w) in enumerate(((0, w_hi), (1, w_hi), (0, w_lo))):
                                ins = mm(ps[:, k % 2, 0:ZG], act1[:, h, kt, tt * P:tt * P + P], w[:, slot, w0:w0 + ZG],
                                         start=kt == 0 and i == 0, stop=kt == KT - 1 and i == 2)
                            if tt == n - 1 and kt % 2 == 1 and kt < KT - 1:
                                ins.then_inc(w_used, 1)
                        ins.then_inc(z_prod, 1)
                        if tt == n - 1:
                            pe.drain().then_inc(w_used, 1)
                barrier(pe, "pe")
                pb = piece_base(l, "up")
                for i, (col, w, n) in enumerate(((CQ, P, ntq(l)), (CQ + P, 64, ntq(l)), (CKV, P, NT))):
                    if i >= 2:
                        pe.wait_ge(piece_c, pb + i - 1)
                    for t in range(n):
                        c_ = S_BANK[i % 2] * 512 + t * P
                        ins = tr(flat[0:w, c_:c_ + P], z[:, t, col:col + w], ident[:])
                    ins.then_inc(piece_t, 1)
                pe.wait_ge(piece_c, pb + 3)
                for i, (kind, t) in enumerate(up_list(l)):
                    if i >= 2:
                        pe.wait_ge(up_copied, up_base(l) + i - 1)
                    bank = 4 + i % 2
                    if kind == "q":
                        mm(ps[:, bank, 0:384], cT[:, 0, t * P:t * P + P], uq_sb[:, 0, :], start=True, stop=False)
                        ins = mm(ps[:, bank, 0:384], cT[0:64, 1, t * P:t * P + P], uq_sb[0:64, 1, :], start=False, stop=True)
                    else:
                        ins = mm(ps[:, bank, :], cT[:, 2, t * P:t * P + P], ukv_sb[:], start=True, stop=True)
                    ins.then_inc(up_done, 1)
                barrier(pe, "pe")
                for b in BR:
                    pb = piece_base(l, b)
                    for i, (src, col, w, n, dst) in enumerate(pieces(l, b)):
                        if i >= 2:
                            pe.wait_ge(piece_c, pb + i - 1)
                        for t in range(n):
                            c_ = S_BANK[i % 2] * 512 + t * P
                            ins = tr(flat[0:w, c_:c_ + P], src[:, t, col:col + w], ident[:])
                        ins.then_inc(piece_t, 1)
                    barrier(pe, "pe")
                    ub, mb = unit_base(l, b)
                    us = units[l][b]

                    def scores(u):
                        h, t = us[u]
                        kts = key_tiles(b, t)
                        for mp in range(nmaps[b]):
                            m = u * nmaps[b] + mp
                            if m >= 2:
                                pe.wait_ge(exp_done, mb + m - 1)
                            s = flat[:, S_BANK[m % 2] * 512:S_BANK[m % 2] * 512 + T]
                            q, k = qk_operands(b, h, mp, t)
                            lat = [x for x in kts if x < NTL]
                            if lat:
                                ins = mm(s[:, 0:P * len(lat)], q, k[:, lat[0] * P:(lat[-1] + 1) * P], start=True, stop=True)
                                ins = mm(s[:, S:T], q, k[:, S:T], start=True, stop=True)
                            else:
                                ins = mm(s[:, 0:C], q, k[:, S:T], start=True, stop=True)
                            ins.then_inc(s_ready, 1)

                    def transposes(u):
                        if b == "diff":
                            pe.wait_ge(diff_done, l * len(us0) + u + 1)
                        else:
                            pe.wait_ge(exp_done, mb + u + 1)
                        if u >= 1:
                            pe.wait_ge(pt_copied, ub + u)
                        for j in range(len(key_tiles(b, us[u][1]))):
                            c_ = PT_BANK * 512 + j * P
                            ins = tr(flat[:, c_:c_ + P], Pp[u % 2][:, j * P:j * P + P], ident[:])
                        ins.then_inc(pt_ready, 1)

                    def values(u):
                        h, t = us[u]
                        kts = key_tiles(b, t)
                        pe.wait_ge(pt_copied, ub + u + 1)
                        if u >= 2:
                            pe.wait_ge(o_done, ub + u - 1)
                        for j, kt in enumerate(kts):
                            ins = mm(ps[:, O_BANK + u % 2, 0:HD], PTs[:, u % 2, j * P:j * P + P],
                                     v_slice(b, h, kt), start=j == 0, stop=j == len(kts) - 1)
                        ins.then_inc(o_ready, 1)

                    us0 = units[0][b]
                    scores(0)
                    for u in range(len(us)):
                        if u + 1 < len(us):
                            scores(u + 1)
                        transposes(u)
                        if u >= 1:
                            values(u - 1)
                    values(len(us) - 1)
                    barrier(pe, "pe")
                for i in range(8):
                    if i >= 3:
                        pe.wait_ge(ot_lo, l * 8 + i - 2)
                    c_in = (MLO, NAQ, DQ, GQ)[i // 2] + (i % 2) * P
                    for t in range(ntq(l)):
                        c_ = (i % 3) * 1024 + t * P
                        ins = tr(flat[:, c_:c_ + P], z[:, t, c_in:c_in + P], ident[:])
                    ins.then_inc(ot_ready, 1)
                barrier(pe, "pe")
                cb, fb = c0 + NZ, 2 + l * NSTEP
                pe.wait_ge(h_ready, h_base(l) + 2 * KT)
                with pe.Fori(0, KT) as m:
                    for bb in range(4):
                        p = bb % 2
                        if l == 0:
                            pe.wait_ge(ada_in[p], m * 32 + 16 * (bb // 2 + 1))
                            ada_product(ada_w[:, p, :], bass.ds(m * 8 + (2 * ADA0 + 2 * bb), 2)).then_inc(ada_used, 1)
                        pe.wait_ge(w_ready, m * 4 + (cb + bb + 1))
                        pe.wait_ge(bank_free, m * 4 + (fb + bb - 1))
                        chunk_products([ps[:, 3 * p, :], ps[:, 3 * p + 2, 0:C]], bb, range(8), act0, 0, sg)
                        chunk_products([ps[:, 3 * p + 1, :], ps[:, 3 * p + 2, C:2 * C]], bb, range(8, 10), act1, 2 * bb,
                                       sg).then_inc(w_used, 1)
                barrier(pe, "pe")
                cb, fb = cb + NP4, fb + NP4
                for j in range(NO):
                    p = j % 2
                    pe.wait_ge(w_ready, cb + j + 1)
                    pe.wait_ge(bank_free, fb + j - 1)

                    def y_rows(kt):
                        pe.wait_ge(y_ready, l * KT + kt + 1)

                    chunk_products([ps[:, 3 * p, :], ps[:, 3 * p + 2, :]], j % SLOTS, range(8), act0, 0, sg,
                                   y_rows if j == 0 else None).then_inc(w_used, 1)
                barrier(pe, "pe")
                norm(sg, True)
                cb, fb = cb + NO, fb + NO
                pe.wait_ge(h_ready, h_base(l) + 3 * KT)
                with pe.Fori(0, 4) as q:
                    for j in range(16):
                        p = j % 2
                        if l == 0 and j < 12:
                            pe.wait_ge(ada_in[p], q * 96 + 16 * (16 + j // 2 + 1))
                            ada_product(ada_w[:, p, :], bass.ds(q * 24 + (2 * ADAN + 2 * j), 2)).then_inc(ada_used, 1)
                        pe.wait_ge(w_ready, q * 16 + (cb + j + 1))
                        pe.wait_ge(bank_free, q * 16 + (fb + j - 1))

                        def a_rows(kt):
                            pe.wait_ge(a_ready, q * 8 + (l * 32 + kt + 1))

                        chunk_products([ps[:, 3 * p, :], ps[:, 3 * p + 2, :]], j % SLOTS, range(8),
                                       act1 if j < 8 else act0, 0, sg, a_rows if j == 8 else None).then_inc(w_used, 1)
                barrier(pe, "pe")


def kernel(x, c, ctx, c_ctx, w_ada, b_ada, g_norm1, g_norm2, w_in, g_mla_qa, w_mla_uq, g_mla_kva, w_mla_ukv,
           g_mla_q, g_mla_k, g_na_q, g_na_k, na_rpb, g_diff_q, g_diff_k, diff_lq1, diff_lk1, diff_lq2, diff_lk2,
           g_diff_sub, g_gqa_q, g_gqa_k, w_branch, w_out, w_up, w_down):
    import concourse.bacc as bacc
    from concourse.bass_utils import run_bass_kernel_spmd

    L = DEPTH
    perm = (np.arange(S) % GR) * GW + np.arange(S) // GR
    tokens = np.concatenate([np.asarray(x)[0][perm], np.asarray(ctx)[0]])
    feature = lambda v: np.moveaxis(np.asarray(v).reshape(*v.shape[:-1], -1, P), -1, 0)
    arrays = {"xT": np.ascontiguousarray(feature(tokens).transpose(0, 2, 1)),
              "cT": np.stack([feature(np.asarray(c)[0]), feature(np.asarray(c_ctx))], -1),
              "b_ada": feature(b_ada),
              "gn": np.stack([feature(g_norm1), feature(g_norm2)], 2),
              "ident": np.eye(P, dtype=np.float32)}

    def tiles(w, cols):
        l, k, n = w.shape
        return w.reshape(l, k // P, P, n // cols, cols).transpose(0, 3, 2, 1, 4).reshape(l, n // cols, P, -1)

    w_in = np.asarray(w_in)
    o = np.cumsum([0, QL, KVL, RD, 768, 768, 512]).tolist()
    na, df, gq = o[3], o[4], o[5]
    col = lambda b, n: np.arange(b, b + n)
    gq_cols = np.concatenate([col(gq + HD * h, HD) for h in GQA_ORDER])
    order = np.concatenate([col(o[1], KVL), col(o[2], RD), col(na + 256, 512), col(df + 256, 512), col(gq + 256, 256),
                            col(o[0], QL), col(na, 256), col(df, 256), gq_cols])
    wz = w_in[:, :, order].reshape(L, KT // 2, 2, P, 5, ZG).transpose(0, 4, 1, 3, 2, 5).reshape(L, NZ, P, 2 * ZG)
    gates = tiles(w_in[:, :, o[6]:], P).reshape(L, 4, KT, P, KT * P).transpose(0, 2, 1, 3, 4)
    wb = np.asarray(w_branch).reshape(L, 4, 2, P, KT, P).transpose(0, 4, 1, 3, 2, 5).reshape(L, KT, 4, P, 2 * P)
    up = tiles(np.asarray(w_up), P).reshape(L, 4, 8, P, KT * P)
    down = np.asarray(w_down).reshape(L, 4, KT, P, KT, P).transpose(0, 1, 4, 3, 2, 5).reshape(L, 4, 8, P, KT * P)
    arrays["w_ada"] = tiles(np.asarray(w_ada), P).reshape(L * ADAN, P, KT * P)
    arrays["wz"] = wz
    arrays["wp"] = np.concatenate([gates, wb], -1).reshape(L * NP4, P, WMAX)
    arrays["wo"] = tiles(np.asarray(w_out), P).reshape(L * NO, P, KT * P)
    arrays["wm"] = np.concatenate([up, down], 2).reshape(L * NM, P, KT * P)
    uq = np.zeros((L, 2 * P, 4 * QK), np.float32)
    uq[:, 0:QL] = w_mla_uq
    arrays["uq"] = uq.reshape(L, 2, P, 4 * QK).transpose(0, 2, 1, 3)
    arrays["ukv"] = np.asarray(w_mla_ukv).reshape(L, KVL, NH, 2, HD).transpose(0, 1, 3, 2, 4).reshape(L, KVL, 512)
    arrays["small"] = np.concatenate([np.asarray(v) for v in (
        g_mla_qa, g_mla_kva, g_mla_q, g_mla_k, g_na_q, g_na_k, g_diff_q, g_diff_k, g_diff_sub, g_gqa_q, g_gqa_k,
        diff_lq1, diff_lk1, diff_lq2, diff_lk2)], -1)

    tok = np.arange(S)
    rows, cols = (tok % GR).astype(np.float32), (tok // GR).astype(np.float32)
    tabs = []
    for rot in (HD, RD):
        n = rot // 4
        inv = np.power(np.float32(10000.0), -np.arange(n, dtype=np.float32) / np.float32(n)).astype(np.float32)
        ar, ac = rows[:, None] * inv, cols[:, None] * inv
        tabs += [np.cos(np.concatenate([ar, ar, ac, ac], -1)), np.sin(np.concatenate([-ar, ar, -ac, ac], -1))]
    arrays["rope"] = np.concatenate(tabs, -1).astype(np.float32).reshape(NTL, P, 192).transpose(1, 0, 2)

    qc, qr = np.arange(P) // GR, np.arange(P) % GR
    kc, kr = np.arange(384) // GR - 16, np.arange(384) % GR
    dc = kc[None] - qc[:, None] + 15
    dr = kr[None] - qr[:, None] + 7
    padded = np.pad(np.asarray(na_rpb), ((0, 0), (0, 0), (0, 0), (0, 1)))
    arrays["na_rows"] = padded[:, :, dr, np.where((dc >= 0) & (dc <= 30), dc, 31)]
    mask = []
    for kind, t in ((0, 0), (1, 1), (2, 3)):
        q_col = 16 * t + qc
        start = np.clip(q_col - 8, 0, GW - 16)[:, None]
        k_col = (16 * t + kc)[NA_SRC[kind]:NA_SRC[kind] + NA_TAB[kind][1]][None]
        mask.append(np.where((k_col >= start) & (k_col < start + 16), 0.0, NEG))
    arrays["na_mask"] = np.concatenate(mask, -1).astype(np.float32)

    nc = bacc.Bacc("TRN2", target_bir_lowering=False, num_devices=1, dynamic_dma_scratch_size=1024)
    arrays = {k: np.ascontiguousarray(v) for k, v in arrays.items()}
    aps = {k: nc.dram_tensor("in_" + k, v.shape, mybir.dt.from_np(v.dtype), kind="ExternalInput").ap() for k, v in arrays.items()}
    out = nc.dram_tensor("out", (P, KT, S), mybir.dt.float32, kind="ExternalOutput").ap()
    program(nc, aps, out)
    ins = {"in_" + k: v for k, v in arrays.items()}
    got = np.asarray(run_bass_kernel_spmd(nc, [ins], core_ids=[0]).results[0]["out"])
    y = np.empty((1, S, D), np.float32)
    y[0, perm] = got.transpose(2, 1, 0).reshape(S, D)
    return y
```

```python
import math
from contextlib import ExitStack

import numpy as np
import concourse.bass as bass
from concourse import mybir

D, DEPTH, S, C = 1024, 2, 512, 256
T = S + C
P = 128
KT = D // P
GW, GR = 64, S // 64
HD, NH = 64, 4
QL, KVL, RD, NOPE, QK = 192, 128, 32, 64, 96
DD = 32
EPS = 1e-6
NEG = -1.0e30
GQA_ORDER = (0, 2, 1, 3)
NT, NTL = T // P, S // P
ZG = 480
NKVG, NQG = 3, 2
ZC = ZG * (NKVG + NQG)
CQ, NAQ, DQ, GQ, CKV, KR, NAK, NAV, DK, DV, GK, GV = np.cumsum(
    [0, 192, 256, 256, 256, 128, 32, 256, 256, 256, 256, 128]).tolist()
MLO = NAK
NZ, NP4, NO, NM = 20, 32, 8, 64
NCH = NZ + NP4 + NO + NM
SLOTS = 4
WMAX = 10 * P
ADA0 = 16
ADAN = 48
names = [("qa", 192), ("kva", 128), ("mq", 96), ("mk", 96), ("nq", 64), ("nk", 64), ("dq", 32),
         ("dk", 32), ("sub", 64), ("gq", 64), ("gk", 64), ("lq1", 32), ("lk1", 32), ("lq2", 32), ("lk2", 32)]
GO, _o = {}, 0
for _n, _w in names:
    GO[_n] = (_o, _w)
    _o += _w
SM = _o


def na_tiles(i):
    return list(range(max(i - 1, 0), min(i + 2, NTL)))


NA_KIND = [0, 1, 1, 2]
NA_TAB = [(0, 256), (256, 384), (640, 256)]
NA_SRC = [128, 0, 0]


def program(nc, a, out):
    f32, f32r = mybir.dt.float32, mybir.dt.float32r
    ALU, ACT, AX = mybir.AluOpType, mybir.ActivationFunctionType, mybir.AxisListType
    ctx = ExitStack()
    with ctx:
        sem = lambda name: ctx.enter_context(nc.semaphore(name))
        persistent = lambda name, shape, dt=f32: ctx.enter_context(nc.sbuf_tensor(name, shape, dt))

        x_sb = persistent("x_sb", [P, KT, T])
        w_hi = persistent("w_hi", [P, SLOTS, WMAX], f32r)
        w_lo = persistent("w_lo", [P, SLOTS, WMAX], f32r)
        w_raw = persistent("w_raw", [P, 2, WMAX])
        ada_w = persistent("ada_w", [P, 2, KT * P])
        ada_acc = persistent("ada_acc", [P, 2, 2 * P])
        rstd = persistent("rstd", [P, T])
        ident = persistent("ident", [P, P])
        ones = persistent("ones", [P, P])
        eps_sb = persistent("eps_sb", [P, 1])
        c_sb = persistent("c_sb", [P, KT, 2])
        csig = persistent("csig", [P, KT, 2])
        csilu = persistent("csilu", [P, KT, 2])
        b_sb = persistent("b_sb", [P, DEPTH, ADAN])
        gn_sb = persistent("gn_sb", [P, DEPTH, 2, KT])
        mod = persistent("mod", [P, DEPTH, ADAN, 2])
        nscale = persistent("nscale", [P, DEPTH, 2, KT, 2])
        neglam = persistent("neglam", [P, 1])
        lam_t = persistent("lam_t", [P, 4])
        lam_p = persistent("lam_p", [P, 2, DD])
        ss_m = persistent("ss_m", [P, 48])
        row_mask = persistent("row_mask", [P, 6])
        nmax = persistent("nmax", [P, 8, 2, 2])
        rsum = persistent("rsum", [P, 8, 2, 2])
        rinv = persistent("rinv", [P, 8, 2])

        KB = 1024
        Z_END = NT * ZC * 4
        F1 = Z_END
        Y0 = F1 + 2 * KT * T * 4
        A0 = (nc.sbuf_usable_end - (Y0 + 25 * KB)) // 64 * 64
        assert nc.sbuf_base <= A0
        at = lambda name, off, shape, dt=f32: nc.alloc_sbuf_tensor_at(name, shape, dt, offset=A0 + off)
        z = at("z", 0, [P, NT, ZC])
        act0 = at("act0", 0, [P, 2, KT, T], f32r)
        act1 = at("act1", F1, [P, 2, KT, T], f32r)
        ada_init = at("ada_init", 0, [P, ADA0, KT * P])
        ada_acc0 = at("ada_acc0", Y0, [P, 2, KT * P])
        sig = at("sig", 48 * KB, [P, 2, T])
        y_sb = at("y_sb", Y0, [P, KT, T])
        n_a = at("n_a", Y0, [P, 2, T])
        n_b = at("n_b", Y0 + 6 * KB, [P, 2, T])
        r_sb = at("r_sb", Y0, [P, 2, T])
        q_sb = at("q_sb", Y0 + 6 * KB, [P, 2, T])
        tmp_z = [at("tmp_z0", Y0, [P, NT, 256]), at("tmp_z1", Y0 + 6 * KB, [P, NT, 256])]
        ss_z = at("ss_z", Y0 + 12 * KB, [P, 256])
        ukv_sb = at("ukv_sb", Y0 + 13 * KB, [P, 512])
        uq_sb = at("uq_sb", Y0 + 15 * KB, [P, 2, 384])
        rope_sb = at("rope_sb", Y0 + 18 * KB, [P, NTL, 192])
        small = at("small", Y0 + 21 * KB, [P, SM])
        A_ = F1
        mtmp = at("mtmp", A_, [P, NT, 384])
        cT = at("cT", A_ + 9 * KB, [P, 3, T])
        mlaq = at("mlaq", A_ + 24 * KB, [P, NT, 384])
        mlak = at("mlak", A_ + 33 * KB, [P, NT, 384])
        mlav = at("mlav", A_ + 42 * KB, [P, NT, 256])
        dtmp = at("dtmp", A_ + 6 * KB, [P, NT, 256])
        QT = at("QT", A_, [P, 2, T])
        KTr = at("KTr", A_ + 6 * KB, [P, 4, T])
        QTm = at("QTm", A_, [P, 4, T])
        KTm = at("KTm", A_ + 12 * KB, [P, 4, T])
        na_T = at("na_T", A_ + 18 * KB, [P, NH, 384])
        na_tab = persistent("na_tab", [P, 896])
        na_mask = at("na_mask", Y0 + 13 * KB, [P, 896])
        Pp = [at("Pp0", Y0, [P, T]), at("Pp1", Y0 + 3 * KB, [P, T])]
        Pq = [at("Pq0", A_ + 18 * KB, [P, T]), at("Pq1", A_ + 21 * KB, [P, T])]
        PTs = at("PTs", Y0 + 6 * KB, [P, 2, T])

        ps = ctx.enter_context(nc.psum_tensor("ps", [P, 8, 512], f32))
        flat = ps[:, :, :].rearrange("p b c -> p (b c)")
        ada_ps = ps[:, 7, :]

        const_in = sem("const_in")
        late_in = sem("late_in")
        na_in = sem("na_in")
        w_in = [sem("w_in0"), sem("w_in1")]
        w_rounded = sem("w_rounded")
        w_ready = sem("w_ready")
        w_used = sem("w_used")
        x_in = sem("x_in")
        ada_first = [sem(f"ada_first{j}") for j in range(4)]
        ada_step = sem("ada_step")
        ada_summed = sem("ada_summed")
        ada_in = [sem("ada_in0"), sem("ada_in1")]
        ada_used = sem("ada_used")
        pe_phase, act_phase, dve_phase = sem("pe_phase"), sem("act_phase"), sem("dve_phase")
        act_step, dve_step = sem("act_step"), sem("dve_step")
        sq_ready, ssq_done = sem("sq_ready"), sem("ssq_done")
        std_ready, normed, modded, h_ready = sem("std_ready"), sem("normed"), sem("modded"), sem("h_ready")
        z_prod, z_copied = sem("z_prod"), sem("z_copied")
        ss_ready, rt_ready = sem("ss_ready"), sem("rt_ready")
        piece_t, piece_c = sem("piece_t"), sem("piece_c")
        up_done, up_copied = sem("up_done"), sem("up_copied")
        s_ready, max_ready, exp_done = sem("s_ready"), sem("max_ready"), sem("exp_done")
        diff_done = sem("diff_done")
        pt_ready, pt_copied = sem("pt_ready"), sem("pt_copied")
        o_ready, o_done = sem("o_ready"), sem("o_done")
        ot_ready, ot_hi, ot_lo = sem("ot_ready"), sem("ot_hi"), sem("ot_lo")
        bank_free = sem("bank_free")
        sig_ready = sem("sig_ready")
        y_hi, y_ready = sem("y_hi"), sem("y_ready")
        a_hi, a_ready = sem("a_hi"), sem("a_ready")
        c_sig, c_ready, lam_e = sem("c_sig"), sem("c_ready"), sem("lam_e")
        ss_ready_d, rt_d = sem("ss_ready_d"), sem("rt_d")
        relu_ready, gated = sem("relu_ready"), sem("gated")
        mla_rt, mla_prepared, lam_s, pool_step = sem("mla_rt"), sem("mla_prepared"), sem("lam_s"), sem("pool_step")
        out_done = sem("out_done")

        block = ctx.enter_context(nc.Block())

        segs = lambda l: [(0, S), (S, C)] if l == 0 else [(0, S)]
        both = [(0, S), (S, C)]
        ntq = lambda l: NT if l == 0 else NTL
        zt = lambda l, g: NT if g >= NQG else ntq(l)
        zbase = lambda l, g: sum(zt(k, j) for k in range(l) for j in range(5)) + sum(zt(l, j) for j in range(g))
        PREP = [("cq", CQ, 1, 192, "qa", True, 0, 0), ("naq", NAQ, 4, 64, "nq", True, 0, 0),
                ("dq", DQ, 8, 32, "dq", True, 32, 0), ("gq", GQ, 4, 64, "gq", True, 64, 0),
                ("ckv", CKV, 1, 128, "kva", False, 0, 1), ("nak", NAK, 4, 64, "nk", False, 0, 1),
                ("dk", DK, 8, 32, "dk", False, 32, 1), ("gk", GK, 2, 64, "gk", False, 64, 2)]
        NB = 3
        ready_group = [1, 3, 4]
        ss_off, off = {}, 0
        batch_span = []
        for k in range(NB):
            b0 = off
            for p in PREP:
                if p[7] == k:
                    ss_off[p[0]] = off
                    off += NT * p[2]
            batch_span.append((b0, off))
        assert off <= 256

        BR = ("na", "diff0", "diff1", "gqa", "mla")
        HEADS = {"na": range(NH), "diff0": (0, 1), "diff1": (2, 3), "gqa": range(NH), "mla": range(NH)}
        PIECES = {"na": 4, "diff0": 2, "diff1": 2, "gqa": 3, "mla": 8}
        is_diff = lambda b: b.startswith("diff")
        units = {l: {b: [(h, t) for h in HEADS[b] for t in range(ntq(l))] for b in BR} for l in range(DEPTH)}
        nmaps = {b: 2 if is_diff(b) else 1 for b in BR}
        diff_base = lambda l, b: sum(len(units[k]["diff0"]) * 2 for k in range(l)) + (len(units[l]["diff0"]) if b == "diff1" else 0)

        def unit_base(l, b):
            u = m = 0
            for k in range(DEPTH):
                for c in BR:
                    if (k, c) == (l, b):
                        return u, m
                    u += len(units[k][c])
                    m += len(units[k][c]) * nmaps[c]

        def piece_base(l, b):
            per = 3 + sum(PIECES.values())
            return l * per + (0 if b == "up" else 3 + sum(PIECES[c] for c in BR[:BR.index(b)]))

        def key_tiles(b, t):
            if t >= NTL:
                return list(range(NTL, NT))
            return (na_tiles(t) if b == "na" else list(range(NTL))) + list(range(NTL, NT))

        def branch_view(b):
            return {"na": ((z, NAQ), (z, NAK), (z, NAV)), "diff0": ((z, DQ), (z, DK), (z, DV)),
                    "diff1": ((z, DQ + 128), (z, DK + 128), (z, DV)),
                    "gqa": ((z, GQ), (z, GK), (z, GV)), "mla": ((mlaq, 0), (mlak, 0), (mlav, 0))}[b]

        def pieces(l, b):
            (qs, q0), (ks, k0), _ = branch_view(b)
            if b == "mla":
                return ([(qs, q0 + 96 * h, 96, ntq(l), [(QTm[0:96, h, :], None)]) for h in range(4)]
                        + [(ks, k0 + 96 * h, 96, NT, [(KTm[0:96, h, :], None)]) for h in range(4)])
            nq = 1 if is_diff(b) else 2
            nk = 2 if b == "na" else 1
            per, m0 = (4, 2) if is_diff(b) else (2, 0)
            return ([(qs, q0 + 128 * j, 128, ntq(l), [(QT[:, j, :], None)]) for j in range(nq)]
                    + [(ks, k0 + 128 * j, 128, NT, [(KTr[:, per * j + i, :], row_mask[:, m0 + i:m0 + i + 1])
                                                    for i in range(per)]) for j in range(nk)])

        def o_dest(b, h, t):
            if b == "gqa":
                h = GQA_ORDER[h]
            c0 = {"na": NAQ, "diff0": DQ, "diff1": DQ, "gqa": GQ, "mla": MLO}[b] + 64 * h
            return z[:, t, c0:c0 + 64]

        def qk_operands(b, h, mp, t):
            q = slice(t * P, t * P + P)
            if b == "mla":
                return QTm[0:96, h, q], KTm[0:96, h, :]
            if is_diff(b):
                return QT[:, 0, q], KTr[:, (h % 2) * 2 + mp, :]
            if b == "na":
                return QT[:, h // 2, q], KTr[:, h, :]
            return QT[:, h // 2, q], KTr[:, h % 2, :]

        def v_slice(b, h, kt):
            (vs, v0) = branch_view(b)[2]
            hv = h % 2 if b == "gqa" else h
            return vs[:, kt, v0 + 64 * hv:v0 + 64 * hv + 64]

        S_BANK = [0, 2]
        PT_BANK, O_BANK = 4, 6

        NSTEP = NP4 + NO + NM
        up_list = lambda l: [("q", t) for t in range(ntq(l))] + [("kv", t) for t in range(NT)]
        up_base = lambda l: sum(len(up_list(k)) for k in range(l))
        h_base = lambda l: l * 3 * KT
        std_seen = lambda l: 2 + 4 * l
        ADA_STEPS = (2, 4, 6, 10, 12, 14)
        LAST_PHASE = 1 + (4 + 2 * len(BR) + 2) * DEPTH

        phase = {"pe": 0, "act": 0, "dve": 0}
        norm_no, norm_f = {"act": 0, "dve": 0}, {"act": 0, "dve": 0, "pe": 0}
        PH = {"pe": pe_phase, "act": act_phase, "dve": dve_phase}

        def barrier(eng, me):
            eng.drain().then_inc(PH[me], 1)
            phase[me] += 1
            for other in PH:
                if other != me:
                    eng.wait_ge(PH[other], phase[me])

        CH0 = lambda l: l * NCH

        def scale_rows(e, link, src, c0, heads, d, nt, ss, g):
            v = src[:, 0:nt, c0:c0 + heads * d].rearrange("p t (h d) -> p t h d", d=d)
            link(e.tensor_tensor(v, v, ss.unsqueeze(3).to_broadcast([P, nt, heads, d]), ALU.mult))
            o, w = GO[g]
            gb = small[:, o:o + w].unsqueeze(1).unsqueeze(1).to_broadcast([P, nt, heads, d])
            link(e.tensor_tensor(v, v, gb, ALU.mult))

        def rope(e, link, src, c0, heads, stride, d, tab, tmp):
            n, s0 = d // 4, c0 - (stride - d)
            v = src[:, 0:NTL, s0:s0 + heads * stride].rearrange("p t (h s) -> p t h s", s=stride)[:, :, :, stride - d:stride]
            w = tmp.rearrange("p t (h d) -> p t h d", d=d)
            for q in range(4):
                o = q ^ 1
                sin = rope_sb[:, :, tab + d + q * n:tab + d + (q + 1) * n].unsqueeze(2).to_broadcast([P, NTL, heads, n])
                ins = e.tensor_tensor(w[:, :, :, q * n:(q + 1) * n], v[:, :, :, o * n:(o + 1) * n], sin, ALU.mult)
            link(ins)
            cos = rope_sb[:, :, tab:tab + d].unsqueeze(2).to_broadcast([P, NTL, heads, d])
            link(e.tensor_tensor(v, v, cos, ALU.mult))
            link(e.tensor_tensor(v, v, w, ALU.add))

        @block.sync
        def _(sp):
            for dst, src in ((c_sb, a["cT"]), (b_sb, a["b_ada"]), (gn_sb, a["gn"]), (ident, a["ident"])):
                sp.dma_start(dst[:], src).then_inc(const_in, 16)
            for j in (0, 2, 1, 3):
                n = ADA0 // 4
                sp.dma_start(ada_init[:, j * n:(j + 1) * n, :],
                             a["w_ada"][j * n:(j + 1) * n].rearrange("j p n -> p j n")).then_inc(ada_first[j], 16)
            sp.dma_start(x_sb[:], a["xT"]).then_inc(x_in, 16)

            def load(c, src, width, k):
                if not isinstance(c, int) or c >= 2:
                    sp.wait_ge(w_ready, c - 1)
                sp.dma_start(w_raw[:, k, 0:width], src).then_inc(w_in[k], 16)

            for l in range(DEPTH):
                c0 = CH0(l)
                for j in range(NZ):
                    load(c0 + j, a["wz"][l, j], 2 * ZG, j % 2)
                c0 += NZ
                with sp.Fori(0, KT) as m:
                    for b in range(4):
                        load(m * 4 + (c0 + b), a["wp"][l * NP4 + 4 * m + b], WMAX, b % 2)
                c0 += NP4
                for j in range(NO):
                    load(c0 + j, a["wo"][l * NO + j], KT * P, j % 2)
                c0 += NO
                with sp.Fori(0, 4) as q:
                    for j in range(16):
                        load(q * 16 + (c0 + j), a["wm"][l * NM + 16 * q + j], KT * P, j % 2)
            sp.wait_ge(dve_phase, LAST_PHASE)
            sp.dma_start(out, x_sb[:, :, 0:S]).then_inc(out_done, 16)
            sp.wait_ge(out_done, 16)

        @block.gpsimd
        def _(pool):
            chain = [0]

            def link(ins):
                chain[0] += 1
                ins.then_inc(pool_step, 1)
                pool.wait_ge(pool_step, chain[0])

            def low(c, width, k):
                pool.wait_ge(w_rounded, c + 1)
                nc.gpsimd.tensor_tensor(w_lo[:, k, 0:width], w_raw[:, k % 2, 0:width],
                                        w_hi[:, k, 0:width].bitcast(f32), ALU.subtract).then_inc(w_ready, 1)

            for l in range(DEPTH):
                c0 = CH0(l)
                for j in range(NZ):
                    low(c0 + j, 2 * ZG, j % SLOTS)
                for b in range(4):
                    low(c0 + NZ + b, WMAX, b)
                pool.wait_ge(mla_rt, l + 1)
                nq = ntq(l)
                rot = z[:, 0:NTL, CKV:CKV + P]
                for src, ss, nt, g in ((mlaq, ss_m[:, 0:4 * nq], nq, "mq"), (mlak, ss_m[:, 24:48], NT, "mk")):
                    scale_rows(nc.gpsimd, link, src, 0, NH, QK, nt, ss.rearrange("p (t h) -> p t h", h=NH), g)
                    rope(nc.gpsimd, link, src, NOPE, NH, QK, RD, 128, rot)
                pool.drain().then_inc(mla_prepared, 1)
                c0 += NZ
                with pool.Fori(1, KT) as m:
                    for b in range(4):
                        low(m * 4 + (c0 + b), WMAX, b)
                c0 += NP4
                for j in range(NO):
                    low(c0 + j, KT * P, j % SLOTS)
                c0 += NO
                with pool.Fori(0, 4) as q:
                    for j in range(16):
                        low(q * 16 + (c0 + j), KT * P, j % SLOTS)

        def residual(l, part, m, sg, p):
            for i, (t0, tn) in enumerate(sg):
                ins = nc.vector.scalar_tensor_tensor(
                    x_sb[:, m, t0:t0 + tn], ps[:, 3 * p + 2 * i, 0:tn], mod[:, l, part * KT + m, i:i + 1],
                    x_sb[:, m, t0:t0 + tn], ALU.mult, ALU.add)
            ins.then_inc(bank_free, 1)

        @block.scalar
        def _(act):
            chain = [0]

            def link(ins):
                chain[0] += 1
                ins.then_inc(act_step, 1)
                act.wait_ge(act_step, chain[0])

            def high(c, width, k, first=False):
                act.wait_ge(w_in[k % 2], (c // 2) * 16 + 16 if isinstance(c, int) else c * 8 + (16 - 8 * (k % 2)))
                if not first:
                    act.wait_ge(w_used, c - 3)
                nc.scalar.activation(w_hi[:, k, 0:width], w_raw[:, k % 2, 0:width], ACT.Copy).then_inc(w_rounded, 1)

            def norm(l, which, dst, sg, fresh):
                n = norm_no["act"]
                if fresh:
                    for kt in range(KT):
                        if kt >= 2:
                            act.wait_ge(ssq_done, norm_f["act"] * KT + kt - 1)
                        nc.scalar.activation(n_a[:, kt % 2, 0:sg[-1][0] + sg[-1][1]],
                                             x_sb[:, kt, 0:sg[-1][0] + sg[-1][1]],
                                             ACT.Square).then_inc(sq_ready, 1)
                    norm_f["act"] += 1
                    act.wait_ge(ssq_done, norm_f["act"] * KT)
                    for i, (t0, tn) in enumerate(sg):
                        nc.scalar.activation(rstd[:, t0:t0 + tn], ps[:, i, 0:tn], ACT.Sqrt, bias=eps_sb[:, 0:1],
                                             scale=1.0 / D).then_inc(std_ready, 1)
                for kt in range(KT):
                    act.wait_ge(normed, n * KT + kt + 1)
                    if kt >= 2:
                        act.wait_ge(h_ready, n * KT + kt - 1)
                    for v, (t0, tn) in enumerate(sg):
                        ins = nc.scalar.activation(n_a[:, kt % 2, t0:t0 + tn], n_b[:, kt % 2, t0:t0 + tn], ACT.Identity,
                                                   bias=mod[:, l, (3 * which) * KT + kt, v:v + 1],
                                                   scale=nscale[:, l, which, kt, v:v + 1])
                        if v < len(sg) - 1:
                            continue
                        link(ins)
                    tt = sg[-1][0] + sg[-1][1]
                    nc.scalar.activation(dst[:, 0, kt, 0:tt], n_a[:, kt % 2, 0:tt], ACT.Copy).then_inc(modded, 1)
                norm_no["act"] += 1

            
            act.wait_ge(const_in, 16 * 4)
            nc.scalar.activation(csig[:], c_sb[:], ACT.Sigmoid).then_inc(c_sig, 1)
            for c in range(SLOTS):
                high(c, 2 * ZG, c, first=True)
            act.wait_ge(x_in, 16)
            barrier(act, "act")

            for l in range(DEPTH):
                sg, c0 = segs(l), CH0(l)
                for dst, src in ((small, a["small"][l:l + 1, :].to_broadcast([P, SM])), (rope_sb, a["rope"]),
                                 (uq_sb, a["uq"][l]), (ukv_sb, a["ukv"][l])):
                    act.dma_start(dst[:], src).then_inc(late_in, 16)
                norm(l, 0, act1, both, True)
                def roots(k):
                    act.wait_ge(ss_ready, l * (NB + 1) + k + 1)
                    for p in (p for p in PREP if p[7] == k):
                        s0 = ss_off[p[0]]
                        s1 = s0 + (ntq(l) if p[5] else NT) * p[2]
                        ins = nc.scalar.activation(ss_z[:, s0:s1], ss_z[:, s0:s1], ACT.Sqrt)
                    ins.then_inc(rt_ready, 1)

                for g in range(5):
                    n = zt(l, g)
                    for tt in range(n):
                        if tt == 3 and g in (2, 4):
                            roots(g // 2 - 1)
                        if tt == n - 2:
                            for i in range(4):
                                cc = 4 * g + 4 + i
                                high(c0 + cc, 2 * ZG if cc < NZ else WMAX, cc % SLOTS)
                        k = zbase(l, g) + tt
                        act.wait_ge(z_prod, k + 1)
                        nc.scalar.activation(z[:, tt, g * ZG:(g + 1) * ZG], ps[:, k % 4, 0:ZG],
                                             ACT.Copy).then_inc(z_copied, 1)
                roots(2)
                act.wait_ge(lam_s, l + 1)
                nc.scalar.activation(lam_t[:, 2:4], lam_t[:, 0:2], ACT.Exp).then_inc(lam_e, 1)
                barrier(act, "act")
                barrier(act, "act")
                act.wait_ge(ss_ready, l * (NB + 1) + NB + 1)
                for s0, s1 in ((0, 4 * ntq(l)), (24, 48)):
                    ins = nc.scalar.activation(ss_m[:, s0:s1], ss_m[:, s0:s1], ACT.Sqrt)
                ins.then_inc(rt_ready, 1)
                act.wait_ge(mla_rt, l + 1)
                act.dma_start(na_T[:], a["na_rows"][l].rearrange("h p n -> p h n")).then_inc(na_in, 16)
                act.dma_start(na_mask[:], a["na_mask"]).then_inc(na_in, 16)
                for b in BR:
                    barrier(act, "act")
                    ub, mb = unit_base(l, b)
                    us = units[l][b]

                    def exps(u):
                        h, t = us[u]
                        kts = key_tiles(b, t)
                        if u >= 2:
                            act.wait_ge(pt_ready, ub + u - 1)
                        for mp in range(nmaps[b]):
                            m = u * nmaps[b] + mp
                            act.wait_ge(max_ready, mb + m + 1)
                            dst = (Pq if mp else Pp)[u % 2]
                            s = flat[:, S_BANK[m % 2] * 512:S_BANK[m % 2] * 512 + T]
                            e = (ub + u) % 8
                            W = P * len(kts)
                            if b == "na" and t < NTL:
                                L = W - C
                                nc.scalar.activation(dst[:, 0:L], dst[:, 0:L], ACT.Exp, bias=nmax[:, e, 0, 0:1],
                                                     accum_out=rsum[:, e, 0, 0:1])
                                nc.scalar.activation(dst[:, L:W], s[:, 512:512 + C], ACT.Exp, bias=nmax[:, e, 0, 0:1],
                                                     accum_out=rsum[:, e, 0, 1:2]).then_inc(exp_done, 1)
                            else:
                                nc.scalar.activation(dst[:, 0:W], s[:, 0:W], ACT.Exp, bias=nmax[:, e, mp, 0:1],
                                                     accum_out=rsum[:, e, mp, 0:1]).then_inc(exp_done, 1)

                    def pt_copy(u):
                        W = P * len(key_tiles(b, us[u][1]))
                        act.wait_ge(pt_ready, ub + u + 1)
                        if u >= 2:
                            act.wait_ge(o_ready, ub + u - 1)
                        nc.scalar.activation(PTs[:, u % 2, 0:W], flat[:, PT_BANK * 512:PT_BANK * 512 + W],
                                             ACT.Copy).then_inc(pt_copied, 1)

                    exps(0)
                    for u in range(len(us)):
                        if u + 1 < len(us):
                            exps(u + 1)
                        pt_copy(u)
                    if b == "diff1":
                        act.wait_ge(ss_ready_d, l + 1)
                        nc.scalar.activation(ss_z[:, 0:4 * ntq(l)], ss_z[:, 0:4 * ntq(l)], ACT.Sqrt).then_inc(rt_d, 1)
                    barrier(act, "act")
                for i in range(8):
                    act.wait_ge(ot_ready, l * 8 + i + 1)
                    tn = ntq(l) * P
                    src = flat[:, (i % 3) * 1024:(i % 3) * 1024 + tn]
                    nc.scalar.activation(act1[:, 0, i, 0:tn], src, ACT.Copy).then_inc(ot_hi, 1)
                barrier(act, "act")
                norm(l, 0, act0, sg, False)
                s0b, cb = l * NSTEP, c0 + NZ
                ada_on = l == 0
                if ada_on:
                    for n in range(2):
                        act.dma_start(ada_w[:, n, :], a["w_ada"][ADA0 + n]).then_inc(ada_in[n], 16)
                with act.Fori(0, KT) as m:
                    for bb in range(4):
                        act.wait_ge(w_used, m * 4 + (cb + bb + 1))
                        p = bb % 2
                        for i, (t0, tn) in enumerate(sg):
                            ins = nc.scalar.activation(sig[:, p, t0:t0 + tn],
                                                       ps[:, 3 * p, 0:tn] if i == 0 else ps[:, 3 * p + 2, 0:tn], ACT.Sigmoid)
                        ins.then_inc(sig_ready, 1)
                        high(m * 4 + (cb + bb + 4), WMAX, bb)
                        if ada_on and bb % 2 == 1:
                            act.wait_ge(ada_summed, m * 2 + (2 + bb // 2 + 1))
                            for i in range(2):
                                act.dma_start(ada_w[:, i, :], a["w_ada"][m * 4 + (ADA0 + bb + 1 + i)]).then_inc(ada_in[i], 16)
                barrier(act, "act")
                tt = sg[-1][0] + sg[-1][1]
                for kt in range(KT):
                    nc.scalar.activation(act0[:, 0, kt, 0:tt], y_sb[:, kt, 0:tt], ACT.Copy).then_inc(y_hi, 1)
                cb += NP4
                for j in range(NO):
                    high(cb + j + 4, KT * P, j % SLOTS)
                barrier(act, "act")
                norm(l, 1, act1, sg, True)
                cb += NO

                def quarter(q, last):
                    for j in range(16):
                        c = q * 16 + (cb + j)
                        act.wait_ge(w_used, c + 1)
                        if j < 8:
                            p = j % 2
                            for i, (t0, tn) in enumerate(sg):
                                ins = nc.scalar.activation(r_sb[:, p, t0:t0 + tn],
                                                           ps[:, 3 * p + 2 * i, 0:tn], ACT.Relu)
                            ins.then_inc(relu_ready, 1)
                            act.wait_ge(relu_ready, q * 8 + (l * 32 + j + 1))
                            nc.scalar.activation(act0[:, 0, j, 0:tt], r_sb[:, p, 0:tt], ACT.Square).then_inc(a_hi, 1)
                        if not last:
                            high(c + 4, KT * P, j % SLOTS)
                        elif j < 12:
                            high(c + 4, KT * P, j % SLOTS)
                        elif l + 1 < DEPTH:
                            high(c + 4, 2 * ZG, j % SLOTS)
                        if ada_on and j in ADA_STEPS and not (last and j == ADA_STEPS[-1]):
                            n = ADA_STEPS.index(j)
                            act.wait_ge(ada_summed, q * 6 + (2 + NP4 // 2 + n + 1))
                            for i in range(2):
                                act.dma_start(ada_w[:, i, :], a["w_ada"][q * 12 + (ADAN + 2 * n + 2 + i)]).then_inc(ada_in[i], 16)

                with act.Fori(0, 3) as q:
                    quarter(q, False)
                quarter(3, True)
                barrier(act, "act")

        @block.vector
        def _(dve):
            chain = [0]

            def link(ins):
                chain[0] += 1
                ins.then_inc(dve_step, 1)
                dve.wait_ge(dve_step, chain[0])

            tt_op = nc.vector.tensor_tensor

            def row_products(w, acc, n, count):
                for kt in range(KT):
                    for v in range(2):
                        o = acc[:, v, :].rearrange("p (n c) -> p n c", c=P)
                        wk = w[:, 0:n, kt * P:(kt + 1) * P]
                        if kt == 0:
                            ins = nc.vector.tensor_scalar(o, wk, csilu[:, kt, v:v + 1], None, ALU.mult)
                        else:
                            dve.wait_ge(ada_step, count + (2 * kt + v - 1))
                            ins = nc.vector.scalar_tensor_tensor(o, wk, csilu[:, kt, v:v + 1], o, ALU.mult, ALU.add)
                        ins.then_inc(ada_summed if (kt, v) == (KT - 1, 1) else ada_step, 1)

            def take_mod(l, j0, j1):
                src = ada_ps[:, l * 2 * ADAN + 2 * j0:l * 2 * ADAN + 2 * j1].rearrange("p (j v) -> p j v", v=2)
                link(tt_op(mod[:, l, j0:j1, :], src, b_sb[:, l, j0:j1].unsqueeze(2).to_broadcast([P, j1 - j0, 2]), ALU.add))

            def take_scale(l, which):
                j0 = (3 * which + 1) * KT
                link(nc.vector.tensor_scalar(nscale[:, l, which, :, :], mod[:, l, j0:j0 + KT, :], 1.0, None, ALU.add))
                link(tt_op(nscale[:, l, which, :, :], nscale[:, l, which, :, :],
                           gn_sb[:, l, which, :].unsqueeze(2).to_broadcast([P, KT, 2]), ALU.mult))

            def norm(l, which, dst, sg, fresh):
                n = norm_no["dve"]
                tt = sg[-1][0] + sg[-1][1]
                if fresh:
                    norm_f["dve"] += len(sg)
                    dve.wait_ge(std_ready, norm_f["dve"])
                    link(nc.vector.reciprocal(rstd[:, 0:tt], rstd[:, 0:tt]))

                def times(kt):
                    if kt >= 2:
                        dve.wait_ge(modded, n * KT + kt - 1)
                    tt_op(n_b[:, kt % 2, 0:tt], x_sb[:, kt, 0:tt], rstd[:, 0:tt], ALU.mult).then_inc(normed, 1)

                times(0)
                for kt in range(KT):
                    if kt + 1 < KT:
                        times(kt + 1)
                    dve.wait_ge(modded, n * KT + kt + 1)
                    tt_op(dst[:, 1, kt, 0:tt], n_a[:, kt % 2, 0:tt], dst[:, 0, kt, 0:tt].bitcast(f32),
                          ALU.subtract).then_inc(h_ready, 1)
                norm_no["dve"] += 1

            def sums(src, c0, heads, d, nt, tmp, ss):
                v = src[:, 0:nt, c0:c0 + heads * d]
                w = tmp[:, 0:nt, 0:heads * d]
                link(tt_op(w, v, v, ALU.mult))
                link(nc.vector.tensor_reduce(ss, w.rearrange("p t (h d) -> p t h d", d=d), AX.X, ALU.add))
                return nc.vector.tensor_scalar(ss, ss, 1.0 / d, EPS, ALU.mult, ALU.add)

            def inverse(ss, mul):
                link(nc.vector.reciprocal(ss, ss))
                if mul != 1.0:
                    link(nc.vector.tensor_scalar(ss, ss, mul, None, ALU.mult))

            nc.vector.memset(ones[:], 1.0)
            link(nc.vector.memset(row_mask[:], 0.0))
            for i in range(2):
                nc.vector.memset(row_mask[64 * i:64 * i + 64, i:i + 1], 1.0)
            for i in range(4):
                nc.vector.memset(row_mask[32 * i:32 * i + 32, 2 + i:3 + i], 1.0)
            ins = nc.vector.memset(eps_sb[:], EPS)
            link(ins)
            
            dve.drain().then_inc(bank_free, 2)
            dve.wait_ge(c_sig, 1)
            dve.wait_ge(const_in, 16 * 4)
            tt_op(csilu[:], c_sb[:], csig[:], ALU.mult).then_inc(c_ready, 1)
            dve.wait_ge(c_ready, 1)
            for j in range(2):
                dve.wait_ge(ada_first[2 + j], 16)
                row_products(ada_init[:, 8 + 4 * j:12 + 4 * j, :], ada_acc0[:, :, j * 512:(j + 1) * 512], 4, 15 * j)
            dve.wait_ge(pe_phase, 1)
            take_mod(0, 0, ADA0)
            take_scale(0, 0)
            barrier(dve, "dve")

            for l in range(DEPTH):
                sg, c0 = segs(l), CH0(l)
                lam_init = 0.8 - 0.6 * math.exp(-0.3 * l)
                norm(l, 0, act1, both, True)
                dve.wait_ge(late_in, 16 * 4 * (l + 1))
                for k in range(NB):
                    g = ready_group[k]
                    dve.wait_ge(z_copied, zbase(l, g) + zt(l, g))
                    group = [p for p in PREP if p[7] == k]
                    for p in group:
                        nt = ntq(l) if p[5] else NT
                        ss = ss_z[:, ss_off[p[0]]:ss_off[p[0]] + nt * p[2]].rearrange("p (t h) -> p t h", h=p[2])
                        ins = sums(z, p[1], p[2], p[3], nt, tmp_z[0], ss)
                        if p is group[-1]:
                            ins.then_inc(ss_ready, 1)
                        else:
                            link(ins)
                    dve.wait_ge(rt_ready, l * (NB + 1) + k + 1)
                    for p in group:
                        nt = ntq(l) if p[5] else NT
                        ss = ss_z[:, ss_off[p[0]]:ss_off[p[0]] + nt * p[2]].rearrange("p (t h) -> p t h", h=p[2])
                        mul = {"naq": HD ** -0.5, "dq": DD ** -0.5, "gq": HD ** -0.5}.get(p[0], 1.0)
                        inverse(ss, mul)
                        scale_rows(nc.vector, link, z, p[1], p[2], p[3], nt, ss, p[4])
                        if p[6]:
                            rope(nc.vector, link, z, p[1], p[2], p[3], p[3], 0 if p[6] == 64 else 128,
                                 tmp_z[1][:, 0:NTL, 0:p[2] * p[3]])
                for i, (u, v) in enumerate((("lq1", "lk1"), ("lq2", "lk2"))):
                    u, v = GO[u][0], GO[v][0]
                    link(tt_op(lam_p[:, i, :], small[:, u:u + DD], small[:, v:v + DD], ALU.mult))
                    ins = nc.vector.tensor_reduce(lam_t[:, i:i + 1], lam_p[:, i, :], AX.X, ALU.add)
                ins.then_inc(lam_s, 1)
                dve.wait_ge(lam_e, l + 1)
                link(tt_op(neglam[:], lam_t[:, 3:4], lam_t[:, 2:3], ALU.subtract))
                link(nc.vector.tensor_scalar(neglam[:], neglam[:], -lam_init, None, ALU.add))
                barrier(dve, "dve")
                pb = piece_base(l, "up")
                for i in range(3):
                    rows, n = ((P, ntq(l)), (64, ntq(l)), (P, NT))[i]
                    dve.wait_ge(piece_t, pb + i + 1)
                    nc.vector.tensor_copy(cT[0:rows, i, 0:n * P],
                                          flat[0:rows, S_BANK[i % 2] * 512:S_BANK[i % 2] * 512 + n * P]).then_inc(piece_c, 1)
                for i in range(len(up_list(l))):
                    kind, t = up_list(l)[i]
                    dve.wait_ge(up_done, up_base(l) + i + 1)
                    bank = 4 + i % 2
                    if kind == "q":
                        nc.vector.tensor_copy(mlaq[:, t, :], ps[:, bank, 0:384]).then_inc(up_copied, 1)
                    else:
                        nc.vector.tensor_copy(mlak[:, t, :].rearrange("p (h d) -> p h d", d=QK)[:, :, 0:NOPE],
                                              ps[:, bank, 0:256].rearrange("p (h d) -> p h d", d=NOPE))
                        nc.vector.tensor_copy(mlak[:, t, :].rearrange("p (h d) -> p h d", d=QK)[:, :, NOPE:QK],
                                              z[:, t, KR:KR + RD].unsqueeze(1).to_broadcast([P, NH, RD]))
                        nc.vector.tensor_copy(mlav[:, t, :], ps[:, bank, 256:512]).then_inc(up_copied, 1)
                dve.wait_ge(up_copied, up_base(l) + len(up_list(l)))
                barrier(dve, "dve")
                ssq = ss_m[:, 0:4 * ntq(l)].rearrange("p (t h) -> p t h", h=4)
                ssk = ss_m[:, 24:48].rearrange("p (t h) -> p t h", h=4)
                link(sums(mlaq, 0, 4, QK, ntq(l), mtmp, ssq))
                sums(mlak, 0, 4, QK, NT, mtmp, ssk).then_inc(ss_ready, 1)
                dve.wait_ge(rt_ready, l * (NB + 1) + NB + 1)
                inverse(ssq, QK ** -0.5)
                link(nc.vector.reciprocal(ssk, ssk))
                dve.drain().then_inc(mla_rt, 1)

                for b in BR:
                    pb = piece_base(l, b)
                    for i, (src, col, w, n, dsts) in enumerate(pieces(l, b)):
                        dve.wait_ge(piece_t, pb + i + 1)
                        piece = flat[0:w, S_BANK[i % 2] * 512:S_BANK[i % 2] * 512 + n * P]
                        for dst, keep in dsts:
                            if keep is None:
                                ins = nc.vector.tensor_copy(dst[:, 0:n * P], piece)
                            else:
                                ins = nc.vector.tensor_scalar(dst[:, 0:n * P], piece, keep, None, ALU.mult)
                        ins.then_inc(piece_c, 1)
                    if b == "na":
                        dve.wait_ge(na_in, 32 * (l + 1))
                    barrier(dve, "dve")
                    ub, mb = unit_base(l, b)
                    us = units[l][b]

                    def maxima(u):
                        h, t = us[u]
                        kts = key_tiles(b, t)
                        W = P * len(kts)
                        e = (ub + u) % 8
                        if b == "na" and t == 0:
                            for (o, w), s0 in zip(NA_TAB, NA_SRC):
                                ins = tt_op(na_tab[:, o:o + w], na_T[:, h, s0:s0 + w], na_mask[:, o:o + w], ALU.add)
                            link(ins)
                        for mp in range(nmaps[b]):
                            m = u * nmaps[b] + mp
                            dve.wait_ge(s_ready, mb + m + 1)
                            s = flat[:, S_BANK[m % 2] * 512:S_BANK[m % 2] * 512 + T]
                            if b == "na" and t < NTL:
                                L = W - C
                                o, w = NA_TAB[NA_KIND[t]]
                                if u >= 2:
                                    dve.wait_ge(pt_ready, ub + u - 1)
                                link(nc.vector.tensor_tensor_reduce(
                                    out=Pp[u % 2][:, 0:L], in0=s[:, 0:L], in1=na_tab[:, o:o + w], scale=1.0,
                                    scalar=NEG, op0=ALU.add, op1=ALU.max, accum_out=nmax[:, e, 1, 0:1]))
                                link(nc.vector.tensor_reduce(nmax[:, e, 1, 1:2], s[:, 512:512 + C], AX.X, ALU.max, negate=True))
                                nc.vector.scalar_tensor_tensor(nmax[:, e, 0, 0:1], nmax[:, e, 1, 0:1], -1.0,
                                                               nmax[:, e, 1, 1:2], ALU.mult, ALU.min).then_inc(max_ready, 1)
                            else:
                                nc.vector.tensor_reduce(nmax[:, e, mp, 0:1], s[:, 0:W], AX.X, ALU.max,
                                                        negate=True).then_inc(max_ready, 1)

                    def combine(u):
                        e = (ub + u) % 8
                        W = P * len(key_tiles(b, us[u][1]))
                        dve.wait_ge(exp_done, mb + 2 * u + 2)
                        link(nc.vector.reciprocal(rinv[:, e, :], rsum[:, e, :, 0]))
                        link(nc.vector.scalar_tensor_tensor(rinv[:, e, 1:2], rinv[:, e, 1:2], neglam[:, 0:1],
                                                            rsum[:, e, 0, 0:1], ALU.mult, ALU.mult))
                        nc.vector.scalar_tensor_tensor(Pp[u % 2][:, 0:W], Pq[u % 2][:, 0:W], rinv[:, e, 1:2],
                                                       Pp[u % 2][:, 0:W], ALU.mult, ALU.add).then_inc(diff_done, 1)

                    def outputs(u):
                        h, t = us[u]
                        e = (ub + u) % 8
                        if not is_diff(b):
                            dve.wait_ge(exp_done, mb + u + 1)
                            if b == "na" and t < NTL:
                                link(tt_op(rsum[:, e, 0, 0:1], rsum[:, e, 0, 0:1], rsum[:, e, 0, 1:2], ALU.add))
                            link(nc.vector.reciprocal(rinv[:, e, 0:1], rsum[:, e, 0, 0:1]))
                        dve.wait_ge(o_ready, ub + u + 1)
                        nc.vector.tensor_scalar(o_dest(b, h, t), ps[:, O_BANK + u % 2, 0:HD],
                                                rinv[:, e, 0:1], None, ALU.mult).then_inc(o_done, 1)

                    maxima(0)
                    if is_diff(b):
                        combine(0)
                    for u in range(len(us)):
                        if u + 1 < len(us):
                            maxima(u + 1)
                        if u >= 1:
                            outputs(u - 1)
                        if is_diff(b) and u + 1 < len(us):
                            combine(u + 1)
                    outputs(len(us) - 1)
                    if b == "diff1":
                        dve.wait_ge(o_done, ub + len(us))
                        ss = ss_z[:, 0:4 * ntq(l)].rearrange("p (t h) -> p t h", h=4)
                        sums(z, DQ, 4, 64, ntq(l), dtmp, ss).then_inc(ss_ready_d, 1)
                        dve.wait_ge(rt_d, l + 1)
                        inverse(ss, 1.0 - lam_init)
                        scale_rows(nc.vector, link, z, DQ, 4, 64, ntq(l), ss, "sub")
                    barrier(dve, "dve")
                for i in range(8):
                    dve.wait_ge(ot_hi, l * 8 + i + 1)
                    tn = ntq(l) * P
                    src = flat[:, (i % 3) * 1024:(i % 3) * 1024 + tn]
                    tt_op(act1[:, 1, i, 0:tn], src, act1[:, 0, i, 0:tn].bitcast(f32), ALU.subtract).then_inc(ot_lo, 1)
                barrier(dve, "dve")
                norm(l, 0, act0, sg, False)
                fb = 2 + l * NSTEP
                with dve.Fori(0, KT) as m:
                    for bb in range(4):
                        p = bb % 2
                        dve.wait_ge(sig_ready, m * 4 + (l * NP4 + bb + 1))
                        for i, (t0, tn) in enumerate(sg):
                            src = ps[:, 3 * p + 1, 0:tn] if i == 0 else ps[:, 3 * p + 2, C:2 * C]
                            dst = y_sb[:, m, t0:t0 + tn] if bb == 0 else sig[:, p, t0:t0 + tn]
                            ins = tt_op(dst, sig[:, p, t0:t0 + tn], src, ALU.mult)
                        tt = sg[-1][0] + sg[-1][1]
                        if bb:
                            ins.then_inc(gated, 1)
                            dve.wait_ge(gated, m * 3 + (l * 24 + bb))
                            ins = tt_op(y_sb[:, m, 0:tt], y_sb[:, m, 0:tt], sig[:, p, 0:tt], ALU.add)
                        ins.then_inc(bank_free, 1)
                        dve.wait_ge(bank_free, m * 4 + (fb + bb + 1))
                        if l == 0 and bb % 2 == 0:
                            for i in range(2):
                                dve.wait_ge(ada_in[i], m * 32 + 16 * (bb // 2 + 1))
                            dve.wait_ge(ada_used, m * 2 + bb // 2)
                            row_products(ada_w, ada_acc, 2, m * 30 + (30 + 15 * (bb // 2)))
                if l == 0:
                    dve.wait_ge(ada_used, NP4 // 2)
                    take_mod(0, ADA0, ADAN)
                    take_scale(0, 1)
                barrier(dve, "dve")
                fb += NP4
                for kt in range(KT):
                    dve.wait_ge(y_hi, l * KT + kt + 1)
                    tt_op(act0[:, 1, kt, 0:tt], y_sb[:, kt, 0:tt], act0[:, 0, kt, 0:tt].bitcast(f32),
                          ALU.subtract).then_inc(y_ready, 1)
                for j in range(NO):
                    dve.wait_ge(w_used, c0 + NZ + NP4 + j + 1)
                    residual(l, 2, j, sg, j % 2)
                fb += NO
                barrier(dve, "dve")
                norm(l, 1, act1, sg, True)
                cb = c0 + NZ + NP4 + NO

                def quarter(q):
                    for j in range(16):
                        if j < 8:
                            dve.wait_ge(a_hi, q * 8 + (l * 32 + j + 1))
                            tt_op(q_sb[:, j % 2, 0:tt], r_sb[:, j % 2, 0:tt], r_sb[:, j % 2, 0:tt], ALU.mult).then_inc(bank_free, 1)
                            dve.wait_ge(bank_free, q * 16 + (fb + j + 1))
                            tt_op(act0[:, 1, j, 0:tt], q_sb[:, j % 2, 0:tt], act0[:, 0, j, 0:tt].bitcast(f32),
                                  ALU.subtract).then_inc(a_ready, 1)
                        else:
                            dve.wait_ge(w_used, q * 16 + (cb + j + 1))
                            residual(l, 5, j - 8, sg, j % 2)
                            dve.wait_ge(bank_free, q * 16 + (fb + j + 1))
                        if l == 0 and j + 1 in ADA_STEPS:
                            n = ADA_STEPS.index(j + 1)
                            for i in range(2):
                                dve.wait_ge(ada_in[i], q * 96 + 16 * (NP4 // 2 + n + 1))
                            dve.wait_ge(ada_used, q * 6 + (NP4 // 2 + n))
                            row_products(ada_w, ada_acc, 2, q * 90 + (30 + 15 * (NP4 // 2) + 15 * n))

                with dve.Fori(0, 4) as q:
                    quarter(q)
                if l == 0:
                    dve.wait_ge(ada_used, (NP4 + ADAN) // 2)
                    take_mod(1, 0, ADAN)
                    take_scale(1, 0)
                    take_scale(1, 1)
                barrier(dve, "dve")

        @block.tensor
        def _(pe):
            mm, tr = nc.tensor.matmul, nc.tensor.transpose

            def norm(sg, fresh):
                if not fresh:
                    return
                n = norm_f["pe"]
                for kt in range(KT):
                    pe.wait_ge(sq_ready, n * KT + kt + 1)
                    for i, (t0, tn) in enumerate(sg):
                        ins = mm(ps[:, i, 0:tn], ones[:], n_a[:, kt % 2, t0:t0 + tn], start=kt == 0, stop=kt == KT - 1)
                    ins.then_inc(ssq_done, 1)
                norm_f["pe"] += 1

            def chunk_products(outs, slot, kts, act_t, act_kt, sg, before=None):
                for i, kt in enumerate(kts):
                    if before:
                        before(i)
                    for n, (w, h) in enumerate(((w_hi, 0), (w_hi, 1), (w_lo, 0))):
                        for o, (t0, tn) in zip(outs, sg):
                            ins = mm(o[:, 0:tn], w[:, slot, kt * P:kt * P + P], act_t[:, h, act_kt + i, t0:t0 + tn],
                                     start=i == 0 and n == 0, stop=i == len(kts) - 1 and n == 2)
                return ins

            def column_sums(acc, n, col):
                for i in range(n):
                    for v in range(2):
                        ins = mm(col(2 * i + v), acc[:, v, i * P:(i + 1) * P], ones[:, 0:1], start=True, stop=True)
                return ins

            pe.wait_ge(const_in, 16 * 4)
            pe.wait_ge(c_ready, 1)
            for j in range(KT):
                if j % 4 == 0:
                    pe.wait_ge(ada_first[j // 4], 16)
                for kt in range(KT):
                    mm(ada_ps[:, 2 * j:2 * j + 2], ada_init[:, j, kt * P:kt * P + P], csilu[:, kt, :],
                       start=kt == 0, stop=kt == KT - 1)
            pe.wait_ge(ada_summed, 2)
            column_sums(ada_acc0, KT, lambda i: ada_ps[:, 2 * KT + i:2 * KT + i + 1])
            barrier(pe, "pe")

            for l in range(DEPTH):
                sg, c0 = segs(l), CH0(l)
                norm(both, True)
                for g in range(5):
                    n = zt(l, g)
                    for tt in range(0, n, 2):
                        for k in (zbase(l, g) + tt, zbase(l, g) + tt + 1):
                            if g == 0 and tt == 0:
                                pe.wait_ge(std_ready, std_seen(l))
                            if k >= 4:
                                pe.wait_ge(z_copied, k - 3)
                        for kt in range(KT):
                            if tt == 0 and kt % 2 == 0:
                                pe.wait_ge(w_ready, c0 + 4 * g + kt // 2 + 1)
                            if g == 0 and tt == 0:
                                pe.wait_ge(h_ready, h_base(l) + kt + 1)
                            slot, w0 = (4 * g + kt // 2) % SLOTS, (kt % 2) * ZG
                            for ti in (tt, tt + 1):
                                k = zbase(l, g) + ti
                                for i, (h, w) in enumerate(((0, w_hi), (1, w_hi), (0, w_lo))):
                                    ins = mm(ps[:, k % 4, 0:ZG], act1[:, h, kt, ti * P:ti * P + P], w[:, slot, w0:w0 + ZG],
                                             start=kt == 0 and i == 0, stop=kt == KT - 1 and i == 2)
                                if kt == KT - 1:
                                    ins.then_inc(z_prod, 1)
                            if tt == n - 2 and kt % 2 == 1:
                                if kt < KT - 1:
                                    ins.then_inc(w_used, 1)
                                else:
                                    pe.drain().then_inc(w_used, 1)
                barrier(pe, "pe")
                pb = piece_base(l, "up")
                for i, (col, w, n) in enumerate(((CQ, P, ntq(l)), (CQ + P, 64, ntq(l)), (CKV, P, NT))):
                    if i >= 2:
                        pe.wait_ge(piece_c, pb + i - 1)
                    for t in range(n):
                        c_ = S_BANK[i % 2] * 512 + t * P
                        ins = tr(flat[0:w, c_:c_ + P], z[:, t, col:col + w], ident[:])
                    ins.then_inc(piece_t, 1)
                pe.wait_ge(piece_c, pb + 3)
                for i, (kind, t) in enumerate(up_list(l)):
                    if i >= 2:
                        pe.wait_ge(up_copied, up_base(l) + i - 1)
                    bank = 4 + i % 2
                    if kind == "q":
                        mm(ps[:, bank, 0:384], cT[:, 0, t * P:t * P + P], uq_sb[:, 0, :], start=True, stop=False)
                        ins = mm(ps[:, bank, 0:384], cT[0:64, 1, t * P:t * P + P], uq_sb[0:64, 1, :], start=False, stop=True)
                    else:
                        ins = mm(ps[:, bank, :], cT[:, 2, t * P:t * P + P], ukv_sb[:], start=True, stop=True)
                    ins.then_inc(up_done, 1)
                barrier(pe, "pe")
                for b in BR:
                    pb = piece_base(l, b)
                    if b == "mla":
                        pe.wait_ge(mla_prepared, l + 1)
                    for i, (src, col, w, n, dst) in enumerate(pieces(l, b)):
                        if i >= 2:
                            pe.wait_ge(piece_c, pb + i - 1)
                        for t in range(n):
                            c_ = S_BANK[i % 2] * 512 + t * P
                            ins = tr(flat[0:w, c_:c_ + P], src[:, t, col:col + w], ident[:])
                        ins.then_inc(piece_t, 1)
                    barrier(pe, "pe")
                    ub, mb = unit_base(l, b)
                    us = units[l][b]

                    def scores(u):
                        h, t = us[u]
                        kts = key_tiles(b, t)
                        for mp in range(nmaps[b]):
                            m = u * nmaps[b] + mp
                            if m >= 2:
                                pe.wait_ge(exp_done, mb + m - 1)
                            s = flat[:, S_BANK[m % 2] * 512:S_BANK[m % 2] * 512 + T]
                            q, k = qk_operands(b, h, mp, t)
                            lat = [x for x in kts if x < NTL]
                            if lat:
                                ins = mm(s[:, 0:P * len(lat)], q, k[:, lat[0] * P:(lat[-1] + 1) * P], start=True, stop=True)
                                ins = mm(s[:, S:T], q, k[:, S:T], start=True, stop=True)
                            else:
                                ins = mm(s[:, 0:C], q, k[:, S:T], start=True, stop=True)
                            ins.then_inc(s_ready, 1)

                    def transposes(u):
                        if is_diff(b):
                            pe.wait_ge(diff_done, diff_base(l, b) + u + 1)
                        else:
                            pe.wait_ge(exp_done, mb + u + 1)
                        if u >= 1:
                            pe.wait_ge(pt_copied, ub + u)
                        for j in range(len(key_tiles(b, us[u][1]))):
                            c_ = PT_BANK * 512 + j * P
                            ins = tr(flat[:, c_:c_ + P], Pp[u % 2][:, j * P:j * P + P], ident[:])
                        ins.then_inc(pt_ready, 1)

                    def values(u):
                        h, t = us[u]
                        kts = key_tiles(b, t)
                        pe.wait_ge(pt_copied, ub + u + 1)
                        if u >= 2:
                            pe.wait_ge(o_done, ub + u - 1)
                        for j, kt in enumerate(kts):
                            ins = mm(ps[:, O_BANK + u % 2, 0:HD], PTs[:, u % 2, j * P:j * P + P],
                                     v_slice(b, h, kt), start=j == 0, stop=j == len(kts) - 1)
                        ins.then_inc(o_ready, 1)

                    scores(0)
                    for u in range(len(us)):
                        if u + 1 < len(us):
                            scores(u + 1)
                        transposes(u)
                        if u >= 1:
                            values(u - 1)
                    values(len(us) - 1)
                    barrier(pe, "pe")
                for i in range(8):
                    if i >= 3:
                        pe.wait_ge(ot_lo, l * 8 + i - 2)
                    c_in = (MLO, NAQ, DQ, GQ)[i // 2] + (i % 2) * P
                    for t in range(ntq(l)):
                        c_ = (i % 3) * 1024 + t * P
                        ins = tr(flat[:, c_:c_ + P], z[:, t, c_in:c_in + P], ident[:])
                    ins.then_inc(ot_ready, 1)
                barrier(pe, "pe")
                cb, fb = c0 + NZ, 2 + l * NSTEP

                def h_rows(base):
                    return lambda kt: pe.wait_ge(h_ready, h_base(l) + base * KT + kt + 1)

                with pe.Fori(0, KT) as m:
                    for bb in range(4):
                        p = bb % 2
                        pe.wait_ge(w_ready, m * 4 + (cb + bb + 1))
                        pe.wait_ge(bank_free, m * 4 + (fb + bb - 1))
                        chunk_products([ps[:, 3 * p, :], ps[:, 3 * p + 2, 0:C]], bb, range(8), act0, 0, sg,
                                       h_rows(1) if bb == 0 else None)
                        chunk_products([ps[:, 3 * p + 1, :], ps[:, 3 * p + 2, C:2 * C]], bb, range(8, 10), act1, 2 * bb,
                                       sg).then_inc(w_used, 1)
                        if l == 0 and bb % 2 == 1:
                            pe.wait_ge(ada_summed, m * 2 + (2 + bb // 2 + 1))
                            column_sums(ada_acc, 2, lambda i: ada_ps[:, bass.ds(m * 8 + (2 * ADA0 + 2 * (bb - 1) + i), 1)]
                                        ).then_inc(ada_used, 1)
                barrier(pe, "pe")
                cb, fb = cb + NP4, fb + NP4
                for j in range(NO):
                    p = j % 2
                    pe.wait_ge(w_ready, cb + j + 1)
                    pe.wait_ge(bank_free, fb + j - 1)

                    def y_rows(kt):
                        pe.wait_ge(y_ready, l * KT + kt + 1)

                    chunk_products([ps[:, 3 * p, :], ps[:, 3 * p + 2, :]], j % SLOTS, range(8), act0, 0, sg,
                                   y_rows if j == 0 else None).then_inc(w_used, 1)
                barrier(pe, "pe")
                norm(sg, True)
                cb, fb = cb + NO, fb + NO
                with pe.Fori(0, 4) as q:
                    for j in range(16):
                        p = j % 2
                        pe.wait_ge(w_ready, q * 16 + (cb + j + 1))
                        pe.wait_ge(bank_free, q * 16 + (fb + j - 1))

                        def a_rows(kt):
                            pe.wait_ge(a_ready, q * 8 + (l * 32 + kt + 1))

                        chunk_products([ps[:, 3 * p, :], ps[:, 3 * p + 2, :]], j % SLOTS, range(8),
                                       act1 if j < 8 else act0, 0, sg, a_rows if j == 8 else h_rows(2) if j == 0 else None).then_inc(w_used, 1)
                        if l == 0 and j in ADA_STEPS:
                            n = ADA_STEPS.index(j)
                            pe.wait_ge(ada_summed, q * 6 + (2 + NP4 // 2 + n + 1))
                            column_sums(ada_acc, 2, lambda i: ada_ps[:, bass.ds(q * 24 + (2 * ADAN + 4 * n + i), 1)]
                                        ).then_inc(ada_used, 1)
                barrier(pe, "pe")


def kernel(x, c, ctx, c_ctx, w_ada, b_ada, g_norm1, g_norm2, w_in, g_mla_qa, w_mla_uq, g_mla_kva, w_mla_ukv,
           g_mla_q, g_mla_k, g_na_q, g_na_k, na_rpb, g_diff_q, g_diff_k, diff_lq1, diff_lk1, diff_lq2, diff_lk2,
           g_diff_sub, g_gqa_q, g_gqa_k, w_branch, w_out, w_up, w_down):
    import concourse.bacc as bacc
    from concourse.bass_utils import run_bass_kernel_spmd

    L = DEPTH
    perm = (np.arange(S) % GR) * GW + np.arange(S) // GR
    tokens = np.concatenate([np.asarray(x)[0][perm], np.asarray(ctx)[0]])
    feature = lambda v: np.moveaxis(np.asarray(v).reshape(*v.shape[:-1], -1, P), -1, 0)
    arrays = {"xT": np.ascontiguousarray(feature(tokens).transpose(0, 2, 1)),
              "cT": np.stack([feature(np.asarray(c)[0]), feature(np.asarray(c_ctx))], -1),
              "b_ada": feature(b_ada),
              "gn": np.stack([feature(g_norm1), feature(g_norm2)], 2),
              "ident": np.eye(P, dtype=np.float32)}

    def tiles(w, cols):
        l, k, n = w.shape
        return w.reshape(l, k // P, P, n // cols, cols).transpose(0, 3, 2, 1, 4).reshape(l, n // cols, P, -1)

    w_in = np.asarray(w_in)
    o = np.cumsum([0, QL, KVL, RD, 768, 768, 512]).tolist()
    na, df, gq = o[3], o[4], o[5]
    col = lambda b, n: np.arange(b, b + n)
    gq_cols = np.concatenate([col(gq + HD * h, HD) for h in GQA_ORDER])
    order = np.concatenate([col(o[0], QL), col(na, 256), col(df, 256), gq_cols,
                            col(o[1], KVL), col(o[2], RD), col(na + 256, 512), col(df + 256, 512), col(gq + 256, 256)])
    wz = w_in[:, :, order].reshape(L, KT // 2, 2, P, 5, ZG).transpose(0, 4, 1, 3, 2, 5).reshape(L, NZ, P, 2 * ZG)
    gates = tiles(w_in[:, :, o[6]:], P).reshape(L, 4, KT, P, KT * P).transpose(0, 2, 1, 3, 4)
    wb = np.asarray(w_branch).reshape(L, 4, 2, P, KT, P).transpose(0, 4, 1, 3, 2, 5).reshape(L, KT, 4, P, 2 * P)
    up = tiles(np.asarray(w_up), P).reshape(L, 4, 8, P, KT * P)
    down = np.asarray(w_down).reshape(L, 4, KT, P, KT, P).transpose(0, 1, 4, 3, 2, 5).reshape(L, 4, 8, P, KT * P)
    arrays["w_ada"] = tiles(np.asarray(w_ada), P).reshape(L * ADAN, P, KT * P)
    arrays["wz"] = wz
    arrays["wp"] = np.concatenate([gates, wb], -1).reshape(L * NP4, P, WMAX)
    arrays["wo"] = tiles(np.asarray(w_out), P).reshape(L * NO, P, KT * P)
    arrays["wm"] = np.concatenate([up, down], 2).reshape(L * NM, P, KT * P)
    uq = np.zeros((L, 2 * P, 4 * QK), np.float32)
    uq[:, 0:QL] = w_mla_uq
    arrays["uq"] = uq.reshape(L, 2, P, 4 * QK).transpose(0, 2, 1, 3)
    arrays["ukv"] = np.asarray(w_mla_ukv).reshape(L, KVL, NH, 2, HD).transpose(0, 1, 3, 2, 4).reshape(L, KVL, 512)
    arrays["small"] = np.concatenate([np.asarray(v) for v in (
        g_mla_qa, g_mla_kva, g_mla_q, g_mla_k, g_na_q, g_na_k, g_diff_q, g_diff_k, g_diff_sub, g_gqa_q, g_gqa_k,
        diff_lq1, diff_lk1, diff_lq2, diff_lk2)], -1)

    tok = np.arange(S)
    rows, cols = (tok % GR).astype(np.float32), (tok // GR).astype(np.float32)
    tabs = []
    for rot in (HD, RD):
        n = rot // 4
        inv = np.power(np.float32(10000.0), -np.arange(n, dtype=np.float32) / np.float32(n)).astype(np.float32)
        ar, ac = rows[:, None] * inv, cols[:, None] * inv
        tabs += [np.cos(np.concatenate([ar, ar, ac, ac], -1)), np.sin(np.concatenate([-ar, ar, -ac, ac], -1))]
    arrays["rope"] = np.concatenate(tabs, -1).astype(np.float32).reshape(NTL, P, 192).transpose(1, 0, 2)

    qc, qr = np.arange(P) // GR, np.arange(P) % GR
    kc, kr = np.arange(384) // GR - 16, np.arange(384) % GR
    dc = kc[None] - qc[:, None] + 15
    dr = kr[None] - qr[:, None] + 7
    padded = np.pad(np.asarray(na_rpb), ((0, 0), (0, 0), (0, 0), (0, 1)))
    arrays["na_rows"] = padded[:, :, dr, np.where((dc >= 0) & (dc <= 30), dc, 31)]
    mask = []
    for kind, t in ((0, 0), (1, 1), (2, 3)):
        q_col = 16 * t + qc
        start = np.clip(q_col - 8, 0, GW - 16)[:, None]
        k_col = (16 * t + kc)[NA_SRC[kind]:NA_SRC[kind] + NA_TAB[kind][1]][None]
        mask.append(np.where((k_col >= start) & (k_col < start + 16), 0.0, NEG))
    arrays["na_mask"] = np.concatenate(mask, -1).astype(np.float32)

    nc = bacc.Bacc("TRN2", target_bir_lowering=False, num_devices=1, dynamic_dma_scratch_size=1024)
    arrays = {k: np.ascontiguousarray(v) for k, v in arrays.items()}
    aps = {k: nc.dram_tensor("in_" + k, v.shape, mybir.dt.from_np(v.dtype), kind="ExternalInput").ap() for k, v in arrays.items()}
    out = nc.dram_tensor("out", (P, KT, S), mybir.dt.float32, kind="ExternalOutput").ap()
    program(nc, aps, out)
    ins = {"in_" + k: v for k, v in arrays.items()}
    got = np.asarray(run_bass_kernel_spmd(nc, [ins], core_ids=[0]).results[0]["out"])
    y = np.empty((1, S, D), np.float32)
    y[0, perm] = got.transpose(2, 1, 0).reshape(S, D)
    return y
```

```python
import math
from contextlib import ExitStack

import numpy as np
import concourse.bass as bass
from concourse import mybir

D, DEPTH, S, C = 1024, 2, 512, 256
T = S + C
P = 128
KT = D // P
GW, GR = 64, S // 64
HD, NH = 64, 4
QL, KVL, RD, NOPE, QK = 192, 128, 32, 64, 96
DD = 32
EPS = 1e-6
NEG = -1.0e30
GQA_ORDER = (0, 2, 1, 3)
NT, NTL = T // P, S // P
ZG = 480
NKVG, NQG = 3, 2
ZC = ZG * (NKVG + NQG)
CQ, NAQ, DQ, GQ, CKV, KR, NAK, NAV, DK, DV, GK, GV = np.cumsum(
    [0, 192, 256, 256, 256, 128, 32, 256, 256, 256, 256, 128]).tolist()
MLO = NAK
NZ, NP4, NO, NM = 20, 32, 8, 64
NCH = NZ + NP4 + NO + NM
SLOTS = 4
WMAX = 10 * P
ADA0 = 16
ADAN = 48
names = [("qa", 192), ("kva", 128), ("mq", 96), ("mk", 96), ("nq", 64), ("nk", 64), ("dq", 32),
         ("dk", 32), ("sub", 64), ("gq", 64), ("gk", 64), ("lq1", 32), ("lk1", 32), ("lq2", 32), ("lk2", 32)]
GO, _o = {}, 0
for _n, _w in names:
    GO[_n] = (_o, _w)
    _o += _w
SM = _o


def na_tiles(i):
    return list(range(max(i - 1, 0), min(i + 2, NTL)))


NA_KIND = [0, 1, 1, 2]
NA_TAB = [(0, 256), (256, 384), (640, 256)]
NA_SRC = [128, 0, 0]


def program(nc, a, out):
    f32, f32r = mybir.dt.float32, mybir.dt.float32r
    ALU, ACT, AX = mybir.AluOpType, mybir.ActivationFunctionType, mybir.AxisListType
    ctx = ExitStack()
    with ctx:
        sem = lambda name: ctx.enter_context(nc.semaphore(name))
        persistent = lambda name, shape, dt=f32: ctx.enter_context(nc.sbuf_tensor(name, shape, dt))

        x_sb = persistent("x_sb", [P, KT, T])
        w_hi = persistent("w_hi", [P, SLOTS, WMAX], f32r)
        w_lo = persistent("w_lo", [P, SLOTS, WMAX], f32r)
        w_raw = persistent("w_raw", [P, 2, WMAX])
        ada_w = persistent("ada_w", [P, 2, KT * P])
        ada_acc = persistent("ada_acc", [P, 2, 2 * P])
        rstd = persistent("rstd", [P, T])
        ident = persistent("ident", [P, P])
        ones = persistent("ones", [P, P])
        eps_sb = persistent("eps_sb", [P, 1])
        c_sb = persistent("c_sb", [P, KT, 2])
        csig = persistent("csig", [P, KT, 2])
        csilu = persistent("csilu", [P, KT, 2])
        b_sb = persistent("b_sb", [P, DEPTH, ADAN])
        gn_sb = persistent("gn_sb", [P, DEPTH, 2, KT])
        mod = persistent("mod", [P, DEPTH, ADAN, 2])
        nscale = persistent("nscale", [P, DEPTH, 2, KT, 2])
        neglam = persistent("neglam", [P, 1])
        lam_t = persistent("lam_t", [P, 4])
        lam_p = persistent("lam_p", [P, 2, DD])
        ss_m = persistent("ss_m", [P, 60])
        row_mask = persistent("row_mask", [P, 6])
        nmax = persistent("nmax", [P, 8, 2, 2])
        rsum = persistent("rsum", [P, 8, 2, 2])
        rinv = persistent("rinv", [P, 8, 2])

        KB = 1024
        Z_END = NT * ZC * 4
        F1 = Z_END
        Y0 = F1 + 2 * KT * T * 4
        A0 = (nc.sbuf_usable_end - (Y0 + 25 * KB)) // 64 * 64
        assert nc.sbuf_base <= A0
        at = lambda name, off, shape, dt=f32: nc.alloc_sbuf_tensor_at(name, shape, dt, offset=A0 + off)
        z = at("z", 0, [P, NT, ZC])
        act0 = at("act0", 0, [P, 2, KT, T], f32r)
        act1 = at("act1", F1, [P, 2, KT, T], f32r)
        ada_init = at("ada_init", 0, [P, ADA0, KT * P])
        ada_acc0 = at("ada_acc0", Y0 + 6 * KB, [P, 2, KT * P])
        sig = at("sig", 48 * KB, [P, 2, T])
        y_sb = at("y_sb", Y0, [P, KT, T])
        n_a = at("n_a", Y0, [P, 2, T])
        n_b = at("n_b", Y0, [P, 4, T])
        r_sb = at("r_sb", Y0, [P, 2, T])
        q_sb = at("q_sb", Y0 + 6 * KB, [P, 2, T])
        tmp_z = [at("tmp_z0", Y0, [P, NT, 256]), at("tmp_z1", Y0 + 6 * KB, [P, NT, 256])]
        ss_z = at("ss_z", Y0 + 12 * KB, [P, 256])
        ukv_sb = at("ukv_sb", Y0 + 13 * KB, [P, 512])
        uq_sb = at("uq_sb", Y0 + 15 * KB, [P, 2, 384])
        rope_sb = at("rope_sb", Y0 + 18 * KB, [P, NTL, 192])
        small = at("small", Y0 + 21 * KB, [P, SM])
        A_ = F1
        cT = at("cT", A_ + 9 * KB, [P, 3, T])
        mlaq = at("mlaq", A_ + 24 * KB, [P, NT, 384])
        mlak = at("mlak", A_ + 33 * KB, [P, NT, 384])
        mlav = at("mlav", A_ + 42 * KB, [P, NT, 256])
        QT = at("QT", A_, [P, 2, T])
        KTr = at("KTr", A_ + 6 * KB, [P, 4, T])
        QTm = at("QTm", A_, [P, 4, T])
        KTm = at("KTm", A_ + 12 * KB, [P, 4, T])
        na_T = at("na_T", A_ + 18 * KB, [P, NH, 384])
        na_tab = ada_w[:, 0, :]
        na_mask = at("na_mask", Y0 + 13 * KB, [P, 896])
        Pp = [at("Pp0", Y0, [P, T]), at("Pp1", Y0 + 3 * KB, [P, T])]
        Pq = [at("Pq0", A_ + 18 * KB, [P, T]), at("Pq1", A_ + 21 * KB, [P, T])]
        PTs = at("PTs", Y0 + 6 * KB, [P, 2, T])

        ps = ctx.enter_context(nc.psum_tensor("ps", [P, 8, 512], f32))
        flat = ps[:, :, :].rearrange("p b c -> p (b c)")
        ada_ps = ps[:, 7, :]

        const_in = sem("const_in")
        late_in = sem("late_in")
        na_in = sem("na_in")
        w_in = [sem("w_in0"), sem("w_in1")]
        w_rounded = sem("w_rounded")
        w_ready = sem("w_ready")
        w_used = sem("w_used")
        x_in = sem("x_in")
        ada_first = [sem(f"ada_first{j}") for j in range(4)]
        ada_step = sem("ada_step")
        ada_summed = sem("ada_summed")
        ada_in = [sem("ada_in0"), sem("ada_in1")]
        ada_used = sem("ada_used")
        pe_phase, act_phase, dve_phase = sem("pe_phase"), sem("act_phase"), sem("dve_phase")
        act_step, dve_step = sem("act_step"), sem("dve_step")
        sq_ready = sem("sq_ready")
        sq_added = sem("sq_added")
        ssq_done = sem("ssq_done")
        std_ready, normed, modded, h_ready = sem("std_ready"), sem("normed"), sem("modded"), sem("h_ready")
        z_prod, z_copied = sem("z_prod"), sem("z_copied")
        ss_ready, rt_ready = sem("ss_ready"), sem("rt_ready")
        piece_t = sem("piece_t")
        piece_c, piece_a = sem("piece_c"), sem("piece_a")
        up_done, up_copied = sem("up_done"), sem("up_copied")
        s_ready, max_ready, exp_done = sem("s_ready"), sem("max_ready"), sem("exp_done")
        diff_done = sem("diff_done")
        pt_ready, pt_copied = sem("pt_ready"), sem("pt_copied")
        o_ready, o_done = sem("o_ready"), sem("o_done")
        ot_ready, ot_hi, ot_lo = sem("ot_ready"), sem("ot_hi"), sem("ot_lo")
        bank_free = sem("bank_free")
        sig_ready = sem("sig_ready")
        y_hi, y_ready = sem("y_hi"), sem("y_ready")
        a_hi, a_ready = sem("a_hi"), sem("a_ready")
        c_sig, c_ready, lam_e = sem("c_sig"), sem("c_ready"), sem("lam_e")
        lat_sums, lat_roots, lat_inv, lat_prepared = sem("lat_sums"), sem("lat_roots"), sem("lat_inv"), sem("lat_prepared")
        sub_sums, sub_roots, sub_inv, sub_prepared = sem("sub_sums"), sem("sub_roots"), sem("sub_inv"), sem("sub_prepared")
        rows_prepared = sem("rows_prepared")
        relu_ready, gated = sem("relu_ready"), sem("gated")
        lam_s, pool_step = sem("lam_s"), sem("pool_step")
        out_done = sem("out_done")

        block = ctx.enter_context(nc.Block())

        segs = lambda l: [(0, S), (S, C)] if l == 0 else [(0, S)]
        both = [(0, S), (S, C)]
        ntq = lambda l: NT if l == 0 else NTL
        zt = lambda l, g: NT if g >= NQG else ntq(l)
        zbase = lambda l, g: sum(zt(k, j) for k in range(l) for j in range(5)) + sum(zt(l, j) for j in range(g))
        PREP = [("cq", CQ, 1, 192, "qa", True, 0, 0), ("naq", NAQ, 4, 64, "nq", True, 0, 0),
                ("dq", DQ, 8, 32, "dq", True, 32, 0), ("gq", GQ, 4, 64, "gq", True, 64, 0),
                ("ckv", CKV, 1, 128, "kva", False, 0, 1), ("nak", NAK, 4, 64, "nk", False, 0, 1),
                ("dk", DK, 8, 32, "dk", False, 32, 1)]
        NB = 2
        ready_group = [1, 3]
        ss_off, off = {}, 0
        for k in range(NB):
            for p in PREP:
                if p[7] == k:
                    ss_off[p[0]] = off
                    off += NT * p[2]
        assert off <= 256

        BR = ("na", "diff0", "diff1", "gqa", "mla")
        HEADS = {"na": range(NH), "diff0": (0, 1), "diff1": (2, 3), "gqa": range(NH), "mla": range(NH)}
        PIECES = {"up": 3, "na": 4, "diff0": 3, "diff1": 3, "gqa": 4, "mla": 8}
        is_diff = lambda b: b.startswith("diff")
        tile_kinds = lambda l: (range(NTL, ntq(l)), range(NTL))
        units = {l: {b: [(h, t) for tiles in tile_kinds(l) for h in HEADS[b] for t in tiles] for b in BR}
                 for l in range(DEPTH)}
        nmaps = {b: 2 if is_diff(b) else 1 for b in BR}
        diff_base = lambda l, b: sum(len(units[k]["diff0"]) * 2 for k in range(l)) + (len(units[l]["diff0"]) if b == "diff1" else 0)

        def unit_base(l, b):
            u = m = 0
            for k in range(DEPTH):
                for c in BR:
                    if (k, c) == (l, b):
                        return u, m
                    u += len(units[k][c])
                    m += len(units[k][c]) * nmaps[c]

        def piece_base(l, b, parity=None):
            count = lambda c: PIECES[c] if parity is None else (PIECES[c] + 1 - parity) // 2
            order = ("up",) + BR
            return (sum(count(c) for c in order) * l + sum(count(c) for c in order[:order.index(b)]))

        def key_tiles(b, t):
            if t >= NTL:
                return list(range(NTL, NT))
            return (na_tiles(t) if b == "na" else list(range(NTL))) + list(range(NTL, NT))

        def branch_view(b):
            return {"na": ((z, NAQ), (z, NAK), (z, NAV)), "diff0": ((z, DQ), (z, DK), (z, DV)),
                    "diff1": ((z, DQ + 128), (z, DK + 128), (z, DV)),
                    "gqa": ((z, GQ), (z, GK), (z, GV)), "mla": ((mlaq, 0), (mlak, 0), (mlav, 0))}[b]

        def up_pieces(l):
            return [(z, col, w, n, [(cT[0:w, i, :], None)]) for i, (col, w, n) in
                    enumerate(((CQ, P, ntq(l)), (CQ + P, 64, ntq(l)), (CKV, P, NT)))]

        def pieces(l, b):
            (qs, q0), (ks, k0), _ = branch_view(b)
            if b == "mla":
                return ([(qs, q0 + 96 * h, 96, ntq(l), [(QTm[0:96, h, :], None)]) for h in range(4)]
                        + [(ks, k0 + 96 * h, 96, NT, [(KTm[0:96, h, :], None)]) for h in range(4)])
            nq = 1 if is_diff(b) else 2
            per, m0 = (4, 2) if is_diff(b) else (2, 0)
            parts = {"na": ((0, (0, 1)), (1, (0, 1))), "gqa": ((0, (0,)), (0, (1,)))}.get(b, ((0, (0, 1)), (0, (2, 3))))
            return ([(qs, q0 + 128 * j, 128, ntq(l), [(QT[:, j, :], None)]) for j in range(nq)]
                    + [(ks, k0 + 128 * j, 128, NT, [(KTr[:, per * j + i, :], row_mask[:, m0 + i:m0 + i + 1])
                                                    for i in kept]) for j, kept in parts])

        def o_dest(b, h, t):
            if b == "gqa":
                h = GQA_ORDER[h]
            c0 = {"na": NAQ, "diff0": DQ, "diff1": DQ, "gqa": GQ, "mla": MLO}[b] + 64 * h
            return z[:, t, c0:c0 + 64]

        def qk_operands(b, h, mp, t):
            q = slice(t * P, t * P + P)
            if b == "mla":
                return QTm[0:96, h, q], KTm[0:96, h, :]
            if is_diff(b):
                return QT[:, 0, q], KTr[:, (h % 2) * 2 + mp, :]
            if b == "na":
                return QT[:, h // 2, q], KTr[:, h, :]
            return QT[:, h // 2, q], KTr[:, h % 2, :]

        def v_slice(b, h, kt):
            (vs, v0) = branch_view(b)[2]
            hv = h % 2 if b == "gqa" else h
            return vs[:, kt, v0 + 64 * hv:v0 + 64 * hv + 64]

        S_BANK = [0, 2]
        PT_BANK, O_BANK = 4, 6

        ZBANKS = 6
        NSTEP = NP4 + NO + NM
        up_list = lambda l: [("q", t) for t in range(ntq(l))] + [("kv", t) for t in range(NT)]
        up_base = lambda l: sum(len(up_list(k)) for k in range(l))
        h_base = lambda l: l * 3 * KT
        std_seen = lambda l: 2 + 4 * l
        ADA_STEPS = (1, 3, 5, 9, 11, 13)
        LAST_PHASE = 1 + 4 * DEPTH
        n_up = lambda l: up_base(l) + len(up_list(l))
        ROOT_UNIT = (18, 13)

        phase = {"pe": 0, "act": 0, "dve": 0}
        norm_no = {"act": 0, "dve": 0}
        stat_base = lambda f: (KT * f, (KT - 1) * f)
        PH = {"pe": pe_phase, "act": act_phase, "dve": dve_phase}

        def barrier(eng, me):
            eng.drain().then_inc(PH[me], 1)
            phase[me] += 1
            for other in PH:
                if other != me:
                    eng.wait_ge(PH[other], phase[me])

        CH0 = lambda l: l * NCH

        def scale_rows(e, link, src, c0, heads, d, nt, ss, g):
            v = src[:, 0:nt, c0:c0 + heads * d].rearrange("p t (h d) -> p t h d", d=d)
            link(e.tensor_tensor(v, v, ss.unsqueeze(3).to_broadcast([P, nt, heads, d]), ALU.mult))
            o, w = GO[g]
            gb = small[:, o:o + w].unsqueeze(1).unsqueeze(1).to_broadcast([P, nt, heads, d])
            link(e.tensor_tensor(v, v, gb, ALU.mult))

        def rope(e, link, src, c0, heads, stride, d, tab, tmp):
            n, s0 = d // 4, c0 - (stride - d)
            v = src[:, 0:NTL, s0:s0 + heads * stride].rearrange("p t (h s) -> p t h s", s=stride)[:, :, :, stride - d:stride]
            w = tmp.rearrange("p t (h d) -> p t h d", d=d)
            for q in range(4):
                o = q ^ 1
                sin = rope_sb[:, :, tab + d + q * n:tab + d + (q + 1) * n].unsqueeze(2).to_broadcast([P, NTL, heads, n])
                ins = e.tensor_tensor(w[:, :, :, q * n:(q + 1) * n], v[:, :, :, o * n:(o + 1) * n], sin, ALU.mult)
            link(ins)
            cos = rope_sb[:, :, tab:tab + d].unsqueeze(2).to_broadcast([P, NTL, heads, d])
            link(e.tensor_tensor(v, v, cos, ALU.mult))
            link(e.tensor_tensor(v, v, w, ALU.add))

        @block.sync
        def _(sp):
            for dst, src in ((c_sb, a["cT"]), (b_sb, a["b_ada"]), (gn_sb, a["gn"]), (ident, a["ident"])):
                sp.dma_start(dst[:], src).then_inc(const_in, 16)
            for j in (2, 0, 3, 1):
                if j == 1:
                    sp.dma_start(x_sb[:], a["xT"]).then_inc(x_in, 16)
                n = ADA0 // 4
                sp.dma_start(ada_init[:, j * n:(j + 1) * n, :],
                             a["w_ada"][j * n:(j + 1) * n].rearrange("j p n -> p j n")).then_inc(ada_first[j], 16)

            def load(c, src, width, k):
                if not isinstance(c, int) or c >= 2:
                    sp.wait_ge(w_ready, c - 1)
                sp.dma_start(w_raw[:, k, 0:width], src).then_inc(w_in[k], 16)

            for l in range(DEPTH):
                c0 = CH0(l)
                for j in range(NZ):
                    load(c0 + j, a["wz"][l, j], 2 * ZG, j % 2)
                c0 += NZ
                with sp.Fori(0, KT) as m:
                    for b in range(4):
                        load(m * 4 + (c0 + b), a["wp"][l * NP4 + 4 * m + b], WMAX, b % 2)
                c0 += NP4
                for j in range(NO):
                    load(c0 + j, a["wo"][l * NO + j], KT * P, j % 2)
                c0 += NO
                with sp.Fori(0, 4) as q:
                    for j in range(16):
                        load(q * 16 + (c0 + j), a["wm"][l * NM + 16 * q + j], KT * P, j % 2)
            sp.wait_ge(dve_phase, LAST_PHASE)
            sp.dma_start(out, x_sb[:, :, 0:S]).then_inc(out_done, 16)
            sp.wait_ge(out_done, 16)

        @block.gpsimd
        def _(pool):
            chain = [0]

            def link(ins):
                chain[0] += 1
                ins.then_inc(pool_step, 1)
                pool.wait_ge(pool_step, chain[0])

            def sums(src, c0, heads, d, nt, tmp, ss):
                v, w = src[:, 0:nt, c0:c0 + heads * d], tmp[:, 0:nt, 0:heads * d]
                link(nc.gpsimd.tensor_tensor(w, v, v, ALU.mult))
                w = w.rearrange("p t (h d) -> p t h d", d=d)
                ss = ss if len(ss.shape) == 3 else ss.rearrange("p (t h) -> p t h", h=heads)
                n = d
                while n % 2 == 0:
                    n = n // 2
                    link(nc.gpsimd.tensor_tensor(w[:, :, :, 0:n], w[:, :, :, 0:n], w[:, :, :, n:2 * n], ALU.add))
                for i in range(1, n):
                    link(nc.gpsimd.tensor_tensor(w[:, :, :, 0:1], w[:, :, :, 0:1], w[:, :, :, i:i + 1], ALU.add))
                link(nc.gpsimd.tensor_scalar(ss, w[:, :, :, 0], 1.0 / d, EPS, ALU.mult, ALU.add))

            def low(c, width, k):
                pool.wait_ge(w_rounded, c + 1)
                nc.gpsimd.tensor_tensor(w_lo[:, k, 0:width], w_raw[:, k % 2, 0:width],
                                        w_hi[:, k, 0:width].bitcast(f32), ALU.subtract).then_inc(w_ready, 1)

            for l in range(DEPTH):
                c0 = CH0(l)
                for j in range(NZ):
                    low(c0 + j, 2 * ZG, j % SLOTS)
                for b in range(4):
                    low(c0 + NZ + b, WMAX, b)
                pool.wait_ge(up_copied, n_up(l))
                nq = ntq(l)
                square = z[:, :, CQ:CQ + QL]
                sums(z, GK, 2, HD, NT, square, ss_m[:, 48:60])
                for src, o, nt in ((mlaq, 0, nq), (mlak, 24, NT)):
                    ss = ss_m[:, o:o + 4 * nt].rearrange("p (t h) -> p t h", h=NH)
                    for j in range(2):
                        sums(src, 2 * QK * j, 2, QK, nt, square, ss[:, :, 2 * j:2 * j + 2])
                pool.drain().then_inc(lat_sums, 1)
                pool.wait_ge(lat_inv, l + 1)
                rot = z[:, 0:NTL, CKV:CKV + P]
                scale_rows(nc.gpsimd, link, z, GK, 2, HD, NT, ss_m[:, 48:60].rearrange("p (t h) -> p t h", h=2), "gk")
                rope(nc.gpsimd, link, z, GK, 2, HD, HD, 0, rot)
                for src, ss, nt, g in ((mlaq, ss_m[:, 0:4 * nq], nq, "mq"), (mlak, ss_m[:, 24:48], NT, "mk")):
                    scale_rows(nc.gpsimd, link, src, 0, NH, QK, nt, ss.rearrange("p (t h) -> p t h", h=NH), g)
                    rope(nc.gpsimd, link, src, NOPE, NH, QK, RD, 128, rot)
                pool.drain().then_inc(lat_prepared, 1)
                pool.wait_ge(o_done, unit_base(l, "gqa")[0])
                ss = ss_z[:, 0:4 * nq].rearrange("p (t h) -> p t h", h=4)
                sums(z, DQ, 4, HD, nq, z[:, :, DK:DK + 256], ss)
                pool.drain().then_inc(sub_sums, 1)
                pool.wait_ge(sub_inv, l + 1)
                scale_rows(nc.gpsimd, link, z, DQ, 4, HD, nq, ss, "sub")
                pool.drain().then_inc(sub_prepared, 1)
                c0 += NZ
                with pool.Fori(1, KT) as m:
                    for b in range(4):
                        low(m * 4 + (c0 + b), WMAX, b)
                c0 += NP4
                for j in range(NO):
                    low(c0 + j, KT * P, j % SLOTS)
                c0 += NO
                with pool.Fori(0, 4) as q:
                    for j in range(16):
                        low(q * 16 + (c0 + j), KT * P, j % SLOTS)

        def residual(l, part, m, sg, p):
            for i, (t0, tn) in enumerate(sg):
                ins = nc.vector.scalar_tensor_tensor(
                    x_sb[:, m, t0:t0 + tn], ps[:, 3 * p + 2 * i, 0:tn], mod[:, l, part * KT + m, i:i + 1],
                    x_sb[:, m, t0:t0 + tn], ALU.mult, ALU.add)
            ins.then_inc(bank_free, 1)

        @block.scalar
        def _(act):
            chain = [0]

            def link(ins):
                chain[0] += 1
                ins.then_inc(act_step, 1)
                act.wait_ge(act_step, chain[0])

            def high(c, width, k, first=False):
                act.wait_ge(w_in[k % 2], (c // 2) * 16 + 16 if isinstance(c, int) else c * 8 + (16 - 8 * (k % 2)))
                if not first:
                    act.wait_ge(w_used, c - 3)
                nc.scalar.activation(w_hi[:, k, 0:width], w_raw[:, k % 2, 0:width], ACT.Copy).then_inc(w_rounded, 1)

            def square(f, kt, tt):
                if kt >= 3:
                    act.wait_ge(sq_added, stat_base(f)[1] + kt - 2)
                nc.scalar.activation(n_a[:, kt % 2, 0:tt] if kt else rstd[:, 0:tt], x_sb[:, kt, 0:tt],
                                     ACT.Square).then_inc(sq_ready, 1)

            def roots_of_sums(f, sg):
                act.wait_ge(ssq_done, f + 1)
                for i, (t0, tn) in enumerate(sg):
                    nc.scalar.activation(rstd[:, t0:t0 + tn], ps[:, i, 0:tn], ACT.Sqrt, bias=eps_sb[:, 0:1],
                                         scale=1.0 / D).then_inc(std_ready, 1)

            def norm(l, which, dst, sg):
                n = norm_no["act"]
                for kt in range(KT):
                    act.wait_ge(normed, n * KT + kt + 1)
                    for v, (t0, tn) in enumerate(sg):
                        ins = nc.scalar.activation(dst[:, 0, kt, t0:t0 + tn], n_b[:, kt % 4, t0:t0 + tn], ACT.Identity,
                                                   bias=mod[:, l, (3 * which) * KT + kt, v:v + 1])
                    ins.then_inc(modded, 1)
                norm_no["act"] += 1

            act.wait_ge(const_in, 16 * 4)
            nc.scalar.activation(csig[:], c_sb[:], ACT.Sigmoid).then_inc(c_sig, 1)
            act.wait_ge(x_in, 16)
            for kt in range(KT):
                square(0, kt, T)
            roots_of_sums(0, both)
            for c in range(SLOTS):
                high(c, 2 * ZG, c, first=True)
            barrier(act, "act")

            for l in range(DEPTH):
                sg, c0 = segs(l), CH0(l)
                for dst, src in ((small, a["small"][l:l + 1, :].to_broadcast([P, SM])), (rope_sb, a["rope"]),
                                 (uq_sb, a["uq"][l]), (ukv_sb, a["ukv"][l])):
                    act.dma_start(dst[:], src).then_inc(late_in, 16)
                if l:
                    roots_of_sums(2 * l, both)
                norm(l, 0, act1, both)
                def roots(k):
                    act.wait_ge(ss_ready, l * NB + k + 1)
                    for p in (p for p in PREP if p[7] == k):
                        s0 = ss_off[p[0]]
                        s1 = s0 + (ntq(l) if p[5] else NT) * p[2]
                        ins = nc.scalar.activation(ss_z[:, s0:s1], ss_z[:, s0:s1], ACT.Sqrt)
                    ins.then_inc(rt_ready, 1)

                for g in range(5):
                    n = zt(l, g)
                    for tt in range(n):
                        if tt == 2 and g in (2, 4):
                            roots(g // 2 - 1)
                        if tt == n - 2:
                            for i in range(4 if g < 4 else 2):
                                cc = 4 * g + 4 + i
                                high(c0 + cc, 2 * ZG if cc < NZ else WMAX, cc % SLOTS)
                        k = zbase(l, g) + tt
                        act.wait_ge(z_prod, k + 1)
                        nc.scalar.activation(z[:, tt, g * ZG:(g + 1) * ZG], ps[:, k % ZBANKS, 0:ZG],
                                             ACT.Copy).then_inc(z_copied, 1)
                act.wait_ge(lam_s, l + 1)
                nc.scalar.activation(lam_t[:, 2:4], lam_t[:, 0:2], ACT.Exp).then_inc(lam_e, 1)

                def copy_pieces(todo, base):
                    for i, (src, col, w, n, dsts) in enumerate(todo):
                        if i % 2 == 0:
                            continue
                        act.wait_ge(piece_t, base + i + 1)
                        piece = flat[0:w, S_BANK[1] * 512:S_BANK[1] * 512 + n * P]
                        for dst, keep in dsts:
                            ins = nc.scalar.activation(dst[:, 0:n * P], piece, ACT.Copy,
                                                       scale=1.0 if keep is None else keep)
                        ins.then_inc(piece_a, 1)

                copy_pieces(up_pieces(l), piece_base(l, "up"))
                high(c0 + NZ + 2, WMAX, 2)
                act.dma_start(na_T[:], a["na_rows"][l].rearrange("h p n -> p h n")).then_inc(na_in, 16)
                act.wait_ge(up_done, n_up(l))
                act.dma_start(na_mask[:], a["na_mask"]).then_inc(na_in, 16)
                copy_pieces(pieces(l, "na"), piece_base(l, "na"))
                high(c0 + NZ + 3, WMAX, 3)
                for b in BR:
                    ub, mb = unit_base(l, b)
                    us = units[l][b]

                    def exps(u):
                        h, t = us[u]
                        kts = key_tiles(b, t)
                        if ub + u >= 2:
                            act.wait_ge(pt_ready, ub + u - 1)
                        for mp in range(nmaps[b]):
                            m = u * nmaps[b] + mp
                            act.wait_ge(max_ready, mb + m + 1)
                            dst = (Pq if mp else Pp)[u % 2]
                            s = flat[:, S_BANK[m % 2] * 512:S_BANK[m % 2] * 512 + T]
                            e = (ub + u) % 8
                            W = P * len(kts)
                            if b == "na" and t < NTL:
                                L = W - C
                                nc.scalar.activation(dst[:, 0:L], dst[:, 0:L], ACT.Exp, bias=nmax[:, e, 0, 0:1],
                                                     accum_out=rsum[:, e, 0, 0:1])
                                nc.scalar.activation(dst[:, L:W], s[:, 512:512 + C], ACT.Exp, bias=nmax[:, e, 0, 0:1],
                                                     accum_out=rsum[:, e, 0, 1:2]).then_inc(exp_done, 1)
                            else:
                                nc.scalar.activation(dst[:, 0:W], s[:, 0:W], ACT.Exp, bias=nmax[:, e, mp, 0:1],
                                                     accum_out=rsum[:, e, mp, 0:1]).then_inc(exp_done, 1)

                    def pt_copy(u):
                        W = P * len(key_tiles(b, us[u][1]))
                        act.wait_ge(pt_ready, ub + u + 1)
                        if ub + u >= 2:
                            act.wait_ge(o_ready, ub + u - 1)
                        nc.scalar.activation(PTs[:, u % 2, 0:W], flat[:, PT_BANK * 512:PT_BANK * 512 + W],
                                             ACT.Copy).then_inc(pt_copied, 1)

                    exps(0)
                    for u in range(len(us)):
                        if u + 1 < len(us) and is_diff(b):
                            exps(u + 1)
                        pt_copy(u)
                        if u + 1 < len(us) and not is_diff(b):
                            exps(u + 1)
                        if u == ROOT_UNIT[l] and b == "na":
                            act.wait_ge(lat_sums, l + 1)
                            for s0, s1 in ((0, 4 * ntq(l)), (24, 60)):
                                ins = nc.scalar.activation(ss_m[:, s0:s1], ss_m[:, s0:s1], ACT.Sqrt)
                            ins.then_inc(lat_roots, 1)
                        if u == ROOT_UNIT[l] and b == "gqa":
                            act.wait_ge(sub_sums, l + 1)
                            nc.scalar.activation(ss_z[:, 0:4 * ntq(l)], ss_z[:, 0:4 * ntq(l)], ACT.Sqrt).then_inc(sub_roots, 1)
                    if b != BR[-1]:
                        nb = BR[BR.index(b) + 1]
                        copy_pieces(pieces(l, nb), piece_base(l, nb))
                for i in range(8):
                    act.wait_ge(ot_ready, l * 8 + i + 1)
                    tn = ntq(l) * P
                    src = flat[:, (i % 3) * 1024:(i % 3) * 1024 + tn]
                    nc.scalar.activation(act1[:, 0, i, 0:tn], src, ACT.Copy).then_inc(ot_hi, 1)
                barrier(act, "act")
                norm(l, 0, act0, sg)
                cb = c0 + NZ
                ada_on = l == 0
                if ada_on:
                    for n in range(2):
                        act.dma_start(ada_w[:, n, :], a["w_ada"][ADA0 + n]).then_inc(ada_in[n], 16)

                def reload_ada(m, pair):
                    act.wait_ge(ada_summed, m * 2 + (2 + pair + 1))
                    for i in range(2):
                        act.dma_start(ada_w[:, i, :], a["w_ada"][m * 4 + (ADA0 + 2 * (pair + 1) + i)]).then_inc(ada_in[i], 16)

                def gates(m, first):
                    for bb in range(4):
                        act.wait_ge(w_used, m * 4 + (cb + bb + 1))
                        p = bb % 2
                        for i, (t0, tn) in enumerate(sg):
                            ins = nc.scalar.activation(sig[:, p, t0:t0 + tn],
                                                       ps[:, 3 * p, 0:tn] if i == 0 else ps[:, 3 * p + 2, 0:tn], ACT.Sigmoid)
                        ins.then_inc(sig_ready, 1)
                        high(m * 4 + (cb + bb + 4), WMAX, bb)
                        if ada_on and bb == (2 if first else 1):
                            reload_ada(m, 0)
                        if ada_on and bb == 3:
                            reload_ada(m, 1)

                gates(0, True)
                with act.Fori(1, KT) as m:
                    gates(m, False)
                barrier(act, "act")
                tt = sg[-1][0] + sg[-1][1]
                for kt in range(KT):
                    nc.scalar.activation(act0[:, 0, kt, 0:tt], y_sb[:, kt, 0:tt], ACT.Copy).then_inc(y_hi, 1)
                cb += NP4
                act.wait_ge(y_ready, (l + 1) * KT)
                for j in range(NO):
                    high(cb + j + 4, KT * P, j % SLOTS)
                    act.wait_ge(bank_free, 2 + l * NSTEP + NP4 + j + 1)
                    square(2 * l + 1, j, tt)
                barrier(act, "act")
                roots_of_sums(2 * l + 1, sg)
                norm(l, 1, act1, sg)
                cb += NO

                def quarter(q, last):
                    for j in range(16):
                        c = q * 16 + (cb + j)
                        act.wait_ge(w_used, c + 1)
                        if j < 8:
                            p = j % 2
                            for i, (t0, tn) in enumerate(sg):
                                ins = nc.scalar.activation(r_sb[:, p, t0:t0 + tn],
                                                           ps[:, 3 * p + 2 * i, 0:tn], ACT.Relu)
                            ins.then_inc(relu_ready, 1)
                            act.wait_ge(relu_ready, q * 8 + (l * 32 + j + 1))
                            nc.scalar.activation(act0[:, 0, j, 0:tt], r_sb[:, p, 0:tt], ACT.Square).then_inc(a_hi, 1)
                        if not last:
                            high(c + 4, KT * P, j % SLOTS)
                        elif j < 12:
                            high(c + 4, KT * P, j % SLOTS)
                        elif l + 1 < DEPTH:
                            high(c + 4, 2 * ZG, j % SLOTS)
                        if last and j >= 8 and l + 1 < DEPTH:
                            act.wait_ge(bank_free, 2 + l * NSTEP + NP4 + NO + 16 * q + j + 1)
                            square(2 * l + 2, j - 8, tt)
                        if ada_on and j - 1 in ADA_STEPS and not (last and j - 1 == ADA_STEPS[-1]):
                            n = ADA_STEPS.index(j - 1)
                            act.wait_ge(ada_summed, q * 6 + (2 + NP4 // 2 + n + 1))
                            for i in range(2):
                                act.dma_start(ada_w[:, i, :], a["w_ada"][q * 12 + (ADAN + 2 * n + 2 + i)]).then_inc(ada_in[i], 16)

                with act.Fori(0, 3) as q:
                    quarter(q, False)
                quarter(3, True)
                barrier(act, "act")

        @block.vector
        def _(dve):
            chain = [0]

            def link(ins):
                chain[0] += 1
                ins.then_inc(dve_step, 1)
                dve.wait_ge(dve_step, chain[0])

            tt_op = nc.vector.tensor_tensor

            def row_products(w, acc, n, count):
                for kt in range(KT):
                    for v in range(2):
                        o = acc[:, v, :].rearrange("p (n c) -> p n c", c=P)
                        wk = w[:, 0:n, kt * P:(kt + 1) * P]
                        if kt == 0:
                            ins = nc.vector.tensor_scalar(o, wk, csilu[:, kt, v:v + 1], None, ALU.mult)
                        else:
                            dve.wait_ge(ada_step, count + (2 * kt + v - 1))
                            ins = nc.vector.scalar_tensor_tensor(o, wk, csilu[:, kt, v:v + 1], o, ALU.mult, ALU.add)
                        ins.then_inc(ada_summed if (kt, v) == (KT - 1, 1) else ada_step, 1)

            def take_mod(l, j0, j1):
                src = ada_ps[:, l * 2 * ADAN + 2 * j0:l * 2 * ADAN + 2 * j1].rearrange("p (j v) -> p j v", v=2)
                link(tt_op(mod[:, l, j0:j1, :], src, b_sb[:, l, j0:j1].unsqueeze(2).to_broadcast([P, j1 - j0, 2]), ALU.add))

            def take_scale(l, which):
                j0 = (3 * which + 1) * KT
                link(nc.vector.tensor_scalar(nscale[:, l, which, :, :], mod[:, l, j0:j0 + KT, :], 1.0, None, ALU.add))
                link(tt_op(nscale[:, l, which, :, :], nscale[:, l, which, :, :],
                           gn_sb[:, l, which, :].unsqueeze(2).to_broadcast([P, KT, 2]), ALU.mult))

            def add_square(f, kt, tt):
                r, a_ = stat_base(f)
                dve.wait_ge(sq_ready, r + kt + 1)
                if kt >= 2:
                    dve.wait_ge(sq_added, a_ + kt - 1)
                tt_op(rstd[:, 0:tt], rstd[:, 0:tt], n_a[:, kt % 2, 0:tt], ALU.add).then_inc(sq_added, 1)

            def inverse_roots(f, tt):
                dve.wait_ge(std_ready, 2 * f + 2 if tt == T else 2 * f + 1)
                link(nc.vector.reciprocal(rstd[:, 0:tt], rstd[:, 0:tt]))

            def norm(l, which, dst, sg):
                n = norm_no["dve"]
                tt = sg[-1][0] + sg[-1][1]

                def times(kt):
                    if kt >= 4:
                        dve.wait_ge(h_ready, n * KT + kt - 3)
                    for v, (t0, tn) in enumerate(sg):
                        ins = nc.vector.scalar_tensor_tensor(
                            n_b[:, kt % 4, t0:t0 + tn], x_sb[:, kt, t0:t0 + tn], nscale[:, l, which, kt, v:v + 1],
                            rstd[:, t0:t0 + tn], ALU.mult, ALU.mult)
                    ins.then_inc(normed, 1)

                times(0)
                for kt in range(KT):
                    if kt + 1 < KT:
                        times(kt + 1)
                    dve.wait_ge(modded, n * KT + kt + 1)
                    for v, (t0, tn) in enumerate(sg):
                        ins = nc.vector.scalar_tensor_tensor(
                            dst[:, 1, kt, t0:t0 + tn], n_b[:, kt % 4, t0:t0 + tn], mod[:, l, (3 * which) * KT + kt, v:v + 1],
                            dst[:, 0, kt, t0:t0 + tn].bitcast(f32), ALU.add, ALU.subtract)
                    ins.then_inc(h_ready, 1)
                norm_no["dve"] += 1

            def sums(src, c0, heads, d, nt, tmp, ss):
                v = src[:, 0:nt, c0:c0 + heads * d]
                w = tmp[:, 0:nt, 0:heads * d]
                link(tt_op(w, v, v, ALU.mult))
                link(nc.vector.tensor_reduce(ss, w.rearrange("p t (h d) -> p t h d", d=d), AX.X, ALU.add))
                return nc.vector.tensor_scalar(ss, ss, 1.0 / d, EPS, ALU.mult, ALU.add)

            def inverse(ss, mul):
                link(nc.vector.reciprocal(ss, ss))
                if mul != 1.0:
                    link(nc.vector.tensor_scalar(ss, ss, mul, None, ALU.mult))

            nc.vector.memset(ones[:], 1.0)
            link(nc.vector.memset(row_mask[:], 0.0))
            for i in range(2):
                nc.vector.memset(row_mask[64 * i:64 * i + 64, i:i + 1], 1.0)
            for i in range(4):
                nc.vector.memset(row_mask[32 * i:32 * i + 32, 2 + i:3 + i], 1.0)
            ins = nc.vector.memset(eps_sb[:], EPS)
            link(ins)
            dve.drain().then_inc(bank_free, 2)
            dve.wait_ge(c_sig, 1)
            dve.wait_ge(const_in, 16 * 4)
            tt_op(csilu[:], c_sb[:], csig[:], ALU.mult).then_inc(c_ready, 1)
            dve.wait_ge(c_ready, 1)
            for j in range(2):
                dve.wait_ge(ada_first[2 + j], 16)
                row_products(ada_init[:, 8 + 4 * j:12 + 4 * j, :], ada_acc0[:, :, j * 512:(j + 1) * 512], 4, 15 * j)
            for kt in range(1, KT):
                add_square(0, kt, T)
            inverse_roots(0, T)
            dve.wait_ge(pe_phase, 1)
            take_mod(0, 0, ADA0)
            take_scale(0, 0)
            barrier(dve, "dve")

            for l in range(DEPTH):
                sg, c0 = segs(l), CH0(l)
                lam_init = 0.8 - 0.6 * math.exp(-0.3 * l)
                if l:
                    inverse_roots(2 * l, T)
                norm(l, 0, act1, both)
                dve.wait_ge(late_in, 16 * 4 * (l + 1))

                def copy_pieces(todo, base, i0, i1):
                    for i in range(i0, min(i1, len(todo)), 2):
                        src, col, w, n, dsts = todo[i]
                        dve.wait_ge(piece_t, base + i + 1)
                        piece = flat[0:w, S_BANK[0] * 512:S_BANK[0] * 512 + n * P]
                        for dst, keep in dsts:
                            if keep is None:
                                ins = nc.vector.tensor_copy(dst[:, 0:n * P], piece)
                            else:
                                ins = nc.vector.tensor_scalar(dst[:, 0:n * P], piece, keep, None, ALU.mult)
                        ins.then_inc(piece_c, 1)

                for k in range(NB):
                    g = ready_group[k]
                    dve.wait_ge(z_copied, zbase(l, g) + zt(l, g))
                    group = [p for p in PREP if p[7] == k]
                    for p in group:
                        nt = ntq(l) if p[5] else NT
                        ss = ss_z[:, ss_off[p[0]]:ss_off[p[0]] + nt * p[2]].rearrange("p (t h) -> p t h", h=p[2])
                        ins = sums(z, p[1], p[2], p[3], nt, tmp_z[0], ss)
                        if p is group[-1]:
                            ins.then_inc(ss_ready, 1)
                        else:
                            link(ins)
                    dve.wait_ge(rt_ready, l * NB + k + 1)
                    for p in group:
                        nt = ntq(l) if p[5] else NT
                        ss = ss_z[:, ss_off[p[0]]:ss_off[p[0]] + nt * p[2]].rearrange("p (t h) -> p t h", h=p[2])
                        mul = {"naq": HD ** -0.5, "dq": DD ** -0.5, "gq": HD ** -0.5}.get(p[0], 1.0)
                        inverse(ss, mul)
                        scale_rows(nc.vector, link, z, p[1], p[2], p[3], nt, ss, p[4])
                        if p[6]:
                            rope(nc.vector, link, z, p[1], p[2], p[3], p[3], 0 if p[6] == 64 else 128,
                                 tmp_z[1][:, 0:NTL, 0:p[2] * p[3]])
                dve.drain().then_inc(rows_prepared, 1)
                for i, (u, v) in enumerate((("lq1", "lk1"), ("lq2", "lk2"))):
                    u, v = GO[u][0], GO[v][0]
                    link(tt_op(lam_p[:, i, :], small[:, u:u + DD], small[:, v:v + DD], ALU.mult))
                    ins = nc.vector.tensor_reduce(lam_t[:, i:i + 1], lam_p[:, i, :], AX.X, ALU.add)
                ins.then_inc(lam_s, 1)
                copy_pieces(up_pieces(l), piece_base(l, "up"), 0, 3)
                for i in range(len(up_list(l))):
                    kind, t = up_list(l)[i]
                    dve.wait_ge(up_done, up_base(l) + i + 1)
                    bank = 4 + i % 2
                    if kind == "q":
                        nc.vector.tensor_copy(mlaq[:, t, :], ps[:, bank, 0:384]).then_inc(up_copied, 1)
                    else:
                        nc.vector.tensor_copy(mlak[:, t, :].rearrange("p (h d) -> p h d", d=QK)[:, :, 0:NOPE],
                                              ps[:, bank, 0:256].rearrange("p (h d) -> p h d", d=NOPE))
                        nc.vector.tensor_copy(mlak[:, t, :].rearrange("p (h d) -> p h d", d=QK)[:, :, NOPE:QK],
                                              z[:, t, KR:KR + RD].unsqueeze(1).to_broadcast([P, NH, RD]))
                        nc.vector.tensor_copy(mlav[:, t, :], ps[:, bank, 256:512]).then_inc(up_copied, 1)
                dve.wait_ge(lam_e, l + 1)
                link(tt_op(neglam[:], lam_t[:, 3:4], lam_t[:, 2:3], ALU.subtract))
                link(nc.vector.tensor_scalar(neglam[:], neglam[:], -lam_init, None, ALU.add))
                copy_pieces(pieces(l, "na"), piece_base(l, "na"), 0, 4)
                dve.wait_ge(na_in, 32 * (l + 1))
                for b in BR:
                    ub, mb = unit_base(l, b)
                    us = units[l][b]

                    def maxima(u):
                        h, t = us[u]
                        kts = key_tiles(b, t)
                        W = P * len(kts)
                        e = (ub + u) % 8
                        if b == "na" and t == 0:
                            for (o, w), s0 in zip(NA_TAB, NA_SRC):
                                ins = tt_op(na_tab[:, o:o + w], na_T[:, h, s0:s0 + w], na_mask[:, o:o + w], ALU.add)
                            link(ins)
                        for mp in range(nmaps[b]):
                            m = u * nmaps[b] + mp
                            dve.wait_ge(s_ready, mb + m + 1)
                            s = flat[:, S_BANK[m % 2] * 512:S_BANK[m % 2] * 512 + T]
                            if b == "na" and t < NTL:
                                L = W - C
                                o, w = NA_TAB[NA_KIND[t]]
                                if ub + u >= 2:
                                    dve.wait_ge(pt_ready, ub + u - 1)
                                link(nc.vector.tensor_tensor_reduce(
                                    out=Pp[u % 2][:, 0:L], in0=s[:, 0:L], in1=na_tab[:, o:o + w], scale=1.0,
                                    scalar=NEG, op0=ALU.add, op1=ALU.max, accum_out=nmax[:, e, 1, 0:1]))
                                link(nc.vector.tensor_reduce(nmax[:, e, 1, 1:2], s[:, 512:512 + C], AX.X, ALU.max, negate=True))
                                nc.vector.scalar_tensor_tensor(nmax[:, e, 0, 0:1], nmax[:, e, 1, 0:1], -1.0,
                                                               nmax[:, e, 1, 1:2], ALU.mult, ALU.min).then_inc(max_ready, 1)
                            else:
                                nc.vector.tensor_reduce(nmax[:, e, mp, 0:1], s[:, 0:W], AX.X, ALU.max,
                                                        negate=True).then_inc(max_ready, 1)

                    def combine(u):
                        e = (ub + u) % 8
                        W = P * len(key_tiles(b, us[u][1]))
                        dve.wait_ge(exp_done, mb + 2 * u + 2)
                        link(nc.vector.reciprocal(rinv[:, e, :], rsum[:, e, :, 0]))
                        link(nc.vector.scalar_tensor_tensor(rinv[:, e, 1:2], rinv[:, e, 1:2], neglam[:, 0:1],
                                                            rsum[:, e, 0, 0:1], ALU.mult, ALU.mult))
                        nc.vector.scalar_tensor_tensor(Pp[u % 2][:, 0:W], Pq[u % 2][:, 0:W], rinv[:, e, 1:2],
                                                       Pp[u % 2][:, 0:W], ALU.mult, ALU.add).then_inc(diff_done, 1)

                    def outputs(u):
                        h, t = us[u]
                        e = (ub + u) % 8
                        if not is_diff(b):
                            dve.wait_ge(exp_done, mb + u + 1)
                            if b == "na" and t < NTL:
                                link(tt_op(rsum[:, e, 0, 0:1], rsum[:, e, 0, 0:1], rsum[:, e, 0, 1:2], ALU.add))
                            link(nc.vector.reciprocal(rinv[:, e, 0:1], rsum[:, e, 0, 0:1]))
                        dve.wait_ge(o_ready, ub + u + 1)
                        nc.vector.tensor_scalar(o_dest(b, h, t), ps[:, O_BANK + u % 2, 0:HD],
                                                rinv[:, e, 0:1], None, ALU.mult).then_inc(o_done, 1)

                    nb = BR[BR.index(b) + 1] if b != BR[-1] else None
                    maxima(0)
                    if is_diff(b):
                        combine(0)
                    for u in range(len(us)):
                        if u + 1 < len(us):
                            maxima(u + 1)
                        else:
                            if nb:
                                copy_pieces(pieces(l, nb), piece_base(l, nb), 0, 2)
                        if u >= 1:
                            outputs(u - 1)
                        if is_diff(b) and u + 1 < len(us):
                            combine(u + 1)
                        if u == ROOT_UNIT[l] + 1 and b == "na":
                            dve.wait_ge(lat_roots, l + 1)
                            link(nc.vector.reciprocal(ss_m[:, 0:4 * ntq(l)], ss_m[:, 0:4 * ntq(l)]))
                            link(nc.vector.tensor_scalar(ss_m[:, 0:4 * ntq(l)], ss_m[:, 0:4 * ntq(l)], QK ** -0.5, None, ALU.mult))
                            nc.vector.reciprocal(ss_m[:, 24:60], ss_m[:, 24:60]).then_inc(lat_inv, 1)
                        if u == ROOT_UNIT[l] + 1 and b == "gqa":
                            dve.wait_ge(sub_roots, l + 1)
                            link(nc.vector.reciprocal(ss_z[:, 0:4 * ntq(l)], ss_z[:, 0:4 * ntq(l)]))
                            nc.vector.tensor_scalar(ss_z[:, 0:4 * ntq(l)], ss_z[:, 0:4 * ntq(l)], 1.0 - lam_init, None,
                                                    ALU.mult).then_inc(sub_inv, 1)
                    if nb:
                        copy_pieces(pieces(l, nb), piece_base(l, nb), 2, PIECES[nb])
                    outputs(len(us) - 1)
                for i in range(8):
                    dve.wait_ge(ot_hi, l * 8 + i + 1)
                    tn = ntq(l) * P
                    src = flat[:, (i % 3) * 1024:(i % 3) * 1024 + tn]
                    tt_op(act1[:, 1, i, 0:tn], src, act1[:, 0, i, 0:tn].bitcast(f32), ALU.subtract).then_inc(ot_lo, 1)
                barrier(dve, "dve")
                norm(l, 0, act0, sg)
                fb = 2 + l * NSTEP
                tt = sg[-1][0] + sg[-1][1]

                def gate(m, first):
                    for bb in range(4):
                        p = bb % 2
                        dve.wait_ge(sig_ready, m * 4 + (l * NP4 + bb + 1))
                        for i, (t0, tn) in enumerate(sg):
                            src = ps[:, 3 * p + 1, 0:tn] if i == 0 else ps[:, 3 * p + 2, C:2 * C]
                            dst = y_sb[:, m, t0:t0 + tn] if bb == 0 else sig[:, p, t0:t0 + tn]
                            ins = tt_op(dst, sig[:, p, t0:t0 + tn], src, ALU.mult)
                        if bb:
                            ins.then_inc(gated, 1)
                            dve.wait_ge(gated, m * 3 + (l * 24 + bb))
                            ins = tt_op(y_sb[:, m, 0:tt], y_sb[:, m, 0:tt], sig[:, p, 0:tt], ALU.add)
                        ins.then_inc(bank_free, 1)
                        dve.wait_ge(bank_free, m * 4 + (fb + bb + 1))
                        if l == 0 and bb in ((1, 2) if first else (0, 2)):
                            for i in range(2):
                                dve.wait_ge(ada_in[i], m * 32 + 16 * (bb // 2 + 1))
                            dve.wait_ge(ada_used, m * 2 + bb // 2)
                            row_products(ada_w, ada_acc, 2, m * 30 + (30 + 15 * (bb // 2)))

                gate(0, True)
                with dve.Fori(1, KT) as m:
                    gate(m, False)
                if l == 0:
                    dve.wait_ge(ada_used, NP4 // 2)
                    take_mod(0, ADA0, ADAN)
                    take_scale(0, 1)
                barrier(dve, "dve")
                fb += NP4
                for kt in range(KT):
                    dve.wait_ge(y_hi, l * KT + kt + 1)
                    tt_op(act0[:, 1, kt, 0:tt], y_sb[:, kt, 0:tt], act0[:, 0, kt, 0:tt].bitcast(f32),
                          ALU.subtract).then_inc(y_ready, 1)
                for j in range(NO):
                    dve.wait_ge(w_used, c0 + NZ + NP4 + j + 1)
                    residual(l, 2, j, sg, j % 2)
                    if j >= 2:
                        add_square(2 * l + 1, j - 1, tt)
                add_square(2 * l + 1, KT - 1, tt)
                fb += NO
                barrier(dve, "dve")
                inverse_roots(2 * l + 1, tt)
                norm(l, 1, act1, sg)
                cb = c0 + NZ + NP4 + NO

                def quarter(q, last):
                    for j in range(16):
                        if j < 8:
                            dve.wait_ge(a_hi, q * 8 + (l * 32 + j + 1))
                            tt_op(q_sb[:, j % 2, 0:tt], r_sb[:, j % 2, 0:tt], r_sb[:, j % 2, 0:tt], ALU.mult).then_inc(bank_free, 1)
                            dve.wait_ge(bank_free, q * 16 + (fb + j + 1))
                            tt_op(act0[:, 1, j, 0:tt], q_sb[:, j % 2, 0:tt], act0[:, 0, j, 0:tt].bitcast(f32),
                                  ALU.subtract).then_inc(a_ready, 1)
                        else:
                            dve.wait_ge(w_used, q * 16 + (cb + j + 1))
                            residual(l, 5, j - 8, sg, j % 2)
                            dve.wait_ge(bank_free, q * 16 + (fb + j + 1))
                        if l == 0 and j in ADA_STEPS:
                            n = ADA_STEPS.index(j)
                            for i in range(2):
                                dve.wait_ge(ada_in[i], q * 96 + 16 * (NP4 // 2 + n + 1))
                            dve.wait_ge(ada_used, q * 6 + (NP4 // 2 + n))
                            row_products(ada_w, ada_acc, 2, q * 90 + (30 + 15 * (NP4 // 2) + 15 * n))
                        if last and j >= 10:
                            add_square(2 * l + 2, j - 9, tt)

                if l + 1 < DEPTH:
                    with dve.Fori(0, 3) as q:
                        quarter(q, False)
                    quarter(3, True)
                    add_square(2 * l + 2, KT - 1, tt)
                else:
                    with dve.Fori(0, 4) as q:
                        quarter(q, False)
                if l == 0:
                    dve.wait_ge(ada_used, (NP4 + ADAN) // 2)
                    take_mod(1, 0, ADAN)
                    take_scale(1, 0)
                    take_scale(1, 1)
                barrier(dve, "dve")

        @block.tensor
        def _(pe):
            mm, tr = nc.tensor.matmul, nc.tensor.transpose

            def sum_squares(f, sg):
                pe.wait_ge(sq_ready, stat_base(f + 1)[0])
                pe.wait_ge(sq_added, stat_base(f + 1)[1])
                for i, (t0, tn) in enumerate(sg):
                    ins = mm(ps[:, i, 0:tn], ones[:], rstd[:, t0:t0 + tn], start=True, stop=True)
                ins.then_inc(ssq_done, 1)

            def chunk_products(outs, slot, kts, act_t, act_kt, sg, before=None):
                for i, kt in enumerate(kts):
                    if before:
                        before(i)
                    for n, (w, h) in enumerate(((w_hi, 0), (w_hi, 1), (w_lo, 0))):
                        for o, (t0, tn) in zip(outs, sg):
                            ins = mm(o[:, 0:tn], w[:, slot, kt * P:kt * P + P], act_t[:, h, act_kt + i, t0:t0 + tn],
                                     start=i == 0 and n == 0, stop=i == len(kts) - 1 and n == 2)
                return ins

            def column_sums(acc, n, col):
                for i in range(n):
                    for v in range(2):
                        ins = mm(col(2 * i + v), acc[:, v, i * P:(i + 1) * P], ones[:, 0:1], start=True, stop=True)
                return ins

            pe.wait_ge(const_in, 16 * 4)
            pe.wait_ge(c_ready, 1)
            for j in range(KT):
                if j == 4:
                    pe.wait_ge(ada_summed, 2)
                    column_sums(ada_acc0, KT, lambda i: ada_ps[:, 2 * KT + i:2 * KT + i + 1])
                    sum_squares(0, both)
                if j % 4 == 0:
                    pe.wait_ge(ada_first[j // 4], 16)
                for kt in range(KT):
                    mm(ada_ps[:, 2 * j:2 * j + 2], ada_init[:, j, kt * P:kt * P + P], csilu[:, kt, :],
                       start=kt == 0, stop=kt == KT - 1)
            barrier(pe, "pe")

            for l in range(DEPTH):
                sg, c0 = segs(l), CH0(l)
                if l:
                    sum_squares(2 * l, both)
                pe.wait_ge(std_ready, std_seen(l))
                for g in range(5):
                    n = zt(l, g)
                    step = n if g == 0 else 2
                    for tt in range(0, n, step):
                        tiles = range(tt, tt + step)
                        if zbase(l, g) + tt + step > ZBANKS:
                            pe.wait_ge(z_copied, zbase(l, g) + tt + step - ZBANKS)
                        for kt in range(KT):
                            if tt == 0 and kt % 2 == 0:
                                pe.wait_ge(w_ready, c0 + 4 * g + kt // 2 + 1)
                            if g == 0 and tt == 0:
                                pe.wait_ge(h_ready, h_base(l) + kt + 1)
                            slot, w0 = (4 * g + kt // 2) % SLOTS, (kt % 2) * ZG
                            for ti in tiles:
                                k = zbase(l, g) + ti
                                for i, (h, w) in enumerate(((0, w_hi), (1, w_hi), (0, w_lo))):
                                    ins = mm(ps[:, k % ZBANKS, 0:ZG], act1[:, h, kt, ti * P:ti * P + P], w[:, slot, w0:w0 + ZG],
                                             start=kt == 0 and i == 0, stop=kt == KT - 1 and i == 2)
                                if kt == KT - 1:
                                    ins.then_inc(z_prod, 1)
                            if tt == n - step and kt % 2 == 1:
                                if kt < KT - 1:
                                    ins.then_inc(w_used, 1)
                                else:
                                    pe.drain().then_inc(w_used, 1)
                def transpose_piece(i, piece, base, maps):
                    src, col, w, n, _ = piece
                    if i < 2:
                        if maps:
                            pe.wait_ge(exp_done, maps - 1 + i)
                    elif i % 2:
                        pe.wait_ge(piece_a, base[1] + i // 2)
                    else:
                        pe.wait_ge(piece_c, base[0] + i // 2)
                    for t in range(n):
                        c_ = S_BANK[i % 2] * 512 + t * P
                        ins = tr(flat[0:w, c_:c_ + P], src[:, t, col:col + w], ident[:])
                    ins.then_inc(piece_t, 1)

                def bases(b):
                    return piece_base(l, b, 0), piece_base(l, b, 1)

                def wait_pieces(b):
                    pe.wait_ge(piece_c, bases(b)[0] + (PIECES[b] + 1) // 2)
                    pe.wait_ge(piece_a, bases(b)[1] + PIECES[b] // 2)

                pe.wait_ge(z_copied, zbase(l, 4) + NT)
                pe.wait_ge(rows_prepared, l + 1)
                for i, piece in enumerate(up_pieces(l)):
                    transpose_piece(i, piece, bases("up"), 0)
                wait_pieces("up")
                for i, (kind, t) in enumerate(up_list(l)):
                    if i >= 2:
                        pe.wait_ge(up_copied, up_base(l) + i - 1)
                    bank = 4 + i % 2
                    if kind == "q":
                        mm(ps[:, bank, 0:384], cT[:, 0, t * P:t * P + P], uq_sb[:, 0, :], start=True, stop=False)
                        ins = mm(ps[:, bank, 0:384], cT[0:64, 1, t * P:t * P + P], uq_sb[0:64, 1, :], start=False, stop=True)
                    else:
                        ins = mm(ps[:, bank, :], cT[:, 2, t * P:t * P + P], ukv_sb[:], start=True, stop=True)
                    ins.then_inc(up_done, 1)
                for i, piece in enumerate(pieces(l, "na")):
                    transpose_piece(i, piece, bases("na"), 0)
                pe.wait_ge(up_copied, n_up(l))
                for b in BR:
                    wait_pieces(b)
                    nb = BR[BR.index(b) + 1] if b != BR[-1] else None
                    ub, mb = unit_base(l, b)
                    us = units[l][b]

                    def scores(u):
                        h, t = us[u]
                        kts = key_tiles(b, t)
                        for mp in range(nmaps[b]):
                            m = u * nmaps[b] + mp
                            if mb + m >= 2:
                                pe.wait_ge(exp_done, mb + m - 1)
                            s = flat[:, S_BANK[m % 2] * 512:S_BANK[m % 2] * 512 + T]
                            q, k = qk_operands(b, h, mp, t)
                            lat = [x for x in kts if x < NTL]
                            if lat:
                                ins = mm(s[:, 0:P * len(lat)], q, k[:, lat[0] * P:(lat[-1] + 1) * P], start=True, stop=True)
                                ins = mm(s[:, S:T], q, k[:, S:T], start=True, stop=True)
                            else:
                                ins = mm(s[:, 0:C], q, k[:, S:T], start=True, stop=True)
                            ins.then_inc(s_ready, 1)

                    def transposes(u):
                        if is_diff(b):
                            pe.wait_ge(diff_done, diff_base(l, b) + u + 1)
                        else:
                            pe.wait_ge(exp_done, mb + u + 1)
                        if ub + u >= 1:
                            pe.wait_ge(pt_copied, ub + u)
                        for j in range(len(key_tiles(b, us[u][1]))):
                            c_ = PT_BANK * 512 + j * P
                            ins = tr(flat[:, c_:c_ + P], Pp[u % 2][:, j * P:j * P + P], ident[:])
                        ins.then_inc(pt_ready, 1)

                    def values(u):
                        h, t = us[u]
                        kts = key_tiles(b, t)
                        pe.wait_ge(pt_copied, ub + u + 1)
                        if ub + u >= 2:
                            pe.wait_ge(o_done, ub + u - 1)
                        for j, kt in enumerate(kts):
                            ins = mm(ps[:, O_BANK + u % 2, 0:HD], PTs[:, u % 2, j * P:j * P + P],
                                     v_slice(b, h, kt), start=j == 0, stop=j == len(kts) - 1)
                        ins.then_inc(o_ready, 1)

                    scores(0)
                    for u in range(len(us)):
                        if u + 1 < len(us):
                            scores(u + 1)
                        if u >= 1:
                            values(u - 1)
                        transposes(u)
                        if u == len(us) - 1 and nb:
                            todo, maps = pieces(l, nb), unit_base(l, nb)[1]
                            if nb == "gqa":
                                pe.wait_ge(lat_prepared, l + 1)
                            for i in range(2):
                                transpose_piece(i, todo[i], bases(nb), maps)
                    if nb:
                        for i in range(2, PIECES[nb]):
                            transpose_piece(i, todo[i], bases(nb), maps)
                    values(len(us) - 1)
                pe.wait_ge(o_done, unit_base(l, BR[-1])[0] + len(units[l][BR[-1]]))
                pe.wait_ge(sub_prepared, l + 1)
                for i in range(8):
                    if i >= 3:
                        pe.wait_ge(ot_lo, l * 8 + i - 2)
                    c_in = (MLO, NAQ, DQ, GQ)[i // 2] + (i % 2) * P
                    for t in range(ntq(l)):
                        c_ = (i % 3) * 1024 + t * P
                        ins = tr(flat[:, c_:c_ + P], z[:, t, c_in:c_in + P], ident[:])
                    ins.then_inc(ot_ready, 1)
                barrier(pe, "pe")
                cb, fb = c0 + NZ, 2 + l * NSTEP

                def two_chunks(c, f, slot, h, which, width):
                    pe.wait_ge(w_ready, c + 2)
                    pe.wait_ge(bank_free, f)
                    for kt in range(KT):
                        pe.wait_ge(h_ready, h_base(l) + which * KT + kt + 1)
                        for p in range(2):
                            for n, (w, half) in enumerate(((w_hi, 0), (w_hi, 1), (w_lo, 0))):
                                for o, (t0, tn) in zip((ps[:, 3 * p, :], ps[:, 3 * p + 2, 0:width]), sg):
                                    ins = mm(o[:, 0:tn], w[:, slot + p, kt * P:kt * P + P], h[:, half, kt, t0:t0 + tn],
                                             start=kt == 0 and n == 0, stop=kt == KT - 1 and n == 2)
                    return ins

                def gated_branches(m, first):
                    for bb in range(4):
                        p = bb % 2
                        if first and bb == 0:
                            pe.wait_ge(w_ready, cb + 2)
                            pe.wait_ge(bank_free, fb)
                            for b2 in range(2):
                                chunk_products([ps[:, 3 * b2 + 1, :], ps[:, 3 * b2 + 2, C:2 * C]], b2, range(8, 10),
                                               act1, 2 * b2, sg)
                            two_chunks(cb, fb, 0, act0, 1, C).then_inc(w_used, 2)
                        elif not (first and bb == 1):
                            pe.wait_ge(w_ready, m * 4 + (cb + bb + 1))
                            pe.wait_ge(bank_free, m * 4 + (fb + bb - 1))
                            chunk_products([ps[:, 3 * p, :], ps[:, 3 * p + 2, 0:C]], bb, range(8), act0, 0, sg)
                            chunk_products([ps[:, 3 * p + 1, :], ps[:, 3 * p + 2, C:2 * C]], bb, range(8, 10), act1, 2 * bb,
                                           sg).then_inc(w_used, 1)
                        if l == 0 and bb == 0 and not first:
                            pair_columns(m, -1)
                        if l == 0 and bb == 2:
                            pair_columns(m, 0)

                def pair_columns(m, pair):
                    pe.wait_ge(ada_summed, m * 2 + (2 + pair + 1))
                    column_sums(ada_acc, 2, lambda i: ada_ps[:, bass.ds(m * 8 + (2 * ADA0 + 4 * pair + i), 1)]
                                ).then_inc(ada_used, 1)

                gated_branches(0, True)
                with pe.Fori(1, KT) as m:
                    gated_branches(m, False)
                if l == 0:
                    pair_columns(KT, -1)
                barrier(pe, "pe")
                cb, fb = cb + NP4, fb + NP4
                for j in range(NO):
                    p = j % 2
                    pe.wait_ge(w_ready, cb + j + 1)
                    pe.wait_ge(bank_free, fb + j - 1)

                    def y_rows(kt):
                        pe.wait_ge(y_ready, l * KT + kt + 1)

                    chunk_products([ps[:, 3 * p, :], ps[:, 3 * p + 2, :]], j % SLOTS, range(8), act0, 0, sg,
                                   y_rows if j == 0 else None).then_inc(w_used, 1)
                barrier(pe, "pe")
                sum_squares(2 * l + 1, sg)
                cb, fb = cb + NO, fb + NO
                def quarter(q, first):
                    for j in range(16):
                        p = j % 2

                        def a_rows(kt):
                            pe.wait_ge(a_ready, q * 8 + (l * 32 + kt + 1))

                        if first and j == 0:
                            two_chunks(cb, fb, 0, act1, 2, C).then_inc(w_used, 2)
                        elif not (first and j == 1):
                            pe.wait_ge(w_ready, q * 16 + (cb + j + 1))
                            pe.wait_ge(bank_free, q * 16 + (fb + j - 1))
                            chunk_products([ps[:, 3 * p, :], ps[:, 3 * p + 2, :]], j % SLOTS, range(8),
                                           act1 if j < 8 else act0, 0, sg, a_rows if j == 8 else None).then_inc(w_used, 1)
                        if l == 0 and j - 2 in ADA_STEPS:
                            n = ADA_STEPS.index(j - 2)
                            pe.wait_ge(ada_summed, q * 6 + (2 + NP4 // 2 + n + 1))
                            column_sums(ada_acc, 2, lambda i: ada_ps[:, bass.ds(q * 24 + (2 * ADAN + 4 * n + i), 1)]
                                        ).then_inc(ada_used, 1)

                quarter(0, True)
                with pe.Fori(1, 4) as q:
                    quarter(q, False)
                barrier(pe, "pe")


def kernel(x, c, ctx, c_ctx, w_ada, b_ada, g_norm1, g_norm2, w_in, g_mla_qa, w_mla_uq, g_mla_kva, w_mla_ukv,
           g_mla_q, g_mla_k, g_na_q, g_na_k, na_rpb, g_diff_q, g_diff_k, diff_lq1, diff_lk1, diff_lq2, diff_lk2,
           g_diff_sub, g_gqa_q, g_gqa_k, w_branch, w_out, w_up, w_down):
    import concourse.bacc as bacc
    from concourse.bass_utils import run_bass_kernel_spmd

    L = DEPTH
    perm = (np.arange(S) % GR) * GW + np.arange(S) // GR
    tokens = np.concatenate([np.asarray(x)[0][perm], np.asarray(ctx)[0]])
    feature = lambda v: np.moveaxis(np.asarray(v).reshape(*v.shape[:-1], -1, P), -1, 0)
    arrays = {"xT": np.ascontiguousarray(feature(tokens).transpose(0, 2, 1)),
              "cT": np.stack([feature(np.asarray(c)[0]), feature(np.asarray(c_ctx))], -1),
              "b_ada": feature(b_ada),
              "gn": np.stack([feature(g_norm1), feature(g_norm2)], 2),
              "ident": np.eye(P, dtype=np.float32)}

    def tiles(w, cols):
        l, k, n = w.shape
        return w.reshape(l, k // P, P, n // cols, cols).transpose(0, 3, 2, 1, 4).reshape(l, n // cols, P, -1)

    w_in = np.asarray(w_in)
    o = np.cumsum([0, QL, KVL, RD, 768, 768, 512]).tolist()
    na, df, gq = o[3], o[4], o[5]
    col = lambda b, n: np.arange(b, b + n)
    gq_cols = np.concatenate([col(gq + HD * h, HD) for h in GQA_ORDER])
    order = np.concatenate([col(o[0], QL), col(na, 256), col(df, 256), gq_cols,
                            col(o[1], KVL), col(o[2], RD), col(na + 256, 512), col(df + 256, 512), col(gq + 256, 256)])
    wz = w_in[:, :, order].reshape(L, KT // 2, 2, P, 5, ZG).transpose(0, 4, 1, 3, 2, 5).reshape(L, NZ, P, 2 * ZG)
    gates = tiles(w_in[:, :, o[6]:], P).reshape(L, 4, KT, P, KT * P).transpose(0, 2, 1, 3, 4)
    wb = np.asarray(w_branch).reshape(L, 4, 2, P, KT, P).transpose(0, 4, 1, 3, 2, 5).reshape(L, KT, 4, P, 2 * P)
    up = tiles(np.asarray(w_up), P).reshape(L, 4, 8, P, KT * P)
    down = np.asarray(w_down).reshape(L, 4, KT, P, KT, P).transpose(0, 1, 4, 3, 2, 5).reshape(L, 4, 8, P, KT * P)
    arrays["w_ada"] = tiles(np.asarray(w_ada), P).reshape(L * ADAN, P, KT * P)
    arrays["wz"] = wz
    arrays["wp"] = np.concatenate([gates, wb], -1).reshape(L * NP4, P, WMAX)
    arrays["wo"] = tiles(np.asarray(w_out), P).reshape(L * NO, P, KT * P)
    arrays["wm"] = np.concatenate([up, down], 2).reshape(L * NM, P, KT * P)
    uq = np.zeros((L, 2 * P, 4 * QK), np.float32)
    uq[:, 0:QL] = w_mla_uq
    arrays["uq"] = uq.reshape(L, 2, P, 4 * QK).transpose(0, 2, 1, 3)
    arrays["ukv"] = np.asarray(w_mla_ukv).reshape(L, KVL, NH, 2, HD).transpose(0, 1, 3, 2, 4).reshape(L, KVL, 512)
    arrays["small"] = np.concatenate([np.asarray(v) for v in (
        g_mla_qa, g_mla_kva, g_mla_q, g_mla_k, g_na_q, g_na_k, g_diff_q, g_diff_k, g_diff_sub, g_gqa_q, g_gqa_k,
        diff_lq1, diff_lk1, diff_lq2, diff_lk2)], -1)

    tok = np.arange(S)
    rows, cols = (tok % GR).astype(np.float32), (tok // GR).astype(np.float32)
    tabs = []
    for rot in (HD, RD):
        n = rot // 4
        inv = np.power(np.float32(10000.0), -np.arange(n, dtype=np.float32) / np.float32(n)).astype(np.float32)
        ar, ac = rows[:, None] * inv, cols[:, None] * inv
        tabs += [np.cos(np.concatenate([ar, ar, ac, ac], -1)), np.sin(np.concatenate([-ar, ar, -ac, ac], -1))]
    arrays["rope"] = np.concatenate(tabs, -1).astype(np.float32).reshape(NTL, P, 192).transpose(1, 0, 2)

    qc, qr = np.arange(P) // GR, np.arange(P) % GR
    kc, kr = np.arange(384) // GR - 16, np.arange(384) % GR
    dc = kc[None] - qc[:, None] + 15
    dr = kr[None] - qr[:, None] + 7
    padded = np.pad(np.asarray(na_rpb), ((0, 0), (0, 0), (0, 0), (0, 1)))
    arrays["na_rows"] = padded[:, :, dr, np.where((dc >= 0) & (dc <= 30), dc, 31)]
    mask = []
    for kind, t in ((0, 0), (1, 1), (2, 3)):
        q_col = 16 * t + qc
        start = np.clip(q_col - 8, 0, GW - 16)[:, None]
        k_col = (16 * t + kc)[NA_SRC[kind]:NA_SRC[kind] + NA_TAB[kind][1]][None]
        mask.append(np.where((k_col >= start) & (k_col < start + 16), 0.0, NEG))
    arrays["na_mask"] = np.concatenate(mask, -1).astype(np.float32)

    nc = bacc.Bacc("TRN2", target_bir_lowering=False, num_devices=1, dynamic_dma_scratch_size=1024)
    arrays = {k: np.ascontiguousarray(v) for k, v in arrays.items()}
    aps = {k: nc.dram_tensor("in_" + k, v.shape, mybir.dt.from_np(v.dtype), kind="ExternalInput").ap() for k, v in arrays.items()}
    out = nc.dram_tensor("out", (P, KT, S), mybir.dt.float32, kind="ExternalOutput").ap()
    program(nc, aps, out)
    ins = {"in_" + k: v for k, v in arrays.items()}
    got = np.asarray(run_bass_kernel_spmd(nc, [ins], core_ids=[0]).results[0]["out"])
    y = np.empty((1, S, D), np.float32)
    y[0, perm] = got.transpose(2, 1, 0).reshape(S, D)
    return y
```
